# Optimizing a Trainium2 kernel written in Bass

```python
import math
import jax, jax.numpy as jnp
from jax import lax
import numpy as np

D_MODEL = 1024
BATCH = 1
SEQ = 1024
DEPTH = 2

CHUNK = 64
EPS = 1e-6
NEG = -1e30
N_EVEN = (DEPTH + 1) // 2
N_ODD = DEPTH // 2

SSD_HEADS = 16
SSD_HEAD_DIM = 64
SSD_INNER = SSD_HEADS * SSD_HEAD_DIM
SSD_GROUPS = 2
SSD_HPG = SSD_HEADS // SSD_GROUPS
SSD_STATE = 128
SSD_GN = SSD_GROUPS * SSD_STATE
SSD_XBC = SSD_INNER + 2 * SSD_GN
SSD_CONV = 4

ML_HEADS = 4
ML_QK_DIM = 128
ML_V_DIM = 256
ML_QK = ML_HEADS * ML_QK_DIM
ML_INNER = ML_HEADS * ML_V_DIM
ML_CONV = 4

DA_HEADS = 8
DA_QK_DIM = 64
DA_V_DIM = 2 * DA_QK_DIM
DA_QK = DA_HEADS * 2 * DA_QK_DIM
DA_INNER = DA_HEADS * DA_V_DIM
Q_BLOCK = 128
ALIBI_SLOPES = tuple(2.0 ** (-8.0 * (h + 1) / DA_HEADS) for h in range(DA_HEADS))

AB_SIZES = (SSD_INNER, SSD_XBC, SSD_HEADS, ML_INNER, ML_QK, ML_QK, ML_INNER, ML_HEADS, ML_HEADS, ML_INNER)
AB_SPLITS = tuple(int(s) for s in np.cumsum(AB_SIZES)[:-1])
AB_COLS = int(sum(AB_SIZES))
AB_OUT = SSD_INNER + ML_INNER
C_SIZES = (DA_QK, DA_QK, DA_INNER, DA_INNER)
C_SPLITS = tuple(int(s) for s in np.cumsum(C_SIZES)[:-1])
C_COLS = int(sum(C_SIZES))

kernel_name = 'hybrid_ssd_mlstm_diffattn_chunk_causal'

def _f32(a):
    return a.astype(jnp.float32)

def _rms(x):
    return x * lax.rsqrt(jnp.mean(x * x, axis=-1, keepdims=True) + EPS)

def _rmsnorm(x, g):
    xf = _f32(x)
    return (_rms(xf) * _f32(g)).astype(x.dtype)

def _causal_conv(x, w, b):
    k = w.shape[0]
    c = x.shape[-1]
    y = lax.conv_general_dilated(x, w[:, None, :], window_strides=(1,), padding=[(k - 1, 0)],
                                 dimension_numbers=('NWC', 'WIO', 'NWC'), feature_group_count=c)
    return y + b

def _ssd(xbc, dt_raw, z, conv_w, conv_b, dt_bias, a_log, d_skip, norm_g):
    bsz, seqlen, _ = xbc.shape
    nc = seqlen // CHUNK
    xbc = jax.nn.silu(_causal_conv(xbc, conv_w, conv_b))
    xs, bm, cm = jnp.split(xbc, [SSD_INNER, SSD_INNER + SSD_GN], axis=-1)
    xs = xs.reshape(bsz, nc, CHUNK, SSD_GROUPS, SSD_HPG, SSD_HEAD_DIM)
    bm = bm.reshape(bsz, nc, CHUNK, SSD_GROUPS, SSD_STATE)
    cm = cm.reshape(bsz, nc, CHUNK, SSD_GROUPS, SSD_STATE)
    dt = jax.nn.softplus(dt_raw + dt_bias).reshape(bsz, nc, CHUNK, SSD_GROUPS, SSD_HPG)
    a = -jnp.exp(a_log).reshape(SSD_GROUPS, SSD_HPG)
    a_cs = jnp.cumsum(dt * a, axis=2)
    xdt = xs * dt[..., None]
    causal = jnp.tril(jnp.ones((CHUNK, CHUNK), dtype=bool))[None, None, :, :, None, None]
    seg = a_cs[:, :, :, None] - a_cs[:, :, None, :]
    decay = jnp.where(causal, jnp.exp(jnp.where(causal, seg, 0.0)), 0.0)
    cb = jnp.einsum('bclgn,bcsgn->bclsg', cm, bm)
    y_diag = jnp.einsum('bclsg,bclsgr,bcsgrp->bclgrp', cb, decay, xdt)

    def step(state, inp):
        xdt_c, b_c, c_c, acs_c = inp
        y_off = jnp.einsum('blgn,bgrpn->blgrp', c_c, state) * jnp.exp(acs_c)[..., None]
        to_end = jnp.exp(acs_c[:, -1:] - acs_c)
        new_state = state * jnp.exp(acs_c[:, -1])[..., None, None] + \
            jnp.einsum('blgn,blgr,blgrp->bgrpn', b_c, to_end, xdt_c)
        return new_state, y_off

    state0 = jnp.zeros((bsz, SSD_GROUPS, SSD_HPG, SSD_HEAD_DIM, SSD_STATE), jnp.float32)
    mv = lambda t: jnp.moveaxis(t, 1, 0)
    _, y_off = lax.scan(step, state0, (mv(xdt), mv(bm), mv(cm), mv(a_cs)))
    y = y_diag + jnp.moveaxis(y_off, 0, 1) + xs * d_skip.reshape(SSD_GROUPS, SSD_HPG)[:, :, None]
    y = y.reshape(bsz, seqlen, SSD_INNER) * jax.nn.silu(z)
    yg = _rms(y.reshape(bsz, seqlen, SSD_GROUPS, SSD_INNER // SSD_GROUPS))
    return yg.reshape(bsz, seqlen, SSD_INNER) * norm_g

def _mlstm(q, k, v, i_raw, f_raw, o_raw, z, conv_w, conv_b, i_bias, f_bias, norm_g):
    bsz, seqlen, _ = v.shape
    nc = seqlen // CHUNK
    qk = jax.nn.silu(_causal_conv(jnp.concatenate([q, k], axis=-1), conv_w, conv_b))
    q, k = jnp.split(qk, 2, axis=-1)
    q = q.reshape(bsz, nc, CHUNK, ML_HEADS, ML_QK_DIM)
    k = k.reshape(bsz, nc, CHUNK, ML_HEADS, ML_QK_DIM) * (ML_QK_DIM ** -0.5)
    v = v.reshape(bsz, nc, CHUNK, ML_HEADS, ML_V_DIM)
    ig = (i_raw + i_bias).reshape(bsz, nc, CHUNK, ML_HEADS)
    bcum = jnp.cumsum(jax.nn.log_sigmoid(f_raw + f_bias).reshape(bsz, nc, CHUNK, ML_HEADS), axis=2)
    causal = jnp.tril(jnp.ones((CHUNK, CHUNK), dtype=bool))[None, :, :, None]

    def step(carry, inp):
        c_mem, n_mem, m_prev = carry
        q_c, k_c, v_c, ig_c, b_c = inp
        d_log = jnp.where(causal, b_c[:, :, None] - b_c[:, None, :] + ig_c[:, None, :], NEG)
        inter_log = b_c + m_prev[:, None]
        m_t = jnp.maximum(inter_log, jnp.max(d_log, axis=2))
        w_intra = jnp.exp(d_log - m_t[:, :, None])
        w_inter = jnp.exp(inter_log - m_t)
        s = jnp.einsum('bthd,bshd->btsh', q_c, k_c) * w_intra
        num = jnp.einsum('btsh,bshv->bthv', s, v_c) + \
            w_inter[..., None] * jnp.einsum('bthd,bhdv->bthv', q_c, c_mem)
        den = jnp.sum(s, axis=2) + w_inter * jnp.einsum('bthd,bhd->bth', q_c, n_mem)
        h = num / jnp.maximum(jnp.abs(den), jnp.exp(-m_t))[..., None]
        b_end = b_c[:, -1]
        g_log = b_end[:, None] - b_c + ig_c
        m_new = jnp.maximum(b_end + m_prev, jnp.max(g_log, axis=1))
        g = jnp.exp(g_log - m_new[:, None])
        dec = jnp.exp(b_end + m_prev - m_new)
        c_new = dec[..., None, None] * c_mem + jnp.einsum('bsh,bshd,bshv->bhdv', g, k_c, v_c)
        n_new = dec[..., None] * n_mem + jnp.einsum('bsh,bshd->bhd', g, k_c)
        return (c_new, n_new, m_new), h

    carry0 = (jnp.zeros((bsz, ML_HEADS, ML_QK_DIM, ML_V_DIM), jnp.float32),
              jnp.zeros((bsz, ML_HEADS, ML_QK_DIM), jnp.float32),
              jnp.zeros((bsz, ML_HEADS), jnp.float32))
    mv = lambda t: jnp.moveaxis(t, 1, 0)
    _, h = lax.scan(step, carry0, (mv(q), mv(k), mv(v), mv(ig), mv(bcum)))
    h = jnp.moveaxis(h, 0, 1).reshape(bsz, seqlen, ML_HEADS, ML_V_DIM)
    h = h * jax.nn.sigmoid(o_raw).reshape(bsz, seqlen, ML_HEADS, ML_V_DIM)
    h = _rms(h).reshape(bsz, seqlen, ML_INNER) * norm_g
    return h * jax.nn.silu(z)

def _diff_attn(q, k, v, z, lam_q1, lam_k1, lam_q2, lam_k2, subln_g, lambda_init):
    bsz, seqlen, _ = q.shape
    q = q.reshape(bsz, seqlen, DA_HEADS, 2, DA_QK_DIM)
    k = k.reshape(bsz, seqlen, DA_HEADS, 2, DA_QK_DIM)
    v = v.reshape(bsz, seqlen, DA_HEADS, DA_V_DIM)
    lam = jnp.exp(jnp.sum(lam_q1 * lam_k1)) - jnp.exp(jnp.sum(lam_q2 * lam_k2)) + lambda_init
    slopes = jnp.asarray(ALIBI_SLOPES, jnp.float32)
    key_pos = jnp.arange(seqlen)
    key_chunk = key_pos // CHUNK
    nb = seqlen // Q_BLOCK
    qb = jnp.moveaxis(q.reshape(bsz, nb, Q_BLOCK, DA_HEADS, 2, DA_QK_DIM), 1, 0)
    scale = DA_QK_DIM ** -0.5

    def block(args):
        q_blk, blk = args
        q_pos = blk * Q_BLOCK + jnp.arange(Q_BLOCK)
        s = jnp.einsum('bqhjd,bkhjd->bhjqk', q_blk, k) * scale
        dist = jnp.abs(q_pos[:, None] - key_pos[None, :]).astype(jnp.float32)
        allowed = key_chunk[None, :] <= (q_pos // CHUNK)[:, None]
        s = s - (slopes[:, None, None] * dist)[None, :, None]
        p = jax.nn.softmax(jnp.where(allowed, s, -jnp.inf), axis=-1)
        a = p[:, :, 0] - lam * p[:, :, 1]
        return jnp.einsum('bhqk,bkhv->bqhv', a, v)

    o = lax.map(block, (qb, jnp.arange(nb)))
    o = jnp.moveaxis(o, 0, 1).reshape(bsz, seqlen, DA_HEADS, DA_V_DIM)
    o = _rms(o) * subln_g * (1.0 - lambda_init)
    return o.reshape(bsz, seqlen, DA_INNER) * jax.nn.silu(z)

def setup_inputs(seed: int = 0) -> dict:
    key = jax.random.key(seed)
    ks = jax.random.split(key, 24)
    nrm = lambda k, shape, sc: jax.random.normal(k, shape, jnp.float32) * sc
    u = jax.random.uniform(ks[5], (N_EVEN, SSD_HEADS), jnp.float32)
    dt0 = jnp.exp(u * (math.log(0.1) - math.log(0.001)) + math.log(0.001))
    return {
        'x': nrm(ks[0], (BATCH, SEQ, D_MODEL), 1.0),
        'ab_norm_g': 1.0 + nrm(ks[1], (N_EVEN, D_MODEL), 0.02),
        'ab_w_in': nrm(ks[2], (N_EVEN, D_MODEL, AB_COLS), D_MODEL ** -0.5),
        'ab_ssd_conv_w': nrm(ks[3], (N_EVEN, SSD_CONV, SSD_XBC), SSD_CONV ** -0.5),
        'ab_ssd_conv_b': nrm(ks[4], (N_EVEN, SSD_XBC), 0.01),
        'ab_dt_bias': dt0 + jnp.log(-jnp.expm1(-dt0)),
        'ab_a_log': jnp.log(jax.random.uniform(ks[6], (N_EVEN, SSD_HEADS), jnp.float32, 1.0, 16.0)),
        'ab_d_skip': 1.0 + nrm(ks[7], (N_EVEN, SSD_HEADS), 0.1),
        'ab_ssd_norm_g': 1.0 + nrm(ks[8], (N_EVEN, SSD_INNER), 0.02),
        'ab_ml_conv_w': nrm(ks[9], (N_EVEN, ML_CONV, 2 * ML_QK), ML_CONV ** -0.5),
        'ab_ml_conv_b': nrm(ks[10], (N_EVEN, 2 * ML_QK), 0.01),
        'ab_i_bias': nrm(ks[11], (N_EVEN, ML_HEADS), 0.1),
        'ab_f_bias': jnp.linspace(3.0, 6.0, ML_HEADS, dtype=jnp.float32)[None] + nrm(ks[12], (N_EVEN, ML_HEADS), 0.1),
        'ab_ml_norm_g': 1.0 + nrm(ks[13], (N_EVEN, ML_INNER), 0.02),
        'ab_w_out': nrm(ks[14], (N_EVEN, AB_OUT, D_MODEL), AB_OUT ** -0.5),
        'c_norm_g': 1.0 + nrm(ks[15], (N_ODD, D_MODEL), 0.02),
        'c_w_in': nrm(ks[16], (N_ODD, D_MODEL, C_COLS), D_MODEL ** -0.5),
        'c_lam_q1': nrm(ks[17], (N_ODD, DA_QK_DIM), 0.1),
        'c_lam_k1': nrm(ks[18], (N_ODD, DA_QK_DIM), 0.1),
        'c_lam_q2': nrm(ks[19], (N_ODD, DA_QK_DIM), 0.1),
        'c_lam_k2': nrm(ks[20], (N_ODD, DA_QK_DIM), 0.1),
        'c_subln_g': 1.0 + nrm(ks[21], (N_ODD, DA_V_DIM), 0.02),
        'c_w_out': nrm(ks[22], (N_ODD, DA_INNER, D_MODEL), DA_INNER ** -0.5),
        'final_norm_g': 1.0 + nrm(ks[23], (D_MODEL,), 0.02),
    }

def reference(x, ab_norm_g, ab_w_in, ab_ssd_conv_w, ab_ssd_conv_b, ab_dt_bias, ab_a_log, ab_d_skip,
              ab_ssd_norm_g, ab_ml_conv_w, ab_ml_conv_b, ab_i_bias, ab_f_bias, ab_ml_norm_g, ab_w_out,
              c_norm_g, c_w_in, c_lam_q1, c_lam_k1, c_lam_q2, c_lam_k2, c_subln_g, c_w_out,
              final_norm_g):
    for layer in range(DEPTH):
        if layer % 2 == 0:
            i = layer // 2
            h = _f32(_rmsnorm(x, ab_norm_g[i]))
            proj = h @ _f32(ab_w_in[i])
            z_a, xbc, dt_raw, z_b, q, k, v, ig, fg, og = jnp.split(proj, AB_SPLITS, axis=-1)
            y_a = _ssd(xbc, dt_raw, z_a, _f32(ab_ssd_conv_w[i]), _f32(ab_ssd_conv_b[i]), _f32(ab_dt_bias[i]),
                       _f32(ab_a_log[i]), _f32(ab_d_skip[i]), _f32(ab_ssd_norm_g[i]))
            y_b = _mlstm(q, k, v, ig, fg, og, z_b, _f32(ab_ml_conv_w[i]), _f32(ab_ml_conv_b[i]),
                         _f32(ab_i_bias[i]), _f32(ab_f_bias[i]), _f32(ab_ml_norm_g[i]))
            y = jnp.concatenate([y_a, y_b], axis=-1) @ _f32(ab_w_out[i])
        else:
            i = layer // 2
            h = _f32(_rmsnorm(x, c_norm_g[i]))
            proj = h @ _f32(c_w_in[i])
            q, k, v, z = jnp.split(proj, C_SPLITS, axis=-1)
            lambda_init = 0.8 - 0.6 * math.exp(-0.3 * layer)
            y_c = _diff_attn(q, k, v, z, _f32(c_lam_q1[i]), _f32(c_lam_k1[i]), _f32(c_lam_q2[i]),
                             _f32(c_lam_k2[i]), _f32(c_subln_g[i]), lambda_init)
            y = y_c @ _f32(c_w_out[i])
        x = x + y.astype(x.dtype)
    return _rmsnorm(x, final_norm_g)


_drawn_inputs = setup_inputs


def setup_inputs(seed=0):
    import zlib

    import numpy as np

    out = dict(_drawn_inputs(seed))
    spreads = {}
    factors = {'ab_ssd_conv_b': 6.856,
     'ab_ssd_norm_g': 5.0,
     'ab_ml_conv_b': 8.0,
     'ab_i_bias': 8.0,
     'ab_ml_norm_g': 7.642,
     'c_norm_g': 5.3,
     'c_lam_q1': 3.461,
     'c_lam_k1': 7.145,
     'c_lam_q2': 7.974,
     'c_lam_k2': 8.0,
     'c_subln_g': 8.0,
     'final_norm_g': 2.911}
    for name, (base, spread) in spreads.items():
        noise = np.random.default_rng([zlib.crc32(name.encode()), seed]).standard_normal(out[name].shape)
        drawn = base * np.exp(spread * noise) if base else spread * noise
        out[name] = __import__('jax').numpy.asarray(drawn.astype(out[name].dtype))
    for name, factor in factors.items():
        out[name] = (out[name] * factor).astype(out[name].dtype)
    return out
```

```python
from contextlib import ExitStack

import numpy as np

import concourse.bass as bass
from concourse import mybir

F32 = mybir.dt.float32
F32R = mybir.dt.float32r
BF16 = mybir.dt.bfloat16
ALU = mybir.AluOpType
ACT = mybir.ActivationFunctionType
AX = mybir.AxisListType

P = 128
SEQ = 1024
D = 1024
TILES = SEQ // P
KT = D // P
BLK = 512
EPS = 1e-6
MASKED = -1e30

SSD_HEADS, SSD_DIM, SSD_STATE, SSD_GROUPS = 16, 64, 128, 2
SSD_INNER = SSD_HEADS * SSD_DIM
SSD_XBC = SSD_INNER + 2 * SSD_GROUPS * SSD_STATE
ML_HEADS, ML_QK, ML_V = 4, 128, 256
ML_INNER = ML_HEADS * ML_V
CONV = 4
GATES = SSD_HEADS + 2 * ML_HEADS
DECAYS = SSD_HEADS + ML_HEADS
XBC_T = SSD_XBC // P
QK_T = 2 * ML_HEADS * ML_QK // P
FEAT_T = XBC_T + QK_T
AB_OUT_T = (SSD_INNER + ML_INNER) // P

DA_HEADS, DA_QK, DA_V = 8, 64, 128

C_ZA = 0
C_XBC = C_ZA + SSD_INNER
C_DT = C_XBC + SSD_XBC
C_ZB = C_DT + SSD_HEADS
C_Q = C_ZB + ML_INNER
C_K = C_Q + ML_HEADS * ML_QK
C_V = C_K + ML_HEADS * ML_QK
C_IG = C_V + ML_INNER
C_OG = C_IG + 2 * ML_HEADS


def over(eng, first, count, body):
    while first < 2 and count:
        body(first, first % 2, first // 2)
        first, count = first + 1, count - 1
    pairs = count // 2
    if pairs:
        with eng.Fori(0, pairs) as i:
            for j in (0, 1):
                body(i * 2 + (first + j), (first + j) % 2, i + (first + j) // 2)
    if count % 2:
        n = first + count - 1
        body(n, n % 2, n // 2)


class Part:

    def __init__(self, nc, ctx, tag):
        self.nc, self.ctx, self.tag = nc, ctx, tag

    def sb(self, name, shape, dt=F32):
        return self.ctx.enter_context(self.nc.sbuf_tensor(f"{self.tag}_{name}", shape, dt))

    def ps(self, name, shape, dt=F32):
        return self.ctx.enter_context(self.nc.psum_tensor(f"{self.tag}_{name}", shape, dt))

    def sem(self, name):
        return self.nc.alloc_semaphore(f"{self.tag}_{name}")


def mid(ap, n):
    a = ap.unsqueeze(1)
    return a.broadcast_to([a.shape[0], n] + list(a.shape[2:]))


def last(ap, n):
    a = ap.unsqueeze(len(ap.shape))
    return a.broadcast_to(list(a.shape[:-1]) + [n])


def identity(gp, t, sem, done):
    gp.memset(t[:, :], 0.0).then_inc(sem, 1)
    gp.wait_ge(sem, done - 1)
    gp.affine_select(out=t[:, :], in_=t[:, :], compare_op=ALU.not_equal, fill=1.0, base=0,
                     pattern=[[-1, P]], channel_multiplier=1).then_inc(sem, 1)


def projection(nc, tag, x, w_in, rows, feat_cols, feat_out, tok_blocks, tok_out, conv=False, gate_out=None):
    nrows = sum(r.shape[0] for r in rows)
    nf, nt = len(feat_cols), len(tok_blocks)
    nb = nf + nt
    w_tiled = w_in.rearrange("(k p) n -> p k n", p=P)
    with ExitStack() as ctx:
        ctx.enter_context(nc.cleanup_on_exit())
        m = Part(nc, ctx, tag)
        h_hi = m.sb("h_hi", [P, KT, SEQ], F32R)
        h_lo = m.sb("h_lo", [P, KT, SEQ], F32R)
        w_raw = [m.sb(f"w_raw{i}", [P, KT, BLK]) for i in (0, 1)]
        w_hi = [m.sb(f"w_hi{i}", [P, KT, BLK], F32R) for i in (0, 1)]
        w_lo = [m.sb(f"w_lo{i}", [P, KT, BLK], F32R) for i in (0, 1)]
        x_in = [m.sb(f"x_in{i}", [P, D]) for i in (0, 1)]
        h_f = [m.sb(f"h_f{i}", [P, 4, P]) for i in (0, 1)]
        stage = [m.sb(f"stage{i}", [P, BLK]) for i in range(4)]
        ident = m.sb("ident", [P, P])
        row_in = m.sb("row_in", [P, P])
        cols = m.sb("cols", [P, nrows])
        junk = m.sb("junk", [P, D])
        sumsq = [m.sb(f"sumsq{i}", [P, 1]) for i in (0, 1)]
        rstd = [m.sb(f"rstd{i}", [P, 1]) for i in (0, 1)]
        half = m.sb("half", [P, 1])
        if conv:
            c_raw = [m.sb(f"c_raw{i}", [P, CONV - 1 + SEQ]) for i in (0, 1)]
            c_acc = [junk, m.sb("c_acc1", [P, SEQ])]
        if gate_out is not None:
            g_raw = m.sb("g_raw", [P, KT, GATES])
            g_hi = m.sb("g_hi", [P, KT, GATES], F32R)
            g_lo = m.sb("g_lo", [P, KT, GATES], F32R)
            g_st = m.sb("g_st", [GATES, SEQ])
        bank = [m.ps(f"bank{i}", [P, 512]) for i in range(8)]

        rows_in = m.sem("rows_in")
        x_landed = [m.sem(f"x_landed{i}") for i in (0, 1)]
        w_landed = [m.sem(f"w_landed{i}") for i in (0, 1)]
        g_landed = m.sem("g_landed")
        ident_ok = m.sem("ident_ok")
        zeroed = m.sem("zeroed")
        rows_T = m.sem("rows_T")
        cols_ok = m.sem("cols_ok")
        squared = m.sem("squared")
        mean_ok = m.sem("mean_ok")
        rstd_ok = m.sem("rstd_ok")
        normed = m.sem("normed")
        x_T = m.sem("x_T")
        hf_ok = m.sem("hf_ok")
        hhi_ok = m.sem("hhi_ok")
        h_ok = m.sem("h_ok")
        hi_ok = m.sem("hi_ok")
        split = m.sem("split")
        g_split = m.sem("g_split")
        full = m.sem("full")
        staged = m.sem("staged")
        stored = [m.sem(f"stored{i}") for i in range(4)]
        conv_in = m.sem("conv_in")
        tapped = m.sem("tapped")
        conv_ok = m.sem("conv_ok")
        silu_ok = m.sem("silu_ok")
        c_stored = [m.sem(f"c_stored{i}") for i in (0, 1)]
        g_full = m.sem("g_full")
        g_staged = m.sem("g_staged")
        g_stored = m.sem("g_stored")

        block = ctx.enter_context(nc.Block())

        @block.sync
        def _(sp):
            at = 0
            for r in rows:
                sp.dma_start(row_in[at:at + r.shape[0], :], r).then_inc(rows_in, 16)
                at += r.shape[0]

            def load_x(t):
                if t >= 2:
                    sp.wait_ge(x_T, 2 * (t - 1))
                sp.dma_start(x_in[t % 2][:, :], x[t * P:(t + 1) * P, :]).then_inc(x_landed[t % 2], 16)

            def load_w(b):
                c = feat_cols[b] if b < nf else tok_blocks[b - nf][0]
                if b >= 2:
                    sp.wait_ge(split, b - 1)
                sp.dma_start(w_raw[b % 2][:, :, :], w_tiled[:, :, c:c + BLK]).then_inc(w_landed[b % 2], 16)

            load_x(0)
            load_x(1)
            load_w(0)
            for t in range(2, TILES):
                load_x(t)
            load_w(1)
            if gate_out is not None:
                with nc.allow_non_contiguous_dma(reason="24 gate columns"):
                    sp.dma_start(g_raw[:, :, 0:SSD_HEADS], w_tiled[:, :, C_DT:C_DT + SSD_HEADS]).then_inc(g_landed, 16)
                    sp.dma_start(g_raw[:, :, SSD_HEADS:GATES],
                                 w_tiled[:, :, C_IG:C_IG + 2 * ML_HEADS]).then_inc(g_landed, 16)
            for b in range(nb):
                if b + 2 < nb:
                    load_w(b + 2)
                if b < nf and conv:
                    for f in range(4):
                        n = 4 * b + f
                        sp.wait_ge(silu_ok, n + 1)
                        sp.dma_start(feat_out[n, :, :], c_acc[f % 2][:, :]).then_inc(c_stored[f % 2], 16)
                    continue
                for o in range(8):
                    sp.wait_ge(staged, 8 * (b - (nf if conv else 0)) + o + 1)
                    if b < nf:
                        dst = feat_out[4 * b + o // 2, :, (o % 2) * BLK:(o % 2 + 1) * BLK]
                    else:
                        dst = tok_out[o * P:(o + 1) * P, (b - nf) * BLK:(b - nf + 1) * BLK]
                    sp.dma_start(dst, stage[o % 4][:, :]).then_inc(stored[o % 4], 16)
            if gate_out is not None:
                sp.wait_ge(g_staged, 2)
                sp.dma_start(gate_out, g_st[:, :]).then_inc(g_stored, 16)
                sp.wait_ge(g_stored, 16)
            for s in range(4):
                sp.wait_ge(stored[s], 16 * 2 * (nb - (nf if conv else 0)))
            if conv:
                for s in (0, 1):
                    sp.wait_ge(c_stored[s], 16 * 2 * nf)

        @block.gpsimd
        def _(gp):
            identity(gp, ident, ident_ok, 2)
            gp.memset(half[:, :], -0.5).then_inc(zeroed, 1)
            if conv:
                for c in c_raw:
                    gp.memset(c[:, 0:CONV - 1], 0.0).then_inc(zeroed, 1)
            gp.wait_ge(zeroed, 1)

            for t in range(TILES):
                r = rstd[t % 2][:, :]
                gp.wait_ge(squared, t + 1)
                if t >= 2:
                    gp.wait_ge(normed, t - 1)
                gp.tensor_scalar(r, sumsq[t % 2][:, :], 1.0 / D, EPS, ALU.mult, ALU.add).then_inc(mean_ok, 1)
                gp.wait_ge(mean_ok, t + 1)
                gp.tensor_tensor(r, r, half[:, :], ALU.pow).then_inc(rstd_ok, 1)

        @block.scalar
        def _(act):
            def square(t, par, prior):
                act.wait_ge(x_landed[par], prior * 16 + 16)
                act.wait_ge(squared, t + 0)
                nc.scalar.activation(junk[:, :], x_in[par][:, :], ACT.Square,
                                     accum_out=sumsq[par][:, :]).then_inc(squared, 1)

            def scale(t, par):
                act.wait_ge(rstd_ok, t + 1)
                nc.scalar.activation(x_in[par][:, :], x_in[par][:, :], ACT.Copy,
                                     scale=rstd[par][:, 0:1]).then_inc(normed, 1)

            def scale_behind(t, par, prior):
                square(t, par, prior)
                scale(t - 1, 1 - par)

            square(0, 0, 0)
            over(act, 1, TILES - 1, scale_behind)
            scale(TILES - 1, 1)

            if conv:
                def feature_block(b):
                    for f in range(4):
                        for s in (0, 1):
                            o = 2 * f + s
                            act.wait_ge(full, b * 8 + (o + 1))
                            nc.scalar.copy(c_raw[f % 2][:, CONV - 1 + s * BLK:CONV - 1 + (s + 1) * BLK],
                                           bank[o][:, :]).then_inc(conv_in, 1)
                        act.wait_ge(conv_ok, b * 4 + (f + 1))
                        nc.scalar.activation(c_acc[f % 2][:, :], c_acc[f % 2][:, :], ACT.Silu).then_inc(silu_ok, 1)

                with act.Fori(0, nf) as b:
                    feature_block(b)
            for b in range(0 if not conv else nf, nb):
                func = ACT.Copy if b < nf else tok_blocks[b - nf][1]
                for o in range(8):
                    k = b - (nf if conv else 0)
                    act.wait_ge(full, 8 * b + o + 1)
                    act.wait_ge(stored[o % 4], 16 * (2 * k + o // 4))
                    nc.scalar.activation(stage[o % 4][:, :], bank[o][:, :], func).then_inc(staged, 1)
            if gate_out is not None:
                for s in (0, 1):
                    act.wait_ge(g_full, s + 1)
                    nc.scalar.copy(g_st[:, s * BLK:(s + 1) * BLK], bank[s][0:GATES, :]).then_inc(g_staged, 1)

        @block.vector
        def _(dve):
            dve.wait_ge(rows_T, 1)
            dve.tensor_copy(cols[:, :], bank[7][:, 0:nrows]).then_inc(cols_ok, 1)
            dve.wait_ge(cols_ok, 1)

            def transposed(t, par, prior):
                for s in (0, 1):
                    dve.wait_ge(x_T, t * 2 + (s + 1))
                    if s == 0:
                        dve.wait_ge(h_ok, t * 2)
                    dve.tensor_tensor(h_f[s][:, :, :], bank[2 * par + s][:, :].rearrange("p (a b) -> p a b", a=4),
                                      last(cols[:, 4 * s:4 * s + 4], P), ALU.mult).then_inc(hf_ok, 1)
                    dve.wait_ge(hf_ok, t * 2 + (s + 1))
                    dve.tensor_copy(h_hi[:, 4 * s:4 * s + 4, bass.ds(t * P, P)], h_f[s][:, :, :]).then_inc(hhi_ok, 1)
                    dve.wait_ge(hhi_ok, t * 2 + (s + 1))
                    dve.tensor_tensor(h_lo[:, 4 * s:4 * s + 4, bass.ds(t * P, P)], h_f[s][:, :, :],
                                      h_hi[:, 4 * s:4 * s + 4, bass.ds(t * P, P)].bitcast(F32),
                                      ALU.subtract).then_inc(h_ok, 1)

            over(dve, 0, TILES, transposed)

            def split_block(n, par, prior):
                dve.wait_ge(w_landed[par], prior * 16 + 16)
                if not isinstance(n, int) or n >= 2:
                    dve.wait_ge(full, (n - 1) * 8)
                dve.tensor_copy(w_hi[par][:, :, :], w_raw[par][:, :, :]).then_inc(hi_ok, 1)
                dve.wait_ge(hi_ok, n + 1)
                dve.tensor_tensor(w_lo[par][:, :, :], w_raw[par][:, :, :], w_hi[par][:, :, :].bitcast(F32),
                                  ALU.subtract).then_inc(split, 1)

            split_block(0, 0, 0)
            if gate_out is not None:
                dve.wait_ge(g_landed, 32)
                dve.tensor_copy(g_hi[:, :, :], g_raw[:, :, :]).then_inc(g_split, 1)
                dve.wait_ge(g_split, 1)
                dve.tensor_tensor(g_lo[:, :, :], g_raw[:, :, :], g_hi[:, :, :].bitcast(F32),
                                  ALU.subtract).then_inc(g_split, 1)
            if conv:
                dve.wait_ge(zeroed, 3)

                def conv_tile(n, b, f):
                    raw, acc = c_raw[f % 2], c_acc[f % 2]
                    dve.wait_ge(conv_in, n * 2 + 2)
                    dve.wait_ge(c_stored[f % 2], b * 32 + 16 * (f // 2))
                    dve.tensor_scalar(acc[:, :], raw[:, 0:SEQ], cols[:, bass.ds(n + KT, 1)],
                                      cols[:, bass.ds(n + (KT + CONV * FEAT_T), 1)], ALU.mult, ALU.add).then_inc(tapped, 1)
                    for j in range(1, CONV):
                        dve.wait_ge(tapped, n * (CONV - 1) + j)
                        out = dve.scalar_tensor_tensor(
                            out=acc[:, :], in0=raw[:, j:j + SEQ], scalar=cols[:, bass.ds(n + (KT + j * FEAT_T), 1)],
                            in1=acc[:, :], op0=ALU.mult, op1=ALU.add)
                        out.then_inc(tapped if j < CONV - 1 else conv_ok, 1)

                def feature_block(b, par, prior):
                    split_block(b + 1, 1 - par, prior + par)
                    for f in range(4):
                        conv_tile(b * 4 + f, b, f)

                over(dve, 0, nf, feature_block)
                over(dve, nf + 1, nb - nf - 1, split_block)
            else:
                over(dve, 1, nb - 1, split_block)

        @block.tensor
        def _(pe):
            pe.wait_ge(rows_in, 16 * len(rows))
            pe.wait_ge(ident_ok, 2)
            pe.transpose(bank[7][:, 0:nrows], row_in[0:nrows, :], ident[0:nrows, 0:nrows]).then_inc(rows_T, 1)

            def transpose_tile(t, par, prior):
                pe.wait_ge(normed, t + 1)
                if not isinstance(t, int) or t > 0:
                    pe.wait_ge(hf_ok, (t - 1) * 2)
                for s in (0, 1):
                    for k in range(4):
                        mm = pe.transpose(bank[2 * par + s][:, k * P:(k + 1) * P],
                                          x_in[par][:, (4 * s + k) * P:(4 * s + k + 1) * P], ident[:, :])
                    mm.then_inc(x_T, 1)

            transpose_tile(0, 0, 0)
            over(pe, 1, TILES - 1, transpose_tile)
            pe.wait_ge(h_ok, 2 * TILES)

            def products(out, pairs):
                for q, (a, c) in enumerate(pairs):
                    mm = pe.matmul(out, a, c, start=(q == 0), stop=(q == len(pairs) - 1))
                return mm

            def feature_block(n, par, prior):
                pe.wait_ge(split, n + 1)
                for o in range(8):
                    if not isinstance(n, int) or n > 0:
                        pe.wait_ge(conv_in if conv else staged, (n - 1) * 8 + (o + 1))
                    f, s = o // 2, o % 2
                    fs, ts = slice(f * P, (f + 1) * P), slice(s * BLK, (s + 1) * BLK)
                    products(bank[o][:, :], [pair for k in range(KT) for pair in (
                        (w_hi[par][:, k, fs], h_hi[:, k, ts]), (w_hi[par][:, k, fs], h_lo[:, k, ts]),
                        (w_lo[par][:, k, fs], h_hi[:, k, ts]))]).then_inc(full, 1)

            def token_block(n, par, prior):
                pe.wait_ge(split, n + 1)
                for o in range(8):
                    if not conv:
                        pe.wait_ge(staged, (n - 1) * 8 + (o + 1))
                    elif isinstance(n, int) and n == nf:
                        pe.wait_ge(conv_in, 8 * (nf - 1) + o + 1)
                    else:
                        pe.wait_ge(staged, (n - (nf + 1)) * 8 + (o + 1))
                    ts = slice(o * P, (o + 1) * P)
                    products(bank[o][:, :], [pair for k in range(KT) for pair in (
                        (h_hi[:, k, ts], w_hi[par][:, k, :]), (h_hi[:, k, ts], w_lo[par][:, k, :]),
                        (h_lo[:, k, ts], w_hi[par][:, k, :]))]).then_inc(full, 1)

            feature_block(0, 0, 0)
            over(pe, 1, nf - 1, feature_block)
            token_block(nf, nf % 2, nf // 2)
            over(pe, nf + 1, nt - 1, token_block)
            if gate_out is not None:
                pe.wait_ge(g_split, 2)
                pe.wait_ge(staged, 8 * (nt - 1) + 2)
                for s in (0, 1):
                    ts = slice(s * BLK, (s + 1) * BLK)
                    mm = products(bank[s][0:GATES, :], [pair for k in range(KT) for pair in (
                        (g_hi[:, k, :], h_hi[:, k, ts]), (g_hi[:, k, :], h_lo[:, k, ts]),
                        (g_lo[:, k, :], h_hi[:, k, ts]))])
                    mm.then_inc(g_full, 1)


T_DT, T_DA, T_EACS, T_NACS, T_U, T_EMT = 0, 16, 32, 48, 64, 68
T_ALL = 72


def scan_gates(nc, keep, gate_rows, dt_bias, a_log, i_bias, f_bias):
    with ExitStack() as ctx:
        ctx.enter_context(nc.cleanup_on_exit())
        m = Part(nc, ctx, "g")
        rows = m.sb("rows", [GATES, SEQ])
        vec = m.sb("vec", [1, GATES + SSD_HEADS])
        ones_row = m.sb("ones_row", [1, P])
        vec_bc = m.sb("vec_bc", [P, GATES + SSD_HEADS])
        a_neg = m.sb("a_neg", [P, SSD_HEADS])
        raw = m.sb("raw", [P, TILES, GATES])
        arg = m.sb("arg", [P, TILES, DECAYS])
        narg = m.sb("narg", [P, TILES, DECAYS])
        e = m.sb("e", [P, TILES, DECAYS])
        s = m.sb("s", [P, TILES, DECAYS])
        s2 = m.sb("s2", [P, TILES, DECAYS])
        q = m.sb("q", [P, TILES, DECAYS])
        sp_ = m.sb("sp", [P, TILES, DECAYS])
        x = m.sb("x", [P, TILES, DECAYS])
        u_row = m.sb("u_row", [ML_HEADS, TILES, P])
        b_row = m.sb("b_row", [ML_HEADS, TILES, P])
        m_row = m.sb("m_row", [ML_HEADS, TILES, P])
        m_prev = m.sb("m_prev", [ML_HEADS, TILES + 1])
        w_log = m.sb("w_log", [ML_HEADS, TILES, P])
        e_row = m.sb("e_row", [ML_HEADS, TILES, P])
        ones = m.sb("ones", [P, P])
        table, maxrows, ident, tri = keep["table"], keep["maxrows"], keep["ident"], keep["tri"]
        p_raw = m.ps("p_raw", [P, 512])
        p_vec = m.ps("p_vec", [P, 512])
        p_cs = m.ps("p_cs", [P, 512])
        p_u = m.ps("p_u", [P, 2, 512])
        p_b = m.ps("p_b", [P, 2, 512])

        landed = m.sem("landed")
        pool_ok = m.sem("pool_ok")
        pe_raw = m.sem("pe_raw")
        pe_vec = m.sem("pe_vec")
        pe_cs = m.sem("pe_cs")
        pe_rows = m.sem("pe_rows")
        pe_emt = m.sem("pe_emt")
        step = m.sem("step")
        a_exp = m.sem("a_exp")
        e_exp = m.sem("e_exp")
        eacs_exp = m.sem("eacs_exp")
        w_exp = m.sem("w_exp")
        emt_exp = m.sem("emt_exp")

        block = ctx.enter_context(nc.Block())

        @block.sync
        def _(sp):
            sp.dma_start(rows[:, :], gate_rows).then_inc(landed, 16)
            at = 0
            for v in (dt_bias, i_bias, f_bias, a_log):
                n = v.shape[1]
                sp.dma_start(vec[:, at:at + n], v).then_inc(landed, 16)
                at += n

        @block.gpsimd
        def _(gp):
            n = 0
            gp.memset(ident[:, :], 0.0).then_inc(pool_ok, 1)
            gp.memset(keep["ident_bf"][:, :], 0.0).then_inc(pool_ok, 1)
            gp.memset(ones[:, :], 1.0).then_inc(pool_ok, 1)
            gp.memset(tri[:, :], 1.0).then_inc(pool_ok, 1)
            gp.memset(keep["later"][:, :], 0.0).then_inc(pool_ok, 1)
            gp.memset(keep["head_row"][:, :, :], 1.0).then_inc(pool_ok, 1)
            gp.memset(ones_row[:, :], 1.0).then_inc(pool_ok, 1)
            gp.memset(m_prev[:, :], 0.0).then_inc(pool_ok, 1)
            gp.memset(keep["half"][:, :], -0.5).then_inc(pool_ok, 1)
            gp.wait_ge(pool_ok, 9)
            for t in (ident, keep["ident_bf"]):
                gp.affine_select(out=t[:, :], in_=t[:, :], compare_op=ALU.not_equal, fill=1.0, base=0,
                                 pattern=[[-1, P]], channel_multiplier=1).then_inc(pool_ok, 1)
            gp.affine_select(out=tri[:, :], in_=tri[:, :], compare_op=ALU.is_ge, fill=0.0, base=0,
                             pattern=[[1, P]], channel_multiplier=-1).then_inc(pool_ok, 1)
            gp.affine_select(out=keep["later"][:, :], in_=keep["later"][:, :], compare_op=ALU.is_ge, fill=MASKED,
                             base=0, pattern=[[1, P]], channel_multiplier=-1).then_inc(pool_ok, 1)
            gp.affine_select(out=keep["head_row"][:, :, :], in_=keep["head_row"][:, :, :], compare_op=ALU.is_equal,
                             fill=0.0, base=0, pattern=[[1, ML_HEADS], [0, P]],
                             channel_multiplier=-1).then_inc(pool_ok, 1)

        @block.tensor
        def _(pe):
            pe.wait_ge(landed, 16 * 5)
            pe.wait_ge(pool_ok, 14)
            pe.matmul(p_vec[:, 0:GATES + SSD_HEADS], ones_row[:, :], vec[:, :], start=True, stop=True).then_inc(pe_vec, 1)
            for c in range(TILES):
                mm = pe.transpose(p_raw[:, c * GATES:(c + 1) * GATES], rows[:, c * P:(c + 1) * P],
                                  ident[0:GATES, 0:GATES])
            mm.then_inc(pe_raw, 1)
            pe.wait_ge(step, 21)
            pe.matmul(p_cs[:, 0:TILES * DECAYS], tri[:, :], x[:, :, :].rearrange("p c h -> p (c h)"),
                      start=True, stop=True).then_inc(pe_cs, 1)
            pe.wait_ge(step, 24)
            for c in range(TILES):
                pe.transpose(p_u[0:ML_HEADS, c // 4, (c % 4) * P:(c % 4 + 1) * P], table[:, c, T_U:T_U + ML_HEADS],
                             ident[:, :])
            for c in range(TILES):
                mm = pe.transpose(p_b[0:ML_HEADS, c // 4, (c % 4) * P:(c % 4 + 1) * P], s[:, c, SSD_HEADS:DECAYS],
                                  ident[:, :])
            mm.then_inc(pe_rows, 1)
            pe.wait_ge(emt_exp, 1)
            for c in range(TILES):
                mm = pe.transpose(p_vec[:, c * ML_HEADS:(c + 1) * ML_HEADS], e_row[:, c, :],
                                  ident[0:ML_HEADS, 0:ML_HEADS])
            mm.then_inc(pe_emt, 1)

        @block.scalar
        def _(act):
            act.wait_ge(step, 1)
            nc.scalar.activation(a_neg[:, :], vec_bc[:, GATES:], ACT.Exp).then_inc(a_exp, 1)
            act.wait_ge(step, 6)
            nc.scalar.activation(e[:, :, :], narg[:, :, :], ACT.Exp).then_inc(e_exp, 1)
            act.wait_ge(step, 22)
            nc.scalar.activation(table[:, :, T_EACS:T_EACS + SSD_HEADS], s[:, :, 0:SSD_HEADS],
                                 ACT.Exp).then_inc(eacs_exp, 1)
            act.wait_ge(step, 24 + 2 + 2 * TILES + 2)
            nc.scalar.activation(maxrows[:, :, 1, :], w_log[:, :, :], ACT.Exp).then_inc(w_exp, 1)
            act.wait_ge(step, 24 + 2 + 2 * TILES + 3)
            nc.scalar.activation(e_row[:, :, :], b_row[:, :, :], ACT.Exp, scale=-1.0).then_inc(emt_exp, 1)

        @block.vector
        def _(dve):
            steps = [0]

            def chain(ins):
                steps[0] += 1
                ins.then_inc(step, 1)
                dve.wait_ge(step, steps[0])

            f = slice(SSD_HEADS, DECAYS)
            dve.wait_ge(pe_vec, 1)
            chain(dve.tensor_copy(vec_bc[:, :], p_vec[:, 0:GATES + SSD_HEADS]))
            dve.wait_ge(pe_raw, 1)
            chain(dve.tensor_tensor(raw[:, :, :], p_raw[:, 0:TILES * GATES].rearrange("p (c g) -> p c g", g=GATES),
                                    mid(vec_bc[:, 0:GATES], TILES), ALU.add))
            chain(dve.tensor_copy(arg[:, :, 0:SSD_HEADS], raw[:, :, 0:SSD_HEADS]))
            chain(dve.tensor_scalar(arg[:, :, f], raw[:, :, SSD_HEADS + ML_HEADS:GATES], -1.0, None, ALU.mult))
            chain(dve.tensor_scalar(q[:, :, :], arg[:, :, :], -1.0, None, ALU.mult))
            chain(dve.tensor_tensor(narg[:, :, :], arg[:, :, :], q[:, :, :], ALU.min))
            dve.wait_ge(e_exp, 1)
            chain(dve.tensor_scalar(q[:, :, :], e[:, :, :], 2.0, None, ALU.add))
            chain(dve.reciprocal(s[:, :, :], q[:, :, :]))
            chain(dve.tensor_tensor(s[:, :, :], s[:, :, :], e[:, :, :], ALU.mult))
            chain(dve.tensor_tensor(s2[:, :, :], s[:, :, :], s[:, :, :], ALU.mult))
            chain(dve.tensor_scalar(q[:, :, :], s2[:, :, :], 1.0 / 15, None, ALU.mult))
            for k in (13, 11, 9, 7, 5, 3):
                chain(dve.scalar_tensor_tensor(out=q[:, :, :], in0=q[:, :, :], scalar=1.0 / k, in1=s2[:, :, :],
                                               op0=ALU.add, op1=ALU.mult))
            chain(dve.scalar_tensor_tensor(out=q[:, :, :], in0=q[:, :, :], scalar=1.0, in1=s[:, :, :],
                                           op0=ALU.add, op1=ALU.mult))
            chain(dve.tensor_scalar(sp_[:, :, :], arg[:, :, :], 0.0, None, ALU.max))
            chain(dve.scalar_tensor_tensor(out=sp_[:, :, :], in0=q[:, :, :], scalar=2.0, in1=sp_[:, :, :],
                                           op0=ALU.mult, op1=ALU.add))
            assert steps[0] == 20, steps
            dve.wait_ge(a_exp, 1)
            dve.tensor_scalar(x[:, :, f], sp_[:, :, f], -1.0, None, ALU.mult)
            dve.scalar_tensor_tensor(out=x[:, :, 0:SSD_HEADS], in0=sp_[:, :, 0:SSD_HEADS], scalar=-1.0,
                                     in1=mid(a_neg[:, :], TILES), op0=ALU.mult, op1=ALU.mult).then_inc(step, 1)
            steps[0] += 1
            dve.wait_ge(pe_cs, 1)
            chain(dve.tensor_copy(s[:, :, :], p_cs[:, 0:TILES * DECAYS].rearrange("p (c h) -> p c h", h=DECAYS)))
            chain(dve.tensor_scalar(table[:, :, T_NACS:T_NACS + SSD_HEADS], s[:, :, 0:SSD_HEADS], -1.0, None, ALU.mult))
            chain(dve.tensor_tensor(table[:, :, T_U:T_U + ML_HEADS], raw[:, :, SSD_HEADS:SSD_HEADS + ML_HEADS],
                                    s[:, :, f], ALU.subtract))
            dve.wait_ge(pe_rows, 1)
            flat = lambda t: t[:, :, :].rearrange("h c t -> h (c t)")
            chain(dve.tensor_copy(flat(u_row), p_u[0:ML_HEADS, :, :].rearrange("h a b -> h (a b)")))
            chain(dve.tensor_copy(flat(b_row), p_b[0:ML_HEADS, :, :].rearrange("h a b -> h (a b)")))
            for c in range(TILES):
                chain(dve.tensor_tensor_scan(m_row[:, c, :], u_row[:, c, :], u_row[:, c, :], m_prev[:, c:c + 1],
                                             ALU.max, ALU.max))
                chain(dve.tensor_tensor(m_prev[:, c + 1:c + 2], m_row[:, c, P - 1:P], b_row[:, c, P - 1:P], ALU.add))
            chain(dve.tensor_scalar(maxrows[:, :, 0, :], m_row[:, :, :], -1.0, None, ALU.mult))
            chain(dve.tensor_tensor(w_log[:, :, :], maxrows[:, :, 0, :], last(m_prev[:, 0:TILES], P), ALU.add))
            chain(dve.tensor_tensor(b_row[:, :, :], b_row[:, :, :], m_row[:, :, :], ALU.add))
            chain(dve.tensor_copy(table[:, :, T_DT:T_DT + SSD_HEADS], sp_[:, :, 0:SSD_HEADS]))
            chain(dve.tensor_copy(table[:, :, T_DA:T_DA + SSD_HEADS], x[:, :, 0:SSD_HEADS]))
            dve.wait_ge(pe_emt, 1)
            chain(dve.tensor_copy(table[:, :, T_EMT:T_EMT + ML_HEADS],
                                  p_vec[:, 0:TILES * ML_HEADS].rearrange("p (c h) -> p c h", h=ML_HEADS)))


def scan_chunks(nc, keep, x, feat, tok, w_out, norm_g, d_skip, x1):
    VW = ML_V + 1
    HG = SSD_HEADS // SSD_GROUPS
    XS, BT, CT, QT, KTL = 0, 8, 10, 12, 16
    with ExitStack() as ctx:
        ctx.enter_context(nc.cleanup_on_exit())
        m = Part(nc, ctx, "s")
        wout = m.sb("wout", [P, AB_OUT_T, D])
        fe = [m.sb(f"fe{i}", [P, FEAT_T, P]) for i in (0, 1)]
        gz = [m.sb(f"gz{i}", [P, 3, D]) for i in (0, 1)]
        va = [m.sb(f"va{i}", [P, ML_HEADS, VW]) for i in (0, 1)]
        xres = [m.sb(f"xres{i}", [P, D]) for i in (0, 1)]
        g = m.sb("g", [P, T_ALL])
        mr = m.sb("mr", [ML_HEADS, 2, P])
        x_tok = m.sb("x_tok", [P, D])
        xdt = m.sb("xdt", [P, D])
        xe = m.sb("xe", [P, D])
        b_tok = m.sb("b_tok", [P, SSD_GROUPS, SSD_STATE])
        dec = m.sb("dec", [P, SSD_HEADS, P])
        wt = m.sb("wt", [P, SSD_HEADS, P])
        e_end = m.sb("e_end", [P, SSD_HEADS])
        wm = m.sb("wm", [P, ML_HEADS, P])
        st = m.sb("st", [P, ML_HEADS, P])
        qs = m.sb("qs", [P, ML_HEADS, P])
        kg = m.sb("kg", [P, ML_HEADS, P])
        gk = m.sb("gk", [P, ML_HEADS])
        c_dec = m.sb("c_dec", [P, ML_HEADS])
        state = m.sb("state", [P, D])
        cmem = m.sb("cmem", [P, ML_HEADS, VW])
        t1 = m.sb("t1", [P, D])
        y = m.sb("y", [P, 2 * D])
        yT = m.sb("yT", [P, AB_OUT_T, P])
        den = m.sb("den", [P, ML_HEADS])
        den2 = m.sb("den2", [P, ML_HEADS])
        x_sq = m.sb("x_sq", [P, 512])
        ssq = m.sb("ssq", [P, 6])
        rms = m.sb("rms", [P, 6])
        drow = m.sb("drow", [1, SSD_HEADS])
        d_bc = m.sb("d_bc", [P, SSD_HEADS])
        row_in = m.sb("row_in", [AB_OUT_T, P])
        gcols = m.sb("gcols", [P, AB_OUT_T])
        ident, ident_bf, tri, later = keep["ident"], keep["ident_bf"], keep["tri"], keep["later"]
        head_row, half, table, maxrows = keep["head_row"], keep["half"], keep["table"], keep["maxrows"]
        ps = m.ps("ps", [P, 8, 512])

        names = """const_in wout_in drow_T cols_T cols_ok drow_ok v_ones zero_ok g_ok mr_ok
                   p_xT p_bc p_kT p_acs p_negm p_wint p_qk p_num p_yoff p_ydiag p_state p_cmem p_yT p_out
                   a_xtok a_btok a_dec a_wm a_sqm a_sqy a_ynorm
                   d_wt d_eend d_st d_qs d_cdec d_gk d_kg d_den d_h d_cmem d_t1 d_y d_state d_yb d_yT d_x1
                   d_meanm d_meany
                   l_xdt l_xe l_xd l_yd l_yz l_sdec l_rstdm l_rstdy""".split()
        S = {n: m.sem(n) for n in names}
        in_landed = [m.sem(f"in_landed{i}") for i in (0, 1)]
        x_landed = [m.sem(f"x_landed{i}") for i in (0, 1)]
        x1_stored = [m.sem(f"x1_stored{i}") for i in (0, 1)]
        hd = lambda ap: ap.rearrange("p (h d) -> p h d", d=SSD_DIM)
        b4 = lambda b: ps[:, b, :].rearrange("p (a t) -> p a t", a=4)

        block = ctx.enter_context(nc.Block())

        @block.sync
        def _(sp):
            def load(n, par):
                t = bass.ds(n * P, P)
                sp.dma_start(fe[par][:, :, :], feat[:, :, t].rearrange("f p t -> p f t")).then_inc(in_landed[par], 16)
                sp.dma_start(gz[par][:, :, :], tok[t, 0:3 * D].rearrange("p (k n) -> p k n", k=3)).then_inc(in_landed[par], 16)
                sp.dma_start(va[par][:, :, 0:ML_V], tok[t, 3 * D:4 * D].rearrange("p (h v) -> p h v", h=ML_HEADS)
                             ).then_inc(in_landed[par], 16)

            load(0, 0)
            sp.dma_start(drow[:, :], d_skip).then_inc(S["const_in"], 16)
            half_rows = AB_OUT_T // 2
            for i, r in enumerate(norm_g):
                sp.dma_start(row_in[i * half_rows:(i + 1) * half_rows, :], r).then_inc(S["const_in"], 16)
            load(1, 1)
            for k in (0, 1):
                sp.dma_start(wout[:, 8 * k:8 * k + 8, :],
                             w_out[k * D:(k + 1) * D, :].rearrange("(k p) n -> p k n", p=P)).then_inc(S["wout_in"], 16)

            def load_x(n, par, prior):
                sp.wait_ge(x1_stored[par], prior * 16)
                sp.dma_start(xres[par][:, :], x[bass.ds(n * P, P), :]).then_inc(x_landed[par], 16)

            def store_x1(n, par):
                sp.wait_ge(S["d_x1"], n * 2 + 2)
                sp.dma_start(x1[bass.ds(n * P, P), :], xres[par][:, :]).then_inc(x1_stored[par], 16)

            load_x(0, 0, 0)

            def body(n, par, prior):
                sp.wait_ge(S["p_cmem"], n + 1)
                sp.wait_ge(S["d_yb"], n + 1)
                sp.wait_ge(S["l_yz"], n + 1)
                load(n + 2, par)
                load_x(n + 1, 1 - par, prior + par)
                store_x1(n, par)

            over(sp, 0, TILES - 2, body)
            load_x(TILES - 1, 1, (TILES - 1) // 2)
            store_x1(TILES - 2, 0)
            store_x1(TILES - 1, 1)
            for s in x1_stored:
                sp.wait_ge(s, 16 * TILES // 2)

        @block.tensor
        def _(pe):
            pe.wait_ge(S["const_in"], 16 * 3)
            pe.transpose(ps[:, 7, 0:AB_OUT_T], row_in[:, :], ident[0:AB_OUT_T, 0:AB_OUT_T]).then_inc(S["cols_T"], 1)
            pe.matmul(ps[:, 6, 0:SSD_HEADS], tri[0:1, :], drow[:, :], start=True, stop=True).then_inc(S["drow_T"], 1)
            pe.wait_ge(S["cols_ok"], 1)
            pe.wait_ge(S["drow_ok"], 1)
            pe.wait_ge(S["zero_ok"], 4)

            def weights(n, par, prior):
                pe.wait_ge(in_landed[par], prior * 48 + 48)
                f = fe[par]
                pe.wait_ge(S["d_y"], n * 2)
                for k in range(8):
                    mm = pe.transpose(ps[:, k // 4, (k % 4) * P:(k % 4 + 1) * P], f[:, XS + k, :], ident[:, :])
                mm.then_inc(S["p_xT"], 1)
                pe.wait_ge(S["d_state"], n * 2)
                for k in range(2):
                    pe.transpose(ps[:, 3, k * P:(k + 1) * P], f[:, BT + k, :], ident[:, :])
                for k in range(2):
                    mm = pe.matmul(ps[:, 3, (2 + k) * P:(3 + k) * P], f[:, BT + k, :], f[:, CT + k, :], start=True, stop=True)
                mm.then_inc(S["p_bc"], 1)
                for k in range(4):
                    mm = pe.transpose(ps[:, 2, k * P:(k + 1) * P], f[:, KTL + k, :], ident[:, :])
                mm.then_inc(S["p_kT"], 1)
                pe.wait_ge(S["g_ok"], n + 1)
                pe.wait_ge(S["d_cmem"], n * 4)
                for q in range(4):
                    bank = 4 + q % 2
                    if q >= 2:
                        pe.wait_ge(S["a_dec"], n * 4 + (q - 1))
                    for k in range(4):
                        h = T_DA + 4 * q + k
                        pe.matmul(ps[:, bank, k * P:(k + 1) * P], g[:, h:h + 1].broadcast_to([P, P]), tri[:, :],
                                  start=(k == 0), stop=False, skip_group_check=True)
                    pe.matmul(ps[:, bank, :], ident_bf[:, :], mid(later[:, :], 4), start=False, stop=True,
                              skip_group_check=True).then_inc(S["p_acs"], 1)
                pe.wait_ge(S["mr_ok"], n + 1)
                for k in range(4):
                    pe.matmul(ps[:, 6, k * P:(k + 1) * P], head_row[:, k, :], mr[:, 0, :],
                              start=(k == 0), stop=False, skip_group_check=True)
                pe.matmul(ps[:, 6, :], ident_bf[:, :], mid(later[:, :], 4), start=False, stop=True,
                          skip_group_check=True).then_inc(S["p_negm"], 1)
                for k in range(4):
                    mm = pe.matmul(ps[:, 7, k * P:(k + 1) * P], head_row[:, k, :], mr[:, 1, :], start=True, stop=True)
                mm.then_inc(S["p_wint"], 1)
                pe.wait_ge(S["a_dec"], n * 4 + 3)
                for k in range(4):
                    mm = pe.matmul(ps[:, 4, k * P:(k + 1) * P], f[:, KTL + k, :], f[:, QT + k, :], start=True, stop=True)
                mm.then_inc(S["p_qk"], 1)

            def outputs(n, par, prior):
                f = fe[par]
                pe.wait_ge(S["d_st"], n + 1)
                pe.wait_ge(S["d_qs"], n + 1)
                pe.wait_ge(S["d_cdec"], n + 1)
                pe.wait_ge(S["a_wm"], n + 1)
                pe.wait_ge(S["d_cmem"], n * 4)
                pe.wait_ge(S["a_dec"], n * 4 + 4)
                for h in range(ML_HEADS):
                    pe.matmul(ps[:, 4 + h, 0:VW], st[:, h, :], va[par][:, h, :], start=True, stop=False)
                    mm = pe.matmul(ps[:, 4 + h, 0:VW], qs[:, h, :], cmem[:, h, :], start=False, stop=True)
                    mm.then_inc(S["p_num"], 1)
                pe.wait_ge(S["d_kg"], n + 1)
                pe.wait_ge(S["a_btok"], n + 1)
                pe.wait_ge(S["d_wt"], n * 2 + 2)
                pe.wait_ge(S["d_state"], n * 2)
                for k in range(2):
                    mm = pe.matmul(ps[:, 2 + k, :], f[:, CT + k, :], state[:, k * 512:(k + 1) * 512], start=True, stop=True)
                    mm.then_inc(S["p_yoff"], 1)
                pe.wait_ge(S["l_xdt"], n + 1)
                pe.wait_ge(S["a_xtok"], n * 2 + 2)
                pe.wait_ge(S["d_x1"], n * 2)
                for h in range(SSD_HEADS):
                    mm = pe.matmul(ps[:, h // HG, (h % HG) * SSD_DIM:(h % HG + 1) * SSD_DIM], wt[:, h, :],
                                   xdt[:, h * SSD_DIM:(h + 1) * SSD_DIM], start=True, stop=True)
                    if h % HG == HG - 1:
                        mm.then_inc(S["p_ydiag"], 1)
                for h in range(ML_HEADS):
                    pe.wait_ge(S["d_h"], n * 4 + (h + 1))
                    mm = pe.matmul(ps[:, 4 + h, 0:VW], kg[:, h, :], va[par][:, h, :], start=True, stop=True)
                mm.then_inc(S["p_cmem"], 1)
                pe.wait_ge(S["l_xe"], n + 1)
                pe.wait_ge(S["d_t1"], n * 2 + 2)
                for k in range(2):
                    mm = pe.matmul(ps[:, 2 + k, :], b_tok[:, k, :], xe[:, k * 512:(k + 1) * 512], start=True, stop=True)
                mm.then_inc(S["p_state"], 1)

            def project(n):
                pe.wait_ge(S["a_ynorm"], n * 2 + 2)
                pe.wait_ge(S["d_yb"], n + 1)
                for b in range(4):
                    for k in range(4):
                        c = (4 * b + k) * P
                        mm = pe.transpose(ps[:, b, k * P:(k + 1) * P], y[:, c:c + P], ident[:, :])
                    mm.then_inc(S["p_yT"], 1)
                pe.wait_ge(S["d_yT"], n * 4 + 4)
                for j in (0, 1):
                    for k in range(AB_OUT_T):
                        mm = pe.matmul(ps[:, j, :], yT[:, k, :], wout[:, k, j * 512:(j + 1) * 512],
                                       start=(k == 0), stop=(k == AB_OUT_T - 1))
                    mm.then_inc(S["p_out"], 1)

            def ahead_of_projection(n):
                pe.wait_ge(S["a_xtok"], n * 2 + 4)
                pe.wait_ge(S["d_kg"], n + 2)
                pe.wait_ge(S["a_btok"], n + 2)
                pe.wait_ge(S["d_wt"], n * 2 + 4)

            weights(0, 0, 0)

            def body(n, par, prior):
                outputs(n, par, prior)
                weights(n + 1, 1 - par, prior + par)
                ahead_of_projection(n)
                pe.wait_ge(S["wout_in"], 32)
                project(n)

            over(pe, 0, TILES - 1, body)
            outputs(TILES - 1, 1, (TILES - 1) // 2)
            pe.wait_ge(S["d_y"], 2 * TILES)
            pe.wait_ge(S["d_state"], 2 * TILES)
            project(TILES - 1)

        @block.scalar
        def _(act):
            def weights(n, par, prior):
                act.wait_ge(S["p_xT"], n + 1)
                act.wait_ge(S["l_yd"], n + 0)
                act.wait_ge(S["l_xdt"], n + 0)
                for k in (0, 1):
                    nc.scalar.copy(x_tok[:, k * 512:(k + 1) * 512], ps[:, k, :]).then_inc(S["a_xtok"], 1)
                act.wait_ge(S["p_bc"], n + 1)
                nc.scalar.copy(b_tok[:, :, :], ps[:, 3, 0:2 * P].rearrange("p (a t) -> p a t", a=2)).then_inc(S["a_btok"], 1)
                act.wait_ge(S["g_ok"], n + 1)
                act.wait_ge(S["d_wt"], n * 2)
                act.wait_ge(S["d_eend"], n + 0)
                act.wait_ge(S["l_xe"], n + 0)
                for q in range(4):
                    act.wait_ge(S["p_acs"], n * 4 + (q + 1))
                    for k in range(4):
                        h = 4 * q + k
                        a = nc.scalar.activation(dec[:, h, :], ps[:, 4 + q % 2, k * P:(k + 1) * P], ACT.Exp,
                                                 bias=g[:, T_NACS + h:T_NACS + h + 1])
                    a.then_inc(S["a_dec"], 1)
                act.wait_ge(S["p_negm"], n + 1)
                act.wait_ge(S["d_st"], n + 0)
                act.wait_ge(S["d_gk"], n + 0)
                for k in range(ML_HEADS):
                    a = nc.scalar.activation(wm[:, k, :], ps[:, 6, k * P:(k + 1) * P], ACT.Exp,
                                             bias=g[:, T_U + k:T_U + k + 1])
                a.then_inc(S["a_wm"], 1)

            def outputs(n, par, prior):
                act.wait_ge(S["d_h"], n * 4 + 4)
                act.wait_ge(S["d_meanm"], n + 0)
                act.wait_ge(S["a_sqy"], n * 2)
                for h in range(ML_HEADS):
                    act.wait_ge(S["a_sqm"], n * 4 + h)
                    nc.scalar.activation(x_sq[:, 0:ML_V], y[:, D + h * ML_V:D + (h + 1) * ML_V], ACT.Square,
                                         accum_out=ssq[:, 2 + h:3 + h]).then_inc(S["a_sqm"], 1)
                act.wait_ge(S["l_yz"], n + 1)
                act.wait_ge(S["a_sqm"], n * 4 + 4)
                act.wait_ge(S["d_meany"], n + 0)
                for k in (0, 1):
                    act.wait_ge(S["a_sqy"], n * 2 + k)
                    nc.scalar.activation(x_sq[:, :], y[:, k * 512:(k + 1) * 512], ACT.Square,
                                         accum_out=ssq[:, k:k + 1]).then_inc(S["a_sqy"], 1)
                act.wait_ge(S["l_rstdy"], n + 1)
                for k in (0, 1):
                    nc.scalar.activation(y[:, k * 512:(k + 1) * 512], y[:, k * 512:(k + 1) * 512], ACT.Copy,
                                         scale=rms[:, k:k + 1]).then_inc(S["a_ynorm"], 1)

            weights(0, 0, 0)

            def body(n, par, prior):
                outputs(n, par, prior)
                weights(n + 1, 1 - par, prior + par)

            over(act, 0, TILES - 1, body)
            outputs(TILES - 1, 1, (TILES - 1) // 2)

        @block.gpsimd
        def _(gp):
            for v in va:
                gp.memset(v[:, :, ML_V:VW], 1.0).then_inc(S["v_ones"], 1)
            gp.memset(state[:, :], 0.0).then_inc(S["zero_ok"], 1)
            gp.memset(cmem[:, :, :], 0.0).then_inc(S["zero_ok"], 1)
            gp.wait_ge(S["v_ones"], 2)
            gp.memset(xdt[:, :], 0.0).then_inc(S["zero_ok"], 1)
            gp.memset(xe[:, :], 0.0).then_inc(S["zero_ok"], 1)
            gp.wait_ge(S["zero_ok"], 4)
            gp.wait_ge(S["drow_ok"], 1)

            def body(n, par, prior):
                gp.wait_ge(S["a_xtok"], n * 2 + 2)
                gp.wait_ge(S["g_ok"], n + 1)
                gp.tensor_tensor(hd(xdt[:, :]), hd(x_tok[:, :]), last(g[:, T_DT:T_DT + SSD_HEADS], SSD_DIM),
                                 ALU.mult).then_inc(S["l_xdt"], 1)
                gp.wait_ge(S["l_xdt"], n + 1)
                gp.tensor_tensor(hd(x_tok[:, :]), hd(x_tok[:, :]), last(d_bc[:, :], SSD_DIM), ALU.mult).then_inc(S["l_xd"], 1)
                gp.wait_ge(S["a_dec"], n * 4 + 4)
                gp.tensor_tensor(hd(xe[:, :]), hd(xdt[:, :]),
                                 dec[:, :, P - 1:P].broadcast_to([P, SSD_HEADS, SSD_DIM]), ALU.mult).then_inc(S["l_xe"], 1)
                gp.wait_ge(S["p_yoff"], n * 2 + 2)
                gp.wait_ge(S["d_eend"], n + 1)
                gp.wait_ge(S["d_state"], n * 2)
                gp.tensor_tensor(hd(state[:, :]), hd(state[:, :]), last(e_end[:, :], SSD_DIM), ALU.mult).then_inc(S["l_sdec"], 1)
                gp.wait_ge(S["d_meanm"], n + 1)
                gp.tensor_tensor(rms[:, 2:6], rms[:, 2:6], half[:, 0:4], ALU.pow).then_inc(S["l_rstdm"], 1)
                gp.wait_ge(S["d_y"], n * 2 + 2)
                gp.wait_ge(S["l_xd"], n + 1)
                gp.tensor_tensor(y[:, 0:D], y[:, 0:D], x_tok[:, :], ALU.add).then_inc(S["l_yd"], 1)
                gp.wait_ge(S["l_yd"], n + 1)
                gp.wait_ge(in_landed[par], prior * 48 + 48)
                gp.tensor_tensor(y[:, 0:D], y[:, 0:D], gz[par][:, 0, :], ALU.mult).then_inc(S["l_yz"], 1)
                gp.wait_ge(S["d_meany"], n + 1)
                gp.tensor_tensor(rms[:, 0:2], rms[:, 0:2], half[:, 0:2], ALU.pow).then_inc(S["l_rstdy"], 1)

            over(gp, 0, TILES, body)

        @block.vector
        def _(dve):
            dve.wait_ge(S["cols_T"], 1)
            dve.tensor_copy(gcols[:, :], ps[:, 7, 0:AB_OUT_T]).then_inc(S["cols_ok"], 1)
            dve.wait_ge(S["drow_T"], 1)
            dve.tensor_copy(d_bc[:, :], ps[:, 6, 0:SSD_HEADS]).then_inc(S["drow_ok"], 1)

            def tables(n):
                dve.wait_ge(S["a_dec"], n * 4)
                dve.wait_ge(S["a_wm"], n + 0)
                dve.wait_ge(S["p_wint"], n + 0)
                dve.wait_ge(S["l_xdt"], n + 0)
                dve.tensor_scalar(g[:, :], table[:, bass.ds(n, 1), :].rearrange("p a k -> p (a k)"), 1.0, None,
                                  ALU.mult).then_inc(S["g_ok"], 1)
                dve.tensor_scalar(mr[:, :, :], maxrows[:, bass.ds(n, 1), :, :].rearrange("h a k t -> h (a k) t"),
                                  1.0, None, ALU.mult).then_inc(S["mr_ok"], 1)
                dve.wait_ge(S["g_ok"], n + 1)

            def weights(n, par, prior):
                dve.wait_ge(S["p_bc"], n + 1)
                for k in (0, 1):
                    dve.wait_ge(S["a_dec"], n * 4 + 2 * (k + 1))
                    dve.tensor_tensor(wt[:, HG * k:HG * (k + 1), :], dec[:, HG * k:HG * (k + 1), :],
                                      mid(ps[:, 3, (2 + k) * P:(3 + k) * P], HG), ALU.mult).then_inc(S["d_wt"], 1)
                dve.wait_ge(S["l_sdec"], n + 0)
                dve.tensor_tensor(e_end[:, :], dec[:, :, P - 1:P].rearrange("p h a -> p (h a)"),
                                  g[:, T_EACS:T_EACS + SSD_HEADS], ALU.mult).then_inc(S["d_eend"], 1)
                dve.wait_ge(S["p_wint"], n + 1)
                dve.wait_ge(in_landed[par], prior * 48 + 48)
                dve.tensor_tensor(qs[:, :, :], fe[par][:, QT:QT + 4, :], b4(7), ALU.mult).then_inc(S["d_qs"], 1)
                dve.wait_ge(S["d_cmem"], n * 4)
                dve.tensor_copy(c_dec[:, :], b4(7)[:, :, P - 1:P].rearrange("p h a -> p (h a)")).then_inc(S["d_cdec"], 1)
                dve.wait_ge(S["a_wm"], n + 1)
                dve.wait_ge(S["p_qk"], n + 1)
                dve.scalar_tensor_tensor(out=st[:, :, :], in0=b4(4), scalar=ML_QK ** -0.5, in1=wm[:, :, :],
                                         op0=ALU.mult, op1=ALU.mult).then_inc(S["d_st"], 1)
                dve.tensor_scalar(gk[:, :], wm[:, :, P - 1:P].rearrange("p h a -> p (h a)"), ML_QK ** -0.5, None,
                                  ALU.mult).then_inc(S["d_gk"], 1)
                dve.wait_ge(S["d_gk"], n + 1)
                dve.wait_ge(S["p_kT"], n + 1)
                dve.tensor_tensor(kg[:, :, :], b4(2), last(gk[:, :], P), ALU.mult).then_inc(S["d_kg"], 1)

            def outputs(n, par, prior):
                dve.wait_ge(S["p_num"], n * 4 + 4)
                dve.tensor_copy(den[:, :], ps[:, 4:8, ML_V:VW].rearrange("p h a -> p (h a)")).then_inc(S["d_den"], 1)
                dve.wait_ge(S["d_den"], n * 4 + 1)
                dve.scalar_tensor_tensor(out=den2[:, :], in0=den[:, :], scalar=-1.0, in1=den[:, :],
                                         op0=ALU.mult, op1=ALU.max).then_inc(S["d_den"], 1)
                dve.wait_ge(S["d_den"], n * 4 + 2)
                dve.tensor_tensor(den2[:, :], den2[:, :], g[:, T_EMT:T_EMT + ML_HEADS], ALU.max).then_inc(S["d_den"], 1)
                dve.wait_ge(S["d_den"], n * 4 + 3)
                dve.reciprocal(den[:, :], den2[:, :]).then_inc(S["d_den"], 1)
                dve.wait_ge(S["d_den"], n * 4 + 4)
                dve.wait_ge(S["p_yT"], n * 4)
                for h in range(ML_HEADS):
                    v = slice(h * ML_V, (h + 1) * ML_V)
                    dve.scalar_tensor_tensor(out=y[:, D + h * ML_V:D + (h + 1) * ML_V], in0=ps[:, 4 + h, 0:ML_V],
                                             scalar=den[:, h:h + 1], in1=gz[par][:, 2, v], op0=ALU.mult,
                                             op1=ALU.mult).then_inc(S["d_h"], 1)
                for k in (0, 1):
                    c = slice(k * 512, (k + 1) * 512)
                    dve.wait_ge(S["p_yoff"], n * 2 + (k + 1))
                    dve.tensor_tensor(hd(t1[:, c]), hd(ps[:, 2 + k, :]),
                                      last(g[:, T_EACS + HG * k:T_EACS + HG * (k + 1)], SSD_DIM), ALU.mult).then_inc(S["d_t1"], 1)
                for k in (0, 1):
                    c = slice(k * 512, (k + 1) * 512)
                    dve.wait_ge(S["p_ydiag"], n * 2 + (k + 1))
                    dve.wait_ge(S["d_t1"], n * 2 + (k + 1))
                    dve.tensor_tensor(y[:, c], ps[:, k, :], t1[:, c], ALU.add).then_inc(S["d_y"], 1)
                dve.wait_ge(S["a_sqm"], n * 4 + 4)
                dve.tensor_scalar(rms[:, 2:6], ssq[:, 2:6], 1.0 / ML_V, EPS, ALU.mult, ALU.add).then_inc(S["d_meanm"], 1)
                dve.wait_ge(S["p_cmem"], n + 1)
                for h in range(ML_HEADS):
                    dve.scalar_tensor_tensor(out=cmem[:, h, :], in0=cmem[:, h, :], scalar=c_dec[:, h:h + 1],
                                             in1=ps[:, 4 + h, 0:VW], op0=ALU.mult, op1=ALU.add).then_inc(S["d_cmem"], 1)
                dve.wait_ge(S["p_state"], n + 1)
                dve.wait_ge(S["l_sdec"], n + 1)
                for k in (0, 1):
                    c = slice(k * 512, (k + 1) * 512)
                    dve.tensor_tensor(state[:, c], state[:, c], ps[:, 2 + k, :], ALU.add).then_inc(S["d_state"], 1)
                dve.wait_ge(S["l_rstdm"], n + 1)
                for h in range(ML_HEADS):
                    v = slice(h * ML_V, (h + 1) * ML_V)
                    yb = y[:, D + h * ML_V:D + (h + 1) * ML_V]
                    a = dve.scalar_tensor_tensor(out=yb, in0=yb, scalar=rms[:, 2 + h:3 + h], in1=gz[par][:, 1, v],
                                                 op0=ALU.mult, op1=ALU.mult)
                a.then_inc(S["d_yb"], 1)
                dve.wait_ge(S["a_sqy"], n * 2 + 2)
                dve.tensor_scalar(rms[:, 0:2], ssq[:, 0:2], 1.0 / 512, EPS, ALU.mult, ALU.add).then_inc(S["d_meany"], 1)

            def project(n, par, prior):
                for b in range(4):
                    dve.wait_ge(S["p_yT"], n * 4 + (b + 1))
                    dve.tensor_tensor(yT[:, 4 * b:4 * b + 4, :], b4(b), last(gcols[:, 4 * b:4 * b + 4], P),
                                      ALU.mult).then_inc(S["d_yT"], 1)
                dve.wait_ge(x_landed[par], prior * 16 + 16)
                for j in (0, 1):
                    c = slice(j * 512, (j + 1) * 512)
                    dve.wait_ge(S["p_out"], n * 2 + (j + 1))
                    dve.tensor_tensor(xres[par][:, c], ps[:, j, :], xres[par][:, c], ALU.add).then_inc(S["d_x1"], 1)

            dve.wait_ge(S["zero_ok"], 4)
            tables(0)
            weights(0, 0, 0)

            def body(n, par, prior):
                outputs(n, par, prior)
                tables(n + 1)
                weights(n + 1, 1 - par, prior + par)
                project(n, par, prior)

            over(dve, 0, TILES - 1, body)
            outputs(TILES - 1, 1, (TILES - 1) // 2)
            project(TILES - 1, 1, (TILES - 1) // 2)


def attention(nc, feat, tok, x1, lams, subln_g, w_out, final_g, out):
    LAMBDA_INIT = 0.8 - 0.6 * float(np.exp(-0.3))
    SCALE = DA_QK ** -0.5
    SLOPES = [2.0 ** (-8.0 * (h + 1) / DA_HEADS) for h in range(DA_HEADS)]
    H = DA_HEADS
    with ExitStack() as ctx:
        ctx.enter_context(nc.cleanup_on_exit())
        m = Part(nc, ctx, "a")
        kT = m.sb("kT", [P, H, SEQ])
        v = m.sb("v", [P, TILES, D])
        bias = m.sb("bias", [P, H, SEQ])
        wout = m.sb("wout", [P, KT, D])
        qT = [m.sb(f"qT{i}", [P, H, P]) for i in (0, 1)]
        z = [m.sb(f"z{i}", [P, D]) for i in (0, 1)]
        xr = [m.sb(f"xr{i}", [P, D]) for i in (0, 1)]
        s0 = [m.sb(f"s0{i}", [P, SEQ]) for i in (0, 1)]
        s1 = [m.sb(f"s1{i}", [P, SEQ]) for i in (0, 1)]
        aT = [m.sb(f"aT{i}", [P, TILES, P]) for i in (0, 1)]
        y = m.sb("y", [P, D])
        yT = m.sb("yT", [P, KT, P])
        res = m.sb("res", [P, D])
        final_bc = m.sb("final_bc", [P, D])
        junk = m.sb("junk", [P, D])
        ident = m.sb("ident", [P, P])
        ones_row = m.sb("ones_row", [1, P])
        lam_in = m.sb("lam_in", [1, 4, DA_QK])
        lam_w = m.sb("lam_w", [1, 2, DA_QK])
        lam2 = m.sb("lam2", [1, 4])
        neg_lam = m.sb("neg_lam", [P, 1])
        g_row = m.sb("g_row", [1, DA_V])
        g_col = m.sb("g_col", [P, 1])
        half = m.sb("half", [P, H])
        mx = [m.sb(f"mx{i}", [P, 2]) for i in (0, 1)]
        nm = [m.sb(f"nm{i}", [P, 2]) for i in (0, 1)]
        sm = [m.sb(f"sm{i}", [P, 2]) for i in (0, 1)]
        rc = [m.sb(f"rc{i}", [P, 2]) for i in (0, 1)]
        coef = [m.sb(f"coef{i}", [P, 1]) for i in (0, 1)]
        r0 = [m.sb(f"r0{i}", [P, H]) for i in (0, 1)]
        rs = m.sb("rs", [P, H])
        fs = m.sb("fs", [P, 1])
        fss = m.sb("fss", [P, 1])
        ps = m.ps("ps", [P, 8, 512])

        names = """const_in wout_in pool_ok iota_ok dist_ok bias_ok lam_mul lam_sum lam_exp lam_ok
                   p_const c_ok p_s0 p_s1 p_at p_o p_yT p_out
                   d_t d_nm d_rc d_coef d_r0 d_a d_o d_sq d_ss d_mean d_yn d_yT d_x2 d_fmean d_res
                   a_p a_at a_fss l_rstd l_yz l_frstd""".split()
        S = {n: m.sem(n) for n in names}
        kv_landed = [m.sem(f"kv_landed{i}") for i in range(TILES)]
        in_landed = [m.sem(f"in_landed{i}") for i in (0, 1)]
        out_stored = m.sem("out_stored")
        score = [ps[:, 2 * j:2 * j + 2, :].rearrange("p b n -> p (b n)") for j in (0, 1)]
        b4 = lambda b: ps[:, b, :].rearrange("p (a t) -> p a t", a=4)
        flat = lambda t: t.rearrange("p a b -> p (a b)")

        block = ctx.enter_context(nc.Block())

        @block.sync
        def _(sp):
            def tile_kv(t):
                ts = slice(t * P, (t + 1) * P)
                sp.dma_start(kT[:, :, ts], feat[H:2 * H, :, ts].rearrange("f p t -> p f t")).then_inc(kv_landed[t], 16)
                sp.dma_start(v[:, t, :], tok[ts, 0:D]).then_inc(kv_landed[t], 16)

            def tile_in(t):
                ts = slice(t * P, (t + 1) * P)
                sp.dma_start(qT[t % 2][:, :, :], feat[0:H, :, ts].rearrange("f p t -> p f t")).then_inc(in_landed[t % 2], 16)
                sp.dma_start(z[t % 2][:, :], tok[ts, D:2 * D]).then_inc(in_landed[t % 2], 16)
                sp.dma_start(xr[t % 2][:, :], x1[ts, :]).then_inc(in_landed[t % 2], 16)

            tile_in(0)
            tile_kv(0)
            for i, r in enumerate(lams):
                sp.dma_start(lam_in[:, i, :], r).then_inc(S["const_in"], 16)
            sp.dma_start(g_row[:, :], subln_g).then_inc(S["const_in"], 16)
            sp.dma_start(final_bc[0:1, :], final_g).then_inc(S["const_in"], 16)
            tile_kv(1)
            tile_in(1)
            sp.dma_start(wout[:, :, :], w_out.rearrange("(k p) n -> p k n", p=P)).then_inc(S["wout_in"], 16)
            for t in range(2, TILES):
                tile_kv(t)
            for t in range(TILES):
                sp.wait_ge(S["d_res"], t + 1)
                sp.dma_start(out[t * P:(t + 1) * P, :], res[:, :]).then_inc(out_stored, 16)
                if t + 2 < TILES:
                    sp.wait_ge(S["l_yz"], t + 1)
                    tile_in(t + 2)
            sp.wait_ge(out_stored, 16 * TILES)

        @block.gpsimd
        def _(gp):
            gp.memset(ident[:, :], 0.0).then_inc(S["pool_ok"], 1)
            gp.memset(ones_row[:, :], 1.0).then_inc(S["pool_ok"], 1)
            gp.memset(half[:, :], -0.5).then_inc(S["pool_ok"], 1)
            gp.wait_ge(S["pool_ok"], 3)
            gp.affine_select(out=ident[:, :], in_=ident[:, :], compare_op=ALU.not_equal, fill=1.0, base=0,
                             pattern=[[-1, P]], channel_multiplier=1).then_inc(S["pool_ok"], 1)
            gp.iota(junk[:, :], pattern=[[-1, SEQ]], base=SEQ - P, channel_multiplier=1,
                    allow_small_or_imprecise_dtypes=True).then_inc(S["iota_ok"], 1)
            gp.wait_ge(S["dist_ok"], 1)
            gp.affine_select(out=junk[:, SEQ - 64:SEQ], in_=junk[:, SEQ - 64:SEQ], compare_op=ALU.is_ge,
                             fill=-MASKED, base=-64, pattern=[[0, 64]], channel_multiplier=1).then_inc(S["iota_ok"], 1)
            for t in range(TILES):
                gp.wait_ge(S["d_mean"], t + 1)
                gp.tensor_tensor(rs[:, :], rs[:, :], half[:, :], ALU.pow).then_inc(S["l_rstd"], 1)
                gp.wait_ge(S["d_yn"], t + 1)
                gp.wait_ge(in_landed[t % 2], 48 * (t // 2 + 1))
                gp.tensor_tensor(y[:, :], y[:, :], z[t % 2][:, :], ALU.mult).then_inc(S["l_yz"], 1)
                gp.wait_ge(S["d_fmean"], t + 1)
                gp.tensor_tensor(fs[:, :], fs[:, :], half[:, 0:1], ALU.pow).then_inc(S["l_frstd"], 1)

        @block.tensor
        def _(pe):
            pe.wait_ge(S["lam_ok"], 1)
            pe.wait_ge(S["const_in"], 16 * 6)
            pe.wait_ge(S["pool_ok"], 4)
            pe.matmul(ps[:, 7, 0:1], ones_row[:, :], lam2[:, 2:3], start=True, stop=True)
            pe.matmul(ps[:, 7, 1:2], g_row[:, :], ones_row[:, 0:1], start=True, stop=True)
            for j in (0, 1):
                mm = pe.matmul(ps[:, 4 + j, :], ones_row[:, :], final_bc[0:1, j * 512:(j + 1) * 512], start=True, stop=True)
            mm.then_inc(S["p_const"], 1)

            def scores(t, h):
                n, W = t * H + h, (t + 1) * P
                if h == 0:
                    pe.wait_ge(in_landed[t % 2], 48 * (t // 2 + 1))
                    pe.wait_ge(kv_landed[t], 32)
                for j in (0, 1):
                    if n:
                        pe.wait_ge(S["d_t"], 2 * n - 1 + j)
                    r = slice(j * DA_QK, (j + 1) * DA_QK)
                    for c in range(0, W, 512):
                        w = min(512, W - c)
                        mm = pe.matmul(ps[:, 2 * j + c // 512, 0:w], qT[t % 2][r, h, :], kT[r, h, c:c + w],
                                       start=True, stop=True)
                    mm.then_inc(S["p_s0" if j == 0 else "p_s1"], 1)

            def values(t, h):
                n = t * H + h
                pe.wait_ge(S["d_a"], n + 1)
                pe.wait_ge(S["a_at"], at_before[n])
                if n == 0:
                    pe.wait_ge(S["c_ok"], 3)
                if h == PROJECT + 1 and t:
                    pe.wait_ge(S["d_x2"], 2 * t)
                for k in range(t + 1):
                    mm = pe.transpose(ps[:, 4 + k // 4, (k % 4) * P:(k % 4 + 1) * P], s0[n % 2][:, k * P:(k + 1) * P],
                                      ident[:, :])
                    if k == 3 or k == t:
                        mm.then_inc(S["p_at"], 1)
                pe.wait_ge(S["a_at"], at_before[n + 1])
                if h == 0:
                    pe.wait_ge(S["d_o"], 2 * t)
                for k in range(t + 1):
                    mm = pe.matmul(ps[:, 6 + h // 4, (h % 4) * P:(h % 4 + 1) * P], aT[n % 2][:, k, :],
                                   v[:, k, h * DA_V:(h + 1) * DA_V], start=(k == 0), stop=(k == t))
                mm.then_inc(S["p_o"], 1)

            def project(t):
                pe.wait_ge(S["l_yz"], t + 1)
                pe.wait_ge(S["wout_in"], 16)
                for k in range(KT):
                    mm = pe.transpose(ps[:, 4 + k // 4, (k % 4) * P:(k % 4 + 1) * P], y[:, k * P:(k + 1) * P], ident[:, :])
                    if k % 4 == 3:
                        mm.then_inc(S["p_yT"], 1)
                pe.wait_ge(S["d_yT"], 2 * t + 2)
                for j in (0, 1):
                    for k in range(KT):
                        mm = pe.matmul(ps[:, 4 + j, :], yT[:, k, :], wout[:, k, j * 512:(j + 1) * 512],
                                       start=(k == 0), stop=(k == KT - 1))
                    mm.then_inc(S["p_out"], 1)

            scores(0, 0)
            for t in range(TILES):
                for h in range(H):
                    if (t, h) != (TILES - 1, H - 1):
                        scores(t + (h + 1) // H, (h + 1) % H)
                    values(t, h)
                    if h == PROJECT and t:
                        project(t - 1)
            project(TILES - 1)

        @block.scalar
        def _(act):
            act.wait_ge(S["lam_sum"], 2)
            nc.scalar.activation(lam2[:, 0:2], lam2[:, 0:2], ACT.Exp).then_inc(S["lam_exp"], 1)

            def softmax(t, h):
                n, W = t * H + h, (t + 1) * P
                act.wait_ge(S["d_nm"], n + 1)
                if n >= 2:
                    act.wait_ge(S["d_coef"], n - 1)
                for j, s in ((0, s0), (1, s1)):
                    nc.scalar.activation(s[n % 2][:, 0:W], s[n % 2][:, 0:W], ACT.Exp, bias=nm[n % 2][:, j:j + 1],
                                         scale=SCALE, accum_out=sm[n % 2][:, j:j + 1]).then_inc(S["a_p"], 1)

            def evict(t, h):
                n = t * H + h
                if n >= 2:
                    act.wait_ge(S["p_o"], n - 1)
                for b in range(t // 4 + 1):
                    w = min(4, t + 1 - 4 * b)
                    act.wait_ge(S["p_at"], at_before[n] + b + 1)
                    nc.scalar.copy(aT[n % 2][:, 4 * b:4 * b + w, :], b4(4 + b)[:, 0:w, :]).then_inc(S["a_at"], 1)

            def final_squares(t):
                act.wait_ge(S["d_x2"], 2 * t + 2)
                act.wait_ge(out_stored, 16 * t)
                nc.scalar.activation(res[:, :], xr[t % 2][:, :], ACT.Square, accum_out=fss[:, :]).then_inc(S["a_fss"], 1)

            softmax(0, 0)
            for t in range(TILES):
                for h in range(H):
                    if (t, h) != (TILES - 1, H - 1):
                        softmax(t + (h + 1) // H, (h + 1) % H)
                    evict(t, h)
                    if h == PROJECT + 1 and t:
                        final_squares(t - 1)
            final_squares(TILES - 1)

        @block.vector
        def _(dve):
            dve.wait_ge(S["const_in"], 16 * 6)
            for i in (0, 1):
                dve.tensor_tensor_reduce(lam_w[:, i, :], lam_in[:, 2 * i, :], lam_in[:, 2 * i + 1, :], 1.0, 0.0,
                                         ALU.mult, ALU.add, lam2[:, i:i + 1]).then_inc(S["lam_sum"], 1)
            dve.wait_ge(S["lam_exp"], 1)
            dve.tensor_tensor(lam2[:, 3:4], lam2[:, 1:2], lam2[:, 0:1], ALU.subtract).then_inc(S["lam_mul"], 1)
            dve.wait_ge(S["lam_mul"], 1)
            dve.tensor_scalar(lam2[:, 2:3], lam2[:, 3:4], -LAMBDA_INIT, None, ALU.add).then_inc(S["lam_ok"], 1)
            dve.wait_ge(S["iota_ok"], 1)
            dve.scalar_tensor_tensor(out=junk[:, :], in0=junk[:, :], scalar=-1.0, in1=junk[:, :], op0=ALU.mult,
                                     op1=ALU.max).then_inc(S["dist_ok"], 1)
            dve.wait_ge(S["iota_ok"], 2)
            for h in range(H):
                dve.tensor_scalar(bias[:, h, :], junk[:, :], -SLOPES[h] / SCALE, None, ALU.mult).then_inc(S["bias_ok"], 1)
            dve.wait_ge(S["p_const"], 1)
            dve.tensor_copy(neg_lam[:, :], ps[:, 7, 0:1]).then_inc(S["c_ok"], 1)
            dve.tensor_scalar(g_col[:, :], ps[:, 7, 1:2], 1.0 - LAMBDA_INIT, None, ALU.mult).then_inc(S["c_ok"], 1)
            dve.tensor_copy(final_bc[:, :], ps[:, 4:6, :].rearrange("p b n -> p (b n)")).then_inc(S["c_ok"], 1)
            dve.wait_ge(S["c_ok"], 3)
            dve.wait_ge(S["bias_ok"], H)

            def maxima(t, h):
                n, W = t * H + h, (t + 1) * P
                if n >= 2:
                    dve.wait_ge(S["p_at"], at_before[n - 1])
                    dve.wait_ge(S["a_p"], 2 * n - 2)
                for j, s in ((0, s0), (1, s1)):
                    dve.wait_ge(S["p_s0" if j == 0 else "p_s1"], n + 1)
                    dve.tensor_tensor_reduce(s[n % 2][:, 0:W], score[j][:, 0:W], bias[:, h, SEQ - W:SEQ], 1.0, -3e38,
                                             ALU.add, ALU.max, mx[n % 2][:, j:j + 1]).then_inc(S["d_t"], 1)
                dve.wait_ge(S["d_t"], 2 * n + 2)
                dve.tensor_scalar(nm[n % 2][:, :], mx[n % 2][:, :], -SCALE, None, ALU.mult).then_inc(S["d_nm"], 1)

            def combine(t, h):
                n, W = t * H + h, (t + 1) * P
                b = n % 2
                dve.wait_ge(S["a_p"], 2 * n + 2)
                dve.reciprocal(rc[b][:, :], sm[b][:, :]).then_inc(S["d_rc"], 1)
                dve.wait_ge(S["d_rc"], n + 1)
                dve.scalar_tensor_tensor(out=coef[b][:, :], in0=sm[b][:, 0:1], scalar=neg_lam[:, 0:1],
                                         in1=rc[b][:, 1:2], op0=ALU.mult, op1=ALU.mult).then_inc(S["d_coef"], 1)
                dve.tensor_copy(r0[t % 2][:, h:h + 1], rc[b][:, 0:1]).then_inc(S["d_r0"], 1)
                dve.wait_ge(S["d_coef"], n + 1)
                dve.scalar_tensor_tensor(out=s0[b][:, 0:W], in0=s1[b][:, 0:W], scalar=coef[b][:, 0:1],
                                         in1=s0[b][:, 0:W], op0=ALU.mult, op1=ALU.add).then_inc(S["d_a"], 1)

            hv = lambda ap: ap.rearrange("p (h v) -> p h v", v=DA_V)

            def normalise(t):
                dve.wait_ge(S["p_o"], H * (t + 1))
                dve.wait_ge(S["d_r0"], H * (t + 1))
                dve.wait_ge(S["p_yT"], 2 * t)
                for j in (0, 1):
                    c = slice(j * 512, (j + 1) * 512)
                    dve.tensor_tensor(hv(y[:, c]), b4(6 + j), last(r0[t % 2][:, 4 * j:4 * j + 4], DA_V),
                                      ALU.mult).then_inc(S["d_o"], 1)
                dve.wait_ge(S["d_o"], 2 * t + 2)
                dve.tensor_tensor(junk[:, :], y[:, :], y[:, :], ALU.mult).then_inc(S["d_sq"], 1)
                dve.wait_ge(S["d_sq"], t + 1)
                dve.tensor_reduce(rs[:, :], hv(junk[:, :]), AX.X, ALU.add).then_inc(S["d_ss"], 1)
                dve.wait_ge(S["d_ss"], t + 1)
                dve.tensor_scalar(rs[:, :], rs[:, :], 1.0 / DA_V, EPS, ALU.mult, ALU.add).then_inc(S["d_mean"], 1)
                dve.wait_ge(S["l_rstd"], t + 1)
                dve.tensor_tensor(hv(y[:, :]), hv(y[:, :]), last(rs[:, :], DA_V), ALU.mult).then_inc(S["d_yn"], 1)

            def turned(t):
                for b in (0, 1):
                    dve.wait_ge(S["p_yT"], 2 * t + b + 1)
                    dve.tensor_scalar(yT[:, 4 * b:4 * b + 4, :], b4(4 + b), g_col[:, 0:1], None, ALU.mult).then_inc(S["d_yT"], 1)

            def residual(t):
                for j in (0, 1):
                    c = slice(j * 512, (j + 1) * 512)
                    dve.wait_ge(S["p_out"], 2 * t + j + 1)
                    dve.tensor_tensor(xr[t % 2][:, c], ps[:, 4 + j, :], xr[t % 2][:, c], ALU.add).then_inc(S["d_x2"], 1)

            def final(t):
                dve.wait_ge(S["a_fss"], t + 1)
                dve.tensor_scalar(fs[:, :], fss[:, :], 1.0 / D, EPS, ALU.mult, ALU.add).then_inc(S["d_fmean"], 1)
                dve.wait_ge(S["l_frstd"], t + 1)
                dve.wait_ge(out_stored, 16 * t)
                dve.scalar_tensor_tensor(out=res[:, :], in0=xr[t % 2][:, :], scalar=fs[:, 0:1], in1=final_bc[:, :],
                                         op0=ALU.mult, op1=ALU.mult).then_inc(S["d_res"], 1)

            maxima(0, 0)
            for t in range(TILES):
                for h in range(H):
                    if (t, h) != (TILES - 1, H - 1):
                        maxima(t + (h + 1) // H, (h + 1) % H)
                    combine(t, h)
                    if t and h == 0:
                        normalise(t - 1)
                    if t and h == PROJECT:
                        turned(t - 1)
                    if t and h == PROJECT + 1:
                        residual(t - 1)
                    if t and h == PROJECT + 2:
                        final(t - 1)
            normalise(TILES - 1)
            turned(TILES - 1)
            residual(TILES - 1)
            final(TILES - 1)


PROJECT = 1
at_before = [sum(n // DA_HEADS // 4 + 1 for n in range(m)) for m in range(TILES * DA_HEADS + 1)]


def hybrid(nc, x, ab_norm_g, ab_w_in, ab_ssd_conv_w, ab_ssd_conv_b, ab_dt_bias, ab_a_log, ab_d_skip, ab_ssd_norm_g,
           ab_ml_conv_w, ab_ml_conv_b, ab_i_bias, ab_f_bias, ab_ml_norm_g, ab_w_out, c_norm_g, c_w_in, c_lam_q1,
           c_lam_k1, c_lam_q2, c_lam_k2, c_subln_g, c_w_out, final_norm_g, out):
    def scratch(name, shape):
        return nc.dram_tensor(name, shape, F32, kind="Internal").ap()

    def rows(v):
        return v.rearrange("a (r c) -> (a r) c", c=P)

    feat0 = scratch("feat0", [FEAT_T, P, SEQ])
    tok0 = scratch("tok0", [SEQ, 4 * D])
    gates = scratch("gates", [GATES, SEQ])
    x1 = scratch("x1", [SEQ, D])
    feat1 = scratch("feat1", [2 * DA_HEADS, P, SEQ])
    tok1 = scratch("tok1", [SEQ, 2 * D])
    x_in = x[0]
    taps = [r for j in range(CONV) for r in (rows(ab_ssd_conv_w[0, j:j + 1, :]), rows(ab_ml_conv_w[0, j:j + 1, :]))]

    projection(nc, "p", x_in, ab_w_in[0], [rows(ab_norm_g)] + taps + [rows(ab_ssd_conv_b), rows(ab_ml_conv_b)],
               [C_XBC, C_XBC + BLK, C_XBC + 2 * BLK, C_Q, C_K], feat0,
               [(C_ZA, ACT.Silu), (C_ZA + BLK, ACT.Silu), (C_ZB, ACT.Silu), (C_ZB + BLK, ACT.Silu),
                (C_OG, ACT.Sigmoid), (C_OG + BLK, ACT.Sigmoid), (C_V, ACT.Copy), (C_V + BLK, ACT.Copy)],
               tok0, conv=True, gate_out=gates)
    with ExitStack() as ctx:
        m = Part(nc, ctx, "k")
        keep = dict(table=m.sb("table", [P, TILES, T_ALL]), maxrows=m.sb("maxrows", [ML_HEADS, TILES, 2, P]),
                    ident=m.sb("ident", [P, P]), ident_bf=m.sb("ident_bf", [P, P], BF16), tri=m.sb("tri", [P, P]),
                    later=m.sb("later", [P, P], BF16), head_row=m.sb("head_row", [ML_HEADS, ML_HEADS, P]),
                    half=m.sb("half", [P, ML_HEADS]))
        scan_gates(nc, keep, gates, ab_dt_bias, ab_a_log, ab_i_bias, ab_f_bias)
        scan_chunks(nc, keep, x_in, feat0, tok0, ab_w_out[0], [rows(ab_ssd_norm_g), rows(ab_ml_norm_g)], ab_d_skip, x1)
    projection(nc, "q", x1, c_w_in[0], [rows(c_norm_g)], [0, BLK, D, D + BLK], feat1,
               [(2 * D, ACT.Copy), (2 * D + BLK, ACT.Copy), (3 * D, ACT.Silu), (3 * D + BLK, ACT.Silu)], tok1)
    attention(nc, feat1, tok1, x1, [c_lam_q1, c_lam_k1, c_lam_q2, c_lam_k2], c_subln_g, c_w_out[0],
              final_norm_g.rearrange("(a n) -> a n", a=1), out[0])


_INS = ['x', 'ab_norm_g', 'ab_w_in', 'ab_ssd_conv_w', 'ab_ssd_conv_b', 'ab_dt_bias', 'ab_a_log', 'ab_d_skip',
        'ab_ssd_norm_g', 'ab_ml_conv_w', 'ab_ml_conv_b', 'ab_i_bias', 'ab_f_bias', 'ab_ml_norm_g', 'ab_w_out',
        'c_norm_g', 'c_w_in', 'c_lam_q1', 'c_lam_k1', 'c_lam_q2', 'c_lam_k2', 'c_subln_g', 'c_w_out',
        'final_norm_g']


def kernel(**inputs):
    import concourse.bacc as bacc
    from concourse.bass_utils import run_bass_kernel_spmd

    nc = bacc.Bacc("TRN2", target_bir_lowering=False, num_devices=1)
    arrays, args = {}, []
    for name in _INS:
        a = np.ascontiguousarray(inputs[name])
        arrays[f"in_{name}"] = a
        args.append(nc.dram_tensor(f"in_{name}", a.shape, mybir.dt.from_np(a.dtype), kind="ExternalInput").ap())
    args.append(nc.dram_tensor("out_0", (1, SEQ, D), F32, kind="ExternalOutput").ap())
    hybrid(nc, *args)
    r = run_bass_kernel_spmd(nc, [arrays], core_ids=[0])
    return r.results[0]["out_0"]
```

```python
from contextlib import ExitStack

import numpy as np

import concourse.bass as bass
from concourse import mybir

F32 = mybir.dt.float32
F32R = mybir.dt.float32r
BF16 = mybir.dt.bfloat16
ALU = mybir.AluOpType
ACT = mybir.ActivationFunctionType
AX = mybir.AxisListType

P = 128
SEQ = 1024
D = 1024
TILES = SEQ // P
KT = D // P
BLK = 512
EPS = 1e-6
MASKED = -1e30

SSD_HEADS, SSD_DIM, SSD_STATE, SSD_GROUPS = 16, 64, 128, 2
SSD_INNER = SSD_HEADS * SSD_DIM
SSD_XBC = SSD_INNER + 2 * SSD_GROUPS * SSD_STATE
ML_HEADS, ML_QK, ML_V = 4, 128, 256
ML_INNER = ML_HEADS * ML_V
CONV = 4
GATES = SSD_HEADS + 2 * ML_HEADS
DECAYS = SSD_HEADS + ML_HEADS
XBC_T = SSD_XBC // P
QK_T = 2 * ML_HEADS * ML_QK // P
FEAT_T = XBC_T + QK_T
AB_OUT_T = (SSD_INNER + ML_INNER) // P

DA_HEADS, DA_QK, DA_V = 8, 64, 128

C_ZA = 0
C_XBC = C_ZA + SSD_INNER
C_DT = C_XBC + SSD_XBC
C_ZB = C_DT + SSD_HEADS
C_Q = C_ZB + ML_INNER
C_K = C_Q + ML_HEADS * ML_QK
C_V = C_K + ML_HEADS * ML_QK
C_IG = C_V + ML_INNER
C_OG = C_IG + 2 * ML_HEADS


def over(eng, first, count, body):
    while first < 2 and count:
        body(first, first % 2, first // 2)
        first, count = first + 1, count - 1
    pairs = count // 2
    if pairs:
        with eng.Fori(0, pairs) as i:
            for j in (0, 1):
                body(i * 2 + (first + j), (first + j) % 2, i + (first + j) // 2)
    if count % 2:
        n = first + count - 1
        body(n, n % 2, n // 2)


class Part:

    def __init__(self, nc, ctx, tag):
        self.nc, self.ctx, self.tag = nc, ctx, tag

    def sb(self, name, shape, dt=F32):
        return self.ctx.enter_context(self.nc.sbuf_tensor(f"{self.tag}_{name}", shape, dt))

    def ps(self, name, shape, dt=F32):
        return self.ctx.enter_context(self.nc.psum_tensor(f"{self.tag}_{name}", shape, dt))

    def sem(self, name):
        return self.nc.alloc_semaphore(f"{self.tag}_{name}")


def mid(ap, n):
    a = ap.unsqueeze(1)
    return a.broadcast_to([a.shape[0], n] + list(a.shape[2:]))


def last(ap, n):
    a = ap.unsqueeze(len(ap.shape))
    return a.broadcast_to(list(a.shape[:-1]) + [n])


def identity(gp, t, sem, done):
    gp.memset(t[:, :], 0.0).then_inc(sem, 1)
    gp.wait_ge(sem, done - 1)
    gp.affine_select(out=t[:, :], in_=t[:, :], compare_op=ALU.not_equal, fill=1.0, base=0,
                     pattern=[[-1, P]], channel_multiplier=1).then_inc(sem, 1)


def projection(nc, tag, x, w_in, rows, feat_cols, feat_out, tok_blocks, tok_out, conv=False, gate_out=None):
    nrows = sum(r.shape[0] for r in rows)
    nf, nt = len(feat_cols), len(tok_blocks)
    nb = nf + nt
    w_tiled = w_in.rearrange("(k p) n -> p k n", p=P)
    with ExitStack() as ctx:
        ctx.enter_context(nc.cleanup_on_exit())
        m = Part(nc, ctx, tag)
        h_hi = m.sb("h_hi", [P, KT, SEQ], F32R)
        h_lo = m.sb("h_lo", [P, KT, SEQ], F32R)
        w_raw = [m.sb(f"w_raw{i}", [P, KT, BLK]) for i in (0, 1)]
        w_hi = [m.sb(f"w_hi{i}", [P, KT, BLK], F32R) for i in (0, 1)]
        w_lo = [m.sb(f"w_lo{i}", [P, KT, BLK], F32R) for i in (0, 1)]
        XIN = 4
        x_in = [w_raw[1][:, 2 * i:2 * i + 2, :].rearrange("p a n -> p (a n)") for i in range(XIN)]
        h_f = [m.sb(f"h_f{i}", [P, 4, P]) for i in (0, 1)]
        stage = [m.sb(f"stage{i}", [P, BLK]) for i in range(4)]
        ident = m.sb("ident", [P, P])
        row_in = m.sb("row_in", [P, P])
        cols = m.sb("cols", [P, nrows])
        junk = m.sb("junk", [P, D])
        sumsq = [m.sb(f"sumsq{i}", [P, 1]) for i in (0, 1)]
        rstd = [m.sb(f"rstd{i}", [P, 1]) for i in (0, 1)]
        half = m.sb("half", [P, 1])
        if conv:
            c_raw = [m.sb(f"c_raw{i}", [P, CONV - 1 + SEQ]) for i in (0, 1)]
            c_acc = [junk, m.sb("c_acc1", [P, SEQ])]
        if gate_out is not None:
            g_raw = m.sb("g_raw", [P, KT, GATES])
            g_hi = m.sb("g_hi", [P, KT, GATES], F32R)
            g_lo = m.sb("g_lo", [P, KT, GATES], F32R)
            g_st = m.sb("g_st", [GATES, SEQ])
        bank = [m.ps(f"bank{i}", [P, 512]) for i in range(8)]
        t_bank = [[bank[1], bank[3]], [bank[5], bank[7]]]
        FIRST_ORDER = [0, 2, 4, 6, 1, 3, 5, 7]
        FIRST = 4

        rows_in = m.sem("rows_in")
        x_landed = [m.sem(f"x_landed{i}") for i in range(XIN)]
        w0_landed = [m.sem(f"w0_landed{i}") for i in range(FIRST)]
        w_landed = [m.sem(f"w_landed{i}") for i in (0, 1)]
        g_landed = m.sem("g_landed")
        ident_ok = m.sem("ident_ok")
        zeroed = m.sem("zeroed")
        rows_T = m.sem("rows_T")
        cols_ok = m.sem("cols_ok")
        squared = m.sem("squared")
        mean_ok = m.sem("mean_ok")
        rstd_ok = m.sem("rstd_ok")
        normed = m.sem("normed")
        x_T = m.sem("x_T")
        hf_ok = m.sem("hf_ok")
        hhi_ok = m.sem("hhi_ok")
        h_ok = m.sem("h_ok")
        hi_ok = m.sem("hi_ok")
        split = m.sem("split")
        g_split = m.sem("g_split")
        full = m.sem("full")
        staged = m.sem("staged")
        stored = [m.sem(f"stored{i}") for i in range(4)]
        conv_in = m.sem("conv_in")
        tapped = m.sem("tapped")
        conv_ok = m.sem("conv_ok")
        silu_ok = m.sem("silu_ok")
        c_stored = [m.sem(f"c_stored{i}") for i in (0, 1)]
        g_full = m.sem("g_full")
        g_staged = m.sem("g_staged")
        g_stored = m.sem("g_stored")

        block = ctx.enter_context(nc.Block())

        @block.sync
        def _(sp):
            at = 0
            sp.dma_start(x_in[0], x[0:P, :]).then_inc(x_landed[0], 16)
            for r in rows:
                sp.dma_start(row_in[at:at + r.shape[0], :], r).then_inc(rows_in, 16)
                at += r.shape[0]

            def load_x(t):
                if t >= XIN:
                    sp.wait_ge(x_T, 2 * (t - XIN + 1))
                sp.dma_start(x_in[t % XIN], x[t * P:(t + 1) * P, :]).then_inc(x_landed[t % XIN], 16)

            def load_w0(f):
                c = feat_cols[0] + f * P
                sp.dma_start(w_raw[0][:, :, f * P:(f + 1) * P], w_tiled[:, :, c:c + P]).then_inc(w0_landed[f], 16)

            def load_w(b):
                c = feat_cols[b] if b < nf else tok_blocks[b - nf][0]
                if b >= 2:
                    sp.wait_ge(split, FIRST + b - 2)
                sp.dma_start(w_raw[b % 2][:, :, :], w_tiled[:, :, c:c + BLK]).then_inc(w_landed[b % 2], 16)

            load_x(1)
            load_w0(0)
            load_x(2)
            load_x(3)
            for f in range(1, FIRST):
                load_w0(f)
                load_x(3 + f)
            load_x(7)
            sp.wait_ge(x_T, 2 * TILES)
            load_w(1)
            if gate_out is not None:
                with nc.allow_non_contiguous_dma(reason="24 gate columns"):
                    sp.dma_start(g_raw[:, :, 0:SSD_HEADS], w_tiled[:, :, C_DT:C_DT + SSD_HEADS]).then_inc(g_landed, 16)
                    sp.dma_start(g_raw[:, :, SSD_HEADS:GATES],
                                 w_tiled[:, :, C_IG:C_IG + 2 * ML_HEADS]).then_inc(g_landed, 16)
            for b in range(nb):
                if b + 2 < nb:
                    load_w(b + 2)
                if b < nf and conv:
                    for f in range(4):
                        n = 4 * b + f
                        sp.wait_ge(silu_ok, n + 1)
                        sp.dma_start(feat_out[n, :, :], c_acc[f % 2][:, :]).then_inc(c_stored[f % 2], 16)
                    continue
                for o in range(8):
                    sp.wait_ge(staged, 8 * (b - (nf if conv else 0)) + o + 1)
                    if b < nf:
                        dst = feat_out[4 * b + o // 2, :, (o % 2) * BLK:(o % 2 + 1) * BLK]
                    else:
                        dst = tok_out[o * P:(o + 1) * P, (b - nf) * BLK:(b - nf + 1) * BLK]
                    sp.dma_start(dst, stage[o % 4][:, :]).then_inc(stored[o % 4], 16)
            if gate_out is not None:
                sp.wait_ge(g_staged, 2)
                sp.dma_start(gate_out, g_st[:, :]).then_inc(g_stored, 16)
                sp.wait_ge(g_stored, 16)
            for s in range(4):
                sp.wait_ge(stored[s], 16 * 2 * (nb - (nf if conv else 0)))
            if conv:
                for s in (0, 1):
                    sp.wait_ge(c_stored[s], 16 * 2 * nf)

        @block.gpsimd
        def _(gp):
            identity(gp, ident, ident_ok, 2)
            gp.memset(half[:, :], -0.5).then_inc(zeroed, 1)
            if conv:
                for c in c_raw:
                    gp.memset(c[:, 0:CONV - 1], 0.0).then_inc(zeroed, 1)
            gp.wait_ge(zeroed, 1)

            for t in range(TILES):
                r = rstd[t % 2][:, :]
                gp.wait_ge(squared, t + 1)
                if t >= 2:
                    gp.wait_ge(normed, t - 1)
                gp.tensor_scalar(r, sumsq[t % 2][:, :], 1.0 / D, EPS, ALU.mult, ALU.add).then_inc(mean_ok, 1)
                gp.wait_ge(mean_ok, t + 1)
                gp.tensor_tensor(r, r, half[:, :], ALU.pow).then_inc(rstd_ok, 1)

        @block.scalar
        def _(act):
            for t in range(TILES):
                act.wait_ge(x_landed[t % XIN], 16 * (t // XIN + 1))
                if t:
                    act.wait_ge(squared, t)
                nc.scalar.activation(junk[:, :], x_in[t % XIN], ACT.Square, accum_out=sumsq[t % 2][:, :]).then_inc(squared, 1)
                act.wait_ge(rstd_ok, t + 1)
                nc.scalar.activation(x_in[t % XIN], x_in[t % XIN], ACT.Copy, scale=rstd[t % 2][:, 0:1]).then_inc(normed, 1)

            if conv:
                def feature_block(b, order=range(8)):
                    for f in range(4):
                        for s in (0, 1):
                            o = 2 * f + s
                            act.wait_ge(full, b * 8 + (order.index(o) + 1))
                            nc.scalar.copy(c_raw[f % 2][:, CONV - 1 + s * BLK:CONV - 1 + (s + 1) * BLK],
                                           bank[o][:, :]).then_inc(conv_in, 1)
                        act.wait_ge(conv_ok, b * 4 + (f + 1))
                        nc.scalar.activation(c_acc[f % 2][:, :], c_acc[f % 2][:, :], ACT.Silu).then_inc(silu_ok, 1)

                feature_block(0, FIRST_ORDER)
                with act.Fori(1, nf) as b:
                    feature_block(b)
            for b in range(0 if not conv else nf, nb):
                func = ACT.Copy if b < nf else tok_blocks[b - nf][1]
                for o in range(8):
                    k = b - (nf if conv else 0)
                    act.wait_ge(full, 8 * b + (FIRST_ORDER.index(o) if b == 0 else o) + 1)
                    act.wait_ge(stored[o % 4], 16 * (2 * k + o // 4))
                    nc.scalar.activation(stage[o % 4][:, :], bank[o][:, :], func).then_inc(staged, 1)
            if gate_out is not None:
                for s in (0, 1):
                    act.wait_ge(g_full, s + 1)
                    nc.scalar.copy(g_st[:, s * BLK:(s + 1) * BLK], bank[s][0:GATES, :]).then_inc(g_staged, 1)

        @block.vector
        def _(dve):
            dve.wait_ge(rows_T, 1)
            dve.tensor_copy(cols[:, :], bank[7][:, 0:nrows]).then_inc(cols_ok, 1)
            dve.wait_ge(cols_ok, 1)

            def transposed(t):
                for s in (0, 1):
                    dve.wait_ge(x_T, t * 2 + (s + 1))
                    if t and s == 0:
                        dve.wait_ge(h_ok, t * 2)
                    dve.tensor_tensor(h_f[s][:, :, :], t_bank[t % 2][s][:, :].rearrange("p (a b) -> p a b", a=4),
                                      last(cols[:, 4 * s:4 * s + 4], P), ALU.mult).then_inc(hf_ok, 1)
                    dve.wait_ge(hf_ok, t * 2 + (s + 1))
                    dve.tensor_copy(h_hi[:, 4 * s:4 * s + 4, t * P:(t + 1) * P], h_f[s][:, :, :]).then_inc(hhi_ok, 1)
                    dve.wait_ge(hhi_ok, t * 2 + (s + 1))
                    dve.tensor_tensor(h_lo[:, 4 * s:4 * s + 4, t * P:(t + 1) * P], h_f[s][:, :, :],
                                      h_hi[:, 4 * s:4 * s + 4, t * P:(t + 1) * P].bitcast(F32),
                                      ALU.subtract).then_inc(h_ok, 1)

            def split_first(f):
                c = slice(f * P, (f + 1) * P)
                dve.wait_ge(w0_landed[f], 16)
                dve.tensor_copy(w_hi[0][:, :, c], w_raw[0][:, :, c]).then_inc(hi_ok, 1)
                dve.wait_ge(hi_ok, f + 1)
                dve.tensor_tensor(w_lo[0][:, :, c], w_raw[0][:, :, c], w_hi[0][:, :, c].bitcast(F32),
                                  ALU.subtract).then_inc(split, 1)

            quarter_after = {1: 0, 3: 1, 4: 2, 5: 3}
            for t in range(TILES):
                transposed(t)
                if t in quarter_after:
                    split_first(quarter_after[t])

            def split_block(n, par, prior):
                dve.wait_ge(w_landed[par], prior * 16 + 16 * par)
                if not isinstance(n, int) or n >= 2:
                    dve.wait_ge(full, (n - 1) * 8)
                dve.tensor_copy(w_hi[par][:, :, :], w_raw[par][:, :, :]).then_inc(hi_ok, 1)
                dve.wait_ge(hi_ok, n + FIRST)
                dve.tensor_tensor(w_lo[par][:, :, :], w_raw[par][:, :, :], w_hi[par][:, :, :].bitcast(F32),
                                  ALU.subtract).then_inc(split, 1)

            if gate_out is not None:
                dve.wait_ge(g_landed, 32)
                dve.tensor_copy(g_hi[:, :, :], g_raw[:, :, :]).then_inc(g_split, 1)
                dve.wait_ge(g_split, 1)
                dve.tensor_tensor(g_lo[:, :, :], g_raw[:, :, :], g_hi[:, :, :].bitcast(F32),
                                  ALU.subtract).then_inc(g_split, 1)
            if conv:
                dve.wait_ge(zeroed, 3)

                def conv_tile(n, b, f):
                    raw, acc = c_raw[f % 2], c_acc[f % 2]
                    dve.wait_ge(conv_in, n * 2 + 2)
                    dve.wait_ge(c_stored[f % 2], b * 32 + 16 * (f // 2))
                    dve.tensor_scalar(acc[:, :], raw[:, 0:SEQ], cols[:, bass.ds(n + KT, 1)],
                                      cols[:, bass.ds(n + (KT + CONV * FEAT_T), 1)], ALU.mult, ALU.add).then_inc(tapped, 1)
                    for j in range(1, CONV):
                        dve.wait_ge(tapped, n * (CONV - 1) + j)
                        out = dve.scalar_tensor_tensor(
                            out=acc[:, :], in0=raw[:, j:j + SEQ], scalar=cols[:, bass.ds(n + (KT + j * FEAT_T), 1)],
                            in1=acc[:, :], op0=ALU.mult, op1=ALU.add)
                        out.then_inc(tapped if j < CONV - 1 else conv_ok, 1)

                def feature_block(b, par, prior):
                    split_block(b + 1, 1 - par, prior + par)
                    for f in range(4):
                        conv_tile(b * 4 + f, b, f)

                over(dve, 0, nf, feature_block)
                over(dve, nf + 1, nb - nf - 1, split_block)
            else:
                over(dve, 1, nb - 1, split_block)

        @block.tensor
        def _(pe):
            pe.wait_ge(rows_in, 16 * len(rows))
            pe.wait_ge(ident_ok, 2)
            pe.transpose(bank[7][:, 0:nrows], row_in[0:nrows, :], ident[0:nrows, 0:nrows]).then_inc(rows_T, 1)

            def transpose_tile(t):
                pe.wait_ge(normed, t + 1)
                if t == 1:
                    pe.wait_ge(cols_ok, 1)
                if t >= 2:
                    pe.wait_ge(hf_ok, (t - 1) * 2)
                for s in (0, 1):
                    for k in range(4):
                        mm = pe.transpose(t_bank[t % 2][s][:, k * P:(k + 1) * P],
                                          x_in[t % XIN][:, (4 * s + k) * P:(4 * s + k + 1) * P], ident[:, :])
                    mm.then_inc(x_T, 1)

            def products(out, pairs):
                for q, (a, c) in enumerate(pairs):
                    mm = pe.matmul(out, a, c, start=(q == 0), stop=(q == len(pairs) - 1))
                return mm

            def feature_output(par, o):
                f, s = o // 2, o % 2
                fs, ts = slice(f * P, (f + 1) * P), slice(s * BLK, (s + 1) * BLK)
                products(bank[o][:, :], [pair for k in range(KT) for pair in (
                    (w_hi[par][:, k, fs], h_hi[:, k, ts]), (w_hi[par][:, k, fs], h_lo[:, k, ts]),
                    (w_lo[par][:, k, fs], h_hi[:, k, ts]))]).then_inc(full, 1)

            def feature_block(n, par, prior):
                pe.wait_ge(split, n + FIRST)
                for o in range(8):
                    pe.wait_ge(conv_in if conv else staged, (n - 1) * 8 + (o + 1))
                    feature_output(par, o)

            def token_block(n, par, prior):
                pe.wait_ge(split, n + FIRST)
                for o in range(8):
                    if not conv:
                        pe.wait_ge(staged, (n - 1) * 8 + (o + 1))
                    elif isinstance(n, int) and n == nf:
                        pe.wait_ge(conv_in, 8 * (nf - 1) + o + 1)
                    else:
                        pe.wait_ge(staged, (n - (nf + 1)) * 8 + (o + 1))
                    ts = slice(o * P, (o + 1) * P)
                    products(bank[o][:, :], [pair for k in range(KT) for pair in (
                        (h_hi[:, k, ts], w_hi[par][:, k, :]), (h_hi[:, k, ts], w_lo[par][:, k, :]),
                        (h_lo[:, k, ts], w_hi[par][:, k, :]))]).then_inc(full, 1)

            for t in range(TILES // 2):
                transpose_tile(t)
            pe.wait_ge(h_ok, TILES)
            for f in range(4):
                pe.wait_ge(split, f + 1)
                feature_output(0, 2 * f)
                transpose_tile(TILES // 2 + f)
            pe.wait_ge(h_ok, 2 * TILES)
            for f in range(4):
                feature_output(0, 2 * f + 1)
            over(pe, 1, nf - 1, feature_block)
            token_block(nf, nf % 2, nf // 2)
            over(pe, nf + 1, nt - 1, token_block)
            if gate_out is not None:
                pe.wait_ge(g_split, 2)
                pe.wait_ge(staged, 8 * (nt - 1) + 2)
                for s in (0, 1):
                    ts = slice(s * BLK, (s + 1) * BLK)
                    mm = products(bank[s][0:GATES, :], [pair for k in range(KT) for pair in (
                        (g_hi[:, k, :], h_hi[:, k, ts]), (g_hi[:, k, :], h_lo[:, k, ts]),
                        (g_lo[:, k, :], h_hi[:, k, ts]))])
                    mm.then_inc(g_full, 1)


T_DT, T_DA, T_EACS, T_NACS, T_U, T_EMT = 0, 16, 32, 48, 64, 68
T_ALL = 72


def scan_gates(nc, keep, gate_rows, dt_bias, a_log, i_bias, f_bias):
    with ExitStack() as ctx:
        ctx.enter_context(nc.cleanup_on_exit())
        m = Part(nc, ctx, "g")
        rows = m.sb("rows", [GATES, SEQ])
        vec = m.sb("vec", [1, GATES + SSD_HEADS])
        ones_row = m.sb("ones_row", [1, P])
        vec_bc = m.sb("vec_bc", [P, GATES + SSD_HEADS])
        a_neg = m.sb("a_neg", [P, SSD_HEADS])
        raw = m.sb("raw", [P, TILES, GATES])
        arg = m.sb("arg", [P, TILES, DECAYS])
        narg = m.sb("narg", [P, TILES, DECAYS])
        e = m.sb("e", [P, TILES, DECAYS])
        s = m.sb("s", [P, TILES, DECAYS])
        s2 = m.sb("s2", [P, TILES, DECAYS])
        q = m.sb("q", [P, TILES, DECAYS])
        sp_ = m.sb("sp", [P, TILES, DECAYS])
        x = m.sb("x", [P, TILES, DECAYS])
        u_row = m.sb("u_row", [ML_HEADS, TILES, P])
        b_row = m.sb("b_row", [ML_HEADS, TILES, P])
        m_row = m.sb("m_row", [ML_HEADS, TILES, P])
        m_prev = m.sb("m_prev", [ML_HEADS, TILES + 1])
        w_log = m.sb("w_log", [ML_HEADS, TILES, P])
        e_row = m.sb("e_row", [ML_HEADS, TILES, P])
        ones = m.sb("ones", [P, P])
        table, maxrows, ident, tri = keep["table"], keep["maxrows"], keep["ident"], keep["tri"]
        p_raw = m.ps("p_raw", [P, 512])
        p_vec = m.ps("p_vec", [P, 512])
        p_cs = m.ps("p_cs", [P, 512])
        p_u = m.ps("p_u", [P, 2, 512])
        p_b = m.ps("p_b", [P, 2, 512])

        landed = m.sem("landed")
        pool_ok = m.sem("pool_ok")
        pe_raw = m.sem("pe_raw")
        pe_vec = m.sem("pe_vec")
        pe_cs = m.sem("pe_cs")
        pe_rows = m.sem("pe_rows")
        pe_emt = m.sem("pe_emt")
        step = m.sem("step")
        a_exp = m.sem("a_exp")
        e_exp = m.sem("e_exp")
        eacs_exp = m.sem("eacs_exp")
        w_exp = m.sem("w_exp")
        emt_exp = m.sem("emt_exp")

        block = ctx.enter_context(nc.Block())

        @block.sync
        def _(sp):
            sp.dma_start(rows[:, :], gate_rows).then_inc(landed, 16)
            at = 0
            for v in (dt_bias, i_bias, f_bias, a_log):
                n = v.shape[1]
                sp.dma_start(vec[:, at:at + n], v).then_inc(landed, 16)
                at += n

        @block.gpsimd
        def _(gp):
            n = 0
            gp.memset(ident[:, :], 0.0).then_inc(pool_ok, 1)
            gp.memset(keep["ident_bf"][:, :], 0.0).then_inc(pool_ok, 1)
            gp.memset(ones[:, :], 1.0).then_inc(pool_ok, 1)
            gp.memset(tri[:, :], 1.0).then_inc(pool_ok, 1)
            gp.memset(keep["later"][:, :], 0.0).then_inc(pool_ok, 1)
            gp.memset(keep["head_row"][:, :, :], 1.0).then_inc(pool_ok, 1)
            gp.memset(ones_row[:, :], 1.0).then_inc(pool_ok, 1)
            gp.memset(m_prev[:, :], 0.0).then_inc(pool_ok, 1)
            gp.memset(keep["half"][:, :], -0.5).then_inc(pool_ok, 1)
            gp.wait_ge(pool_ok, 9)
            for t in (ident, keep["ident_bf"]):
                gp.affine_select(out=t[:, :], in_=t[:, :], compare_op=ALU.not_equal, fill=1.0, base=0,
                                 pattern=[[-1, P]], channel_multiplier=1).then_inc(pool_ok, 1)
            gp.affine_select(out=tri[:, :], in_=tri[:, :], compare_op=ALU.is_ge, fill=0.0, base=0,
                             pattern=[[1, P]], channel_multiplier=-1).then_inc(pool_ok, 1)
            gp.affine_select(out=keep["later"][:, :], in_=keep["later"][:, :], compare_op=ALU.is_ge, fill=MASKED,
                             base=0, pattern=[[1, P]], channel_multiplier=-1).then_inc(pool_ok, 1)
            gp.affine_select(out=keep["head_row"][:, :, :], in_=keep["head_row"][:, :, :], compare_op=ALU.is_equal,
                             fill=0.0, base=0, pattern=[[1, ML_HEADS], [0, P]],
                             channel_multiplier=-1).then_inc(pool_ok, 1)

        @block.tensor
        def _(pe):
            pe.wait_ge(landed, 16 * 5)
            pe.wait_ge(pool_ok, 14)
            pe.matmul(p_vec[:, 0:GATES + SSD_HEADS], ones_row[:, :], vec[:, :], start=True, stop=True).then_inc(pe_vec, 1)
            for c in range(TILES):
                mm = pe.transpose(p_raw[:, c * GATES:(c + 1) * GATES], rows[:, c * P:(c + 1) * P],
                                  ident[0:GATES, 0:GATES])
            mm.then_inc(pe_raw, 1)
            pe.wait_ge(step, 21)
            pe.matmul(p_cs[:, 0:TILES * DECAYS], tri[:, :], x[:, :, :].rearrange("p c h -> p (c h)"),
                      start=True, stop=True).then_inc(pe_cs, 1)
            pe.wait_ge(step, 24)
            for c in range(TILES):
                pe.transpose(p_u[0:ML_HEADS, c // 4, (c % 4) * P:(c % 4 + 1) * P], table[:, c, T_U:T_U + ML_HEADS],
                             ident[:, :])
            for c in range(TILES):
                mm = pe.transpose(p_b[0:ML_HEADS, c // 4, (c % 4) * P:(c % 4 + 1) * P], s[:, c, SSD_HEADS:DECAYS],
                                  ident[:, :])
            mm.then_inc(pe_rows, 1)
            pe.wait_ge(emt_exp, 1)
            for c in range(TILES):
                mm = pe.transpose(p_vec[:, c * ML_HEADS:(c + 1) * ML_HEADS], e_row[:, c, :],
                                  ident[0:ML_HEADS, 0:ML_HEADS])
            mm.then_inc(pe_emt, 1)

        @block.scalar
        def _(act):
            act.wait_ge(step, 1)
            nc.scalar.activation(a_neg[:, :], vec_bc[:, GATES:], ACT.Exp).then_inc(a_exp, 1)
            act.wait_ge(step, 6)
            nc.scalar.activation(e[:, :, :], narg[:, :, :], ACT.Exp).then_inc(e_exp, 1)
            act.wait_ge(step, 22)
            nc.scalar.activation(table[:, :, T_EACS:T_EACS + SSD_HEADS], s[:, :, 0:SSD_HEADS],
                                 ACT.Exp).then_inc(eacs_exp, 1)
            act.wait_ge(step, 24 + 2 + 2 * TILES + 2)
            nc.scalar.activation(maxrows[:, :, 1, :], w_log[:, :, :], ACT.Exp).then_inc(w_exp, 1)
            act.wait_ge(step, 24 + 2 + 2 * TILES + 3)
            nc.scalar.activation(e_row[:, :, :], b_row[:, :, :], ACT.Exp, scale=-1.0).then_inc(emt_exp, 1)

        @block.vector
        def _(dve):
            steps = [0]

            def chain(ins):
                steps[0] += 1
                ins.then_inc(step, 1)
                dve.wait_ge(step, steps[0])

            f = slice(SSD_HEADS, DECAYS)
            dve.wait_ge(pe_vec, 1)
            chain(dve.tensor_copy(vec_bc[:, :], p_vec[:, 0:GATES + SSD_HEADS]))
            dve.wait_ge(pe_raw, 1)
            chain(dve.tensor_tensor(raw[:, :, :], p_raw[:, 0:TILES * GATES].rearrange("p (c g) -> p c g", g=GATES),
                                    mid(vec_bc[:, 0:GATES], TILES), ALU.add))
            chain(dve.tensor_copy(arg[:, :, 0:SSD_HEADS], raw[:, :, 0:SSD_HEADS]))
            chain(dve.tensor_scalar(arg[:, :, f], raw[:, :, SSD_HEADS + ML_HEADS:GATES], -1.0, None, ALU.mult))
            chain(dve.tensor_scalar(q[:, :, :], arg[:, :, :], -1.0, None, ALU.mult))
            chain(dve.tensor_tensor(narg[:, :, :], arg[:, :, :], q[:, :, :], ALU.min))
            dve.wait_ge(e_exp, 1)
            chain(dve.tensor_scalar(q[:, :, :], e[:, :, :], 2.0, None, ALU.add))
            chain(dve.reciprocal(s[:, :, :], q[:, :, :]))
            chain(dve.tensor_tensor(s[:, :, :], s[:, :, :], e[:, :, :], ALU.mult))
            chain(dve.tensor_tensor(s2[:, :, :], s[:, :, :], s[:, :, :], ALU.mult))
            chain(dve.tensor_scalar(q[:, :, :], s2[:, :, :], 1.0 / 15, None, ALU.mult))
            for k in (13, 11, 9, 7, 5, 3):
                chain(dve.scalar_tensor_tensor(out=q[:, :, :], in0=q[:, :, :], scalar=1.0 / k, in1=s2[:, :, :],
                                               op0=ALU.add, op1=ALU.mult))
            chain(dve.scalar_tensor_tensor(out=q[:, :, :], in0=q[:, :, :], scalar=1.0, in1=s[:, :, :],
                                           op0=ALU.add, op1=ALU.mult))
            chain(dve.tensor_scalar(sp_[:, :, :], arg[:, :, :], 0.0, None, ALU.max))
            chain(dve.scalar_tensor_tensor(out=sp_[:, :, :], in0=q[:, :, :], scalar=2.0, in1=sp_[:, :, :],
                                           op0=ALU.mult, op1=ALU.add))
            assert steps[0] == 20, steps
            dve.wait_ge(a_exp, 1)
            dve.tensor_scalar(x[:, :, f], sp_[:, :, f], -1.0, None, ALU.mult)
            dve.scalar_tensor_tensor(out=x[:, :, 0:SSD_HEADS], in0=sp_[:, :, 0:SSD_HEADS], scalar=-1.0,
                                     in1=mid(a_neg[:, :], TILES), op0=ALU.mult, op1=ALU.mult).then_inc(step, 1)
            steps[0] += 1
            dve.wait_ge(pe_cs, 1)
            chain(dve.tensor_copy(s[:, :, :], p_cs[:, 0:TILES * DECAYS].rearrange("p (c h) -> p c h", h=DECAYS)))
            chain(dve.tensor_scalar(table[:, :, T_NACS:T_NACS + SSD_HEADS], s[:, :, 0:SSD_HEADS], -1.0, None, ALU.mult))
            chain(dve.tensor_tensor(table[:, :, T_U:T_U + ML_HEADS], raw[:, :, SSD_HEADS:SSD_HEADS + ML_HEADS],
                                    s[:, :, f], ALU.subtract))
            dve.wait_ge(pe_rows, 1)
            flat = lambda t: t[:, :, :].rearrange("h c t -> h (c t)")
            chain(dve.tensor_copy(flat(u_row), p_u[0:ML_HEADS, :, :].rearrange("h a b -> h (a b)")))
            chain(dve.tensor_copy(flat(b_row), p_b[0:ML_HEADS, :, :].rearrange("h a b -> h (a b)")))
            for c in range(TILES):
                chain(dve.tensor_tensor_scan(m_row[:, c, :], u_row[:, c, :], u_row[:, c, :], m_prev[:, c:c + 1],
                                             ALU.max, ALU.max))
                chain(dve.tensor_tensor(m_prev[:, c + 1:c + 2], m_row[:, c, P - 1:P], b_row[:, c, P - 1:P], ALU.add))
            chain(dve.tensor_scalar(maxrows[:, :, 0, :], m_row[:, :, :], -1.0, None, ALU.mult))
            chain(dve.tensor_tensor(w_log[:, :, :], maxrows[:, :, 0, :], last(m_prev[:, 0:TILES], P), ALU.add))
            chain(dve.tensor_tensor(b_row[:, :, :], b_row[:, :, :], m_row[:, :, :], ALU.add))
            chain(dve.tensor_copy(table[:, :, T_DT:T_DT + SSD_HEADS], sp_[:, :, 0:SSD_HEADS]))
            chain(dve.tensor_copy(table[:, :, T_DA:T_DA + SSD_HEADS], x[:, :, 0:SSD_HEADS]))
            dve.wait_ge(pe_emt, 1)
            chain(dve.tensor_copy(table[:, :, T_EMT:T_EMT + ML_HEADS],
                                  p_vec[:, 0:TILES * ML_HEADS].rearrange("p (c h) -> p c h", h=ML_HEADS)))


def scan_chunks(nc, keep, yT, feat, tok, norm_g, d_skip):
    VW = ML_V + 1
    HG = SSD_HEADS // SSD_GROUPS
    XS, BT, CT, QT, KTL = 0, 8, 10, 12, 16
    with ExitStack() as ctx:
        ctx.enter_context(nc.cleanup_on_exit())
        m = Part(nc, ctx, "s")
        fe = [m.sb(f"fe{i}", [P, FEAT_T, P]) for i in (0, 1)]
        gz = [m.sb(f"gz{i}", [P, 3, D]) for i in (0, 1)]
        va = [m.sb(f"va{i}", [P, ML_HEADS, VW]) for i in (0, 1)]
        g = m.sb("g", [P, T_ALL])
        mr = m.sb("mr", [ML_HEADS, 2, P])
        x_tok = m.sb("x_tok", [P, D])
        xdt = m.sb("xdt", [P, D])
        xe = m.sb("xe", [P, D])
        b_tok = m.sb("b_tok", [P, SSD_GROUPS, SSD_STATE])
        dec = m.sb("dec", [P, SSD_HEADS, P])
        wt = m.sb("wt", [P, SSD_HEADS, P])
        e_end = m.sb("e_end", [P, SSD_HEADS])
        wm = m.sb("wm", [P, ML_HEADS, P])
        st = m.sb("st", [P, ML_HEADS, P])
        qs = m.sb("qs", [P, ML_HEADS, P])
        kg = m.sb("kg", [P, ML_HEADS, P])
        gk = m.sb("gk", [P, ML_HEADS])
        c_dec = m.sb("c_dec", [P, ML_HEADS])
        state = m.sb("state", [P, D])
        cmem = m.sb("cmem", [P, ML_HEADS, VW])
        t1 = m.sb("t1", [P, D])
        y = m.sb("y", [P, 2 * D])
        den = m.sb("den", [P, ML_HEADS])
        den2 = m.sb("den2", [P, ML_HEADS])
        x_sq = m.sb("x_sq", [P, 512])
        ssq = m.sb("ssq", [P, 6])
        rms = m.sb("rms", [P, 6])
        drow = m.sb("drow", [1, SSD_HEADS])
        d_bc = m.sb("d_bc", [P, SSD_HEADS])
        row_in = m.sb("row_in", [AB_OUT_T, P])
        gcols = m.sb("gcols", [P, AB_OUT_T])
        ident, ident_bf, tri, later = keep["ident"], keep["ident_bf"], keep["tri"], keep["later"]
        head_row, half, table, maxrows = keep["head_row"], keep["half"], keep["table"], keep["maxrows"]
        ps = m.ps("ps", [P, 8, 512])

        names = """const_in drow_T cols_T cols_ok drow_ok v_ones zero_ok g_ok mr_ok
                   p_xT p_bc p_kT p_acs p_negm p_wint p_qk p_num p_yoff p_ydiag p_state p_cmem p_yT
                   a_xtok a_btok a_dec a_wm a_sqm a_sqy a_ynorm
                   d_wt d_eend d_st d_qs d_cdec d_gk d_kg d_den d_h d_cmem d_t1 d_y d_state d_yb d_yT
                   d_meanm d_meany
                   l_xdt l_xe l_xd l_yd l_yz l_sdec l_rstdm l_rstdy""".split()
        S = {n: m.sem(n) for n in names}
        in_landed = [m.sem(f"in_landed{i}") for i in (0, 1)]
        hd = lambda ap: ap.rearrange("p (h d) -> p h d", d=SSD_DIM)
        b4 = lambda b: ps[:, b, :].rearrange("p (a t) -> p a t", a=4)

        block = ctx.enter_context(nc.Block())

        @block.sync
        def _(sp):
            def load(n, par):
                t = bass.ds(n * P, P)
                sp.dma_start(fe[par][:, :, :], feat[:, :, t].rearrange("f p t -> p f t")).then_inc(in_landed[par], 16)
                sp.dma_start(gz[par][:, :, :], tok[t, 0:3 * D].rearrange("p (k n) -> p k n", k=3)).then_inc(in_landed[par], 16)
                sp.dma_start(va[par][:, :, 0:ML_V], tok[t, 3 * D:4 * D].rearrange("p (h v) -> p h v", h=ML_HEADS)
                             ).then_inc(in_landed[par], 16)

            load(0, 0)
            sp.dma_start(drow[:, :], d_skip).then_inc(S["const_in"], 16)
            half_rows = AB_OUT_T // 2
            for i, r in enumerate(norm_g):
                sp.dma_start(row_in[i * half_rows:(i + 1) * half_rows, :], r).then_inc(S["const_in"], 16)
            load(1, 1)
            def body(n, par, prior):
                sp.wait_ge(S["p_cmem"], n + 1)
                sp.wait_ge(S["d_yb"], n + 1)
                sp.wait_ge(S["l_yz"], n + 1)
                load(n + 2, par)

            over(sp, 0, TILES - 2, body)

        @block.tensor
        def _(pe):
            pe.wait_ge(S["const_in"], 16 * 3)
            pe.transpose(ps[:, 7, 0:AB_OUT_T], row_in[:, :], ident[0:AB_OUT_T, 0:AB_OUT_T]).then_inc(S["cols_T"], 1)
            pe.matmul(ps[:, 6, 0:SSD_HEADS], tri[0:1, :], drow[:, :], start=True, stop=True).then_inc(S["drow_T"], 1)
            pe.wait_ge(S["cols_ok"], 1)
            pe.wait_ge(S["drow_ok"], 1)
            pe.wait_ge(S["zero_ok"], 4)

            def weights(n, par, prior):
                pe.wait_ge(in_landed[par], prior * 48 + 48)
                f = fe[par]
                pe.wait_ge(S["d_y"], n * 2)
                for k in range(8):
                    mm = pe.transpose(ps[:, k // 4, (k % 4) * P:(k % 4 + 1) * P], f[:, XS + k, :], ident[:, :])
                mm.then_inc(S["p_xT"], 1)
                pe.wait_ge(S["d_state"], n * 2)
                for k in range(2):
                    pe.transpose(ps[:, 3, k * P:(k + 1) * P], f[:, BT + k, :], ident[:, :])
                for k in range(2):
                    mm = pe.matmul(ps[:, 3, (2 + k) * P:(3 + k) * P], f[:, BT + k, :], f[:, CT + k, :], start=True, stop=True)
                mm.then_inc(S["p_bc"], 1)
                for k in range(4):
                    mm = pe.transpose(ps[:, 2, k * P:(k + 1) * P], f[:, KTL + k, :], ident[:, :])
                mm.then_inc(S["p_kT"], 1)
                pe.wait_ge(S["g_ok"], n + 1)
                pe.wait_ge(S["d_cmem"], n * 4)
                for q in range(4):
                    bank = 4 + q % 2
                    if q >= 2:
                        pe.wait_ge(S["a_dec"], n * 4 + (q - 1))
                    for k in range(4):
                        h = T_DA + 4 * q + k
                        pe.matmul(ps[:, bank, k * P:(k + 1) * P], g[:, h:h + 1].broadcast_to([P, P]), tri[:, :],
                                  start=(k == 0), stop=False, skip_group_check=True)
                    pe.matmul(ps[:, bank, :], ident_bf[:, :], mid(later[:, :], 4), start=False, stop=True,
                              skip_group_check=True).then_inc(S["p_acs"], 1)
                pe.wait_ge(S["mr_ok"], n + 1)
                for k in range(4):
                    pe.matmul(ps[:, 6, k * P:(k + 1) * P], head_row[:, k, :], mr[:, 0, :],
                              start=(k == 0), stop=False, skip_group_check=True)
                pe.matmul(ps[:, 6, :], ident_bf[:, :], mid(later[:, :], 4), start=False, stop=True,
                          skip_group_check=True).then_inc(S["p_negm"], 1)
                for k in range(4):
                    mm = pe.matmul(ps[:, 7, k * P:(k + 1) * P], head_row[:, k, :], mr[:, 1, :], start=True, stop=True)
                mm.then_inc(S["p_wint"], 1)
                pe.wait_ge(S["a_dec"], n * 4 + 3)
                for k in range(4):
                    mm = pe.matmul(ps[:, 4, k * P:(k + 1) * P], f[:, KTL + k, :], f[:, QT + k, :], start=True, stop=True)
                mm.then_inc(S["p_qk"], 1)

            def outputs(n, par, prior):
                f = fe[par]
                pe.wait_ge(S["d_st"], n + 1)
                pe.wait_ge(S["d_qs"], n + 1)
                pe.wait_ge(S["d_cdec"], n + 1)
                pe.wait_ge(S["a_wm"], n + 1)
                pe.wait_ge(S["d_cmem"], n * 4)
                pe.wait_ge(S["a_dec"], n * 4 + 4)
                for h in range(ML_HEADS):
                    pe.matmul(ps[:, 4 + h, 0:VW], st[:, h, :], va[par][:, h, :], start=True, stop=False)
                    mm = pe.matmul(ps[:, 4 + h, 0:VW], qs[:, h, :], cmem[:, h, :], start=False, stop=True)
                    mm.then_inc(S["p_num"], 1)
                pe.wait_ge(S["d_kg"], n + 1)
                pe.wait_ge(S["a_btok"], n + 1)
                pe.wait_ge(S["d_wt"], n * 2 + 2)
                pe.wait_ge(S["d_state"], n * 2)
                pe.wait_ge(S["d_yT"], n * 4)
                for k in range(2):
                    mm = pe.matmul(ps[:, 2 + k, :], f[:, CT + k, :], state[:, k * 512:(k + 1) * 512], start=True, stop=True)
                    mm.then_inc(S["p_yoff"], 1)
                pe.wait_ge(S["l_xdt"], n + 1)
                pe.wait_ge(S["a_xtok"], n * 2 + 2)
                for h in range(SSD_HEADS):
                    mm = pe.matmul(ps[:, h // HG, (h % HG) * SSD_DIM:(h % HG + 1) * SSD_DIM], wt[:, h, :],
                                   xdt[:, h * SSD_DIM:(h + 1) * SSD_DIM], start=True, stop=True)
                    if h % HG == HG - 1:
                        mm.then_inc(S["p_ydiag"], 1)
                for h in range(ML_HEADS):
                    pe.wait_ge(S["d_h"], n * 4 + (h + 1))
                    mm = pe.matmul(ps[:, 4 + h, 0:VW], kg[:, h, :], va[par][:, h, :], start=True, stop=True)
                mm.then_inc(S["p_cmem"], 1)
                pe.wait_ge(S["l_xe"], n + 1)
                pe.wait_ge(S["d_t1"], n * 2 + 2)
                for k in range(2):
                    mm = pe.matmul(ps[:, 2 + k, :], b_tok[:, k, :], xe[:, k * 512:(k + 1) * 512], start=True, stop=True)
                mm.then_inc(S["p_state"], 1)

            def turn(n):
                pe.wait_ge(S["a_ynorm"], n * 2 + 2)
                pe.wait_ge(S["d_yb"], n + 1)
                for b in range(4):
                    for k in range(4):
                        c = (4 * b + k) * P
                        mm = pe.transpose(ps[:, b, k * P:(k + 1) * P], y[:, c:c + P], ident[:, :])
                    mm.then_inc(S["p_yT"], 1)

            def ahead_of_turn(n):
                pe.wait_ge(S["a_xtok"], n * 2 + 4)
                pe.wait_ge(S["d_kg"], n + 2)
                pe.wait_ge(S["a_btok"], n + 2)
                pe.wait_ge(S["d_wt"], n * 2 + 4)

            weights(0, 0, 0)

            def body(n, par, prior):
                outputs(n, par, prior)
                weights(n + 1, 1 - par, prior + par)
                ahead_of_turn(n)
                turn(n)

            over(pe, 0, TILES - 1, body)
            outputs(TILES - 1, 1, (TILES - 1) // 2)
            pe.wait_ge(S["d_y"], 2 * TILES)
            pe.wait_ge(S["d_state"], 2 * TILES)
            turn(TILES - 1)

        @block.scalar
        def _(act):
            def weights(n, par, prior):
                act.wait_ge(S["p_xT"], n + 1)
                act.wait_ge(S["l_yd"], n + 0)
                act.wait_ge(S["l_xdt"], n + 0)
                for k in (0, 1):
                    nc.scalar.copy(x_tok[:, k * 512:(k + 1) * 512], ps[:, k, :]).then_inc(S["a_xtok"], 1)
                act.wait_ge(S["p_bc"], n + 1)
                nc.scalar.copy(b_tok[:, :, :], ps[:, 3, 0:2 * P].rearrange("p (a t) -> p a t", a=2)).then_inc(S["a_btok"], 1)
                act.wait_ge(S["g_ok"], n + 1)
                act.wait_ge(S["d_wt"], n * 2)
                act.wait_ge(S["d_eend"], n + 0)
                act.wait_ge(S["l_xe"], n + 0)
                for q in range(4):
                    act.wait_ge(S["p_acs"], n * 4 + (q + 1))
                    for k in range(4):
                        h = 4 * q + k
                        a = nc.scalar.activation(dec[:, h, :], ps[:, 4 + q % 2, k * P:(k + 1) * P], ACT.Exp,
                                                 bias=g[:, T_NACS + h:T_NACS + h + 1])
                    a.then_inc(S["a_dec"], 1)
                act.wait_ge(S["p_negm"], n + 1)
                act.wait_ge(S["d_st"], n + 0)
                act.wait_ge(S["d_gk"], n + 0)
                for k in range(ML_HEADS):
                    a = nc.scalar.activation(wm[:, k, :], ps[:, 6, k * P:(k + 1) * P], ACT.Exp,
                                             bias=g[:, T_U + k:T_U + k + 1])
                a.then_inc(S["a_wm"], 1)

            def outputs(n, par, prior):
                act.wait_ge(S["d_h"], n * 4 + 4)
                act.wait_ge(S["d_meanm"], n + 0)
                act.wait_ge(S["a_sqy"], n * 2)
                for h in range(ML_HEADS):
                    act.wait_ge(S["a_sqm"], n * 4 + h)
                    nc.scalar.activation(x_sq[:, 0:ML_V], y[:, D + h * ML_V:D + (h + 1) * ML_V], ACT.Square,
                                         accum_out=ssq[:, 2 + h:3 + h]).then_inc(S["a_sqm"], 1)
                act.wait_ge(S["l_yz"], n + 1)
                act.wait_ge(S["a_sqm"], n * 4 + 4)
                act.wait_ge(S["d_meany"], n + 0)
                for k in (0, 1):
                    act.wait_ge(S["a_sqy"], n * 2 + k)
                    nc.scalar.activation(x_sq[:, :], y[:, k * 512:(k + 1) * 512], ACT.Square,
                                         accum_out=ssq[:, k:k + 1]).then_inc(S["a_sqy"], 1)
                act.wait_ge(S["l_rstdy"], n + 1)
                for k in (0, 1):
                    nc.scalar.activation(y[:, k * 512:(k + 1) * 512], y[:, k * 512:(k + 1) * 512], ACT.Copy,
                                         scale=rms[:, k:k + 1]).then_inc(S["a_ynorm"], 1)

            weights(0, 0, 0)

            def body(n, par, prior):
                outputs(n, par, prior)
                weights(n + 1, 1 - par, prior + par)

            over(act, 0, TILES - 1, body)
            outputs(TILES - 1, 1, (TILES - 1) // 2)

        @block.gpsimd
        def _(gp):
            for v in va:
                gp.memset(v[:, :, ML_V:VW], 1.0).then_inc(S["v_ones"], 1)
            gp.memset(state[:, :], 0.0).then_inc(S["zero_ok"], 1)
            gp.memset(cmem[:, :, :], 0.0).then_inc(S["zero_ok"], 1)
            gp.wait_ge(S["v_ones"], 2)
            gp.memset(xdt[:, :], 0.0).then_inc(S["zero_ok"], 1)
            gp.memset(xe[:, :], 0.0).then_inc(S["zero_ok"], 1)
            gp.wait_ge(S["zero_ok"], 4)
            gp.wait_ge(S["drow_ok"], 1)

            def body(n, par, prior):
                gp.wait_ge(S["a_xtok"], n * 2 + 2)
                gp.wait_ge(S["g_ok"], n + 1)
                gp.tensor_tensor(hd(xdt[:, :]), hd(x_tok[:, :]), last(g[:, T_DT:T_DT + SSD_HEADS], SSD_DIM),
                                 ALU.mult).then_inc(S["l_xdt"], 1)
                gp.wait_ge(S["l_xdt"], n + 1)
                gp.tensor_tensor(hd(x_tok[:, :]), hd(x_tok[:, :]), last(d_bc[:, :], SSD_DIM), ALU.mult).then_inc(S["l_xd"], 1)
                gp.wait_ge(S["a_dec"], n * 4 + 4)
                gp.tensor_tensor(hd(xe[:, :]), hd(xdt[:, :]),
                                 dec[:, :, P - 1:P].broadcast_to([P, SSD_HEADS, SSD_DIM]), ALU.mult).then_inc(S["l_xe"], 1)
                gp.wait_ge(S["p_yoff"], n * 2 + 2)
                gp.wait_ge(S["d_eend"], n + 1)
                gp.wait_ge(S["d_state"], n * 2)
                gp.tensor_tensor(hd(state[:, :]), hd(state[:, :]), last(e_end[:, :], SSD_DIM), ALU.mult).then_inc(S["l_sdec"], 1)
                gp.wait_ge(S["d_meanm"], n + 1)
                gp.tensor_tensor(rms[:, 2:6], rms[:, 2:6], half[:, 0:4], ALU.pow).then_inc(S["l_rstdm"], 1)
                gp.wait_ge(S["d_y"], n * 2 + 2)
                gp.wait_ge(S["l_xd"], n + 1)
                gp.tensor_tensor(y[:, 0:D], y[:, 0:D], x_tok[:, :], ALU.add).then_inc(S["l_yd"], 1)
                gp.wait_ge(S["l_yd"], n + 1)
                gp.wait_ge(in_landed[par], prior * 48 + 48)
                gp.tensor_tensor(y[:, 0:D], y[:, 0:D], gz[par][:, 0, :], ALU.mult).then_inc(S["l_yz"], 1)
                gp.wait_ge(S["d_meany"], n + 1)
                gp.tensor_tensor(rms[:, 0:2], rms[:, 0:2], half[:, 0:2], ALU.pow).then_inc(S["l_rstdy"], 1)

            over(gp, 0, TILES, body)

        @block.vector
        def _(dve):
            dve.wait_ge(S["cols_T"], 1)
            dve.tensor_copy(gcols[:, :], ps[:, 7, 0:AB_OUT_T]).then_inc(S["cols_ok"], 1)
            dve.wait_ge(S["drow_T"], 1)
            dve.tensor_copy(d_bc[:, :], ps[:, 6, 0:SSD_HEADS]).then_inc(S["drow_ok"], 1)

            def tables(n):
                dve.wait_ge(S["a_dec"], n * 4)
                dve.wait_ge(S["a_wm"], n + 0)
                dve.wait_ge(S["p_wint"], n + 0)
                dve.wait_ge(S["l_xdt"], n + 0)
                dve.tensor_scalar(g[:, :], table[:, bass.ds(n, 1), :].rearrange("p a k -> p (a k)"), 1.0, None,
                                  ALU.mult).then_inc(S["g_ok"], 1)
                dve.tensor_scalar(mr[:, :, :], maxrows[:, bass.ds(n, 1), :, :].rearrange("h a k t -> h (a k) t"),
                                  1.0, None, ALU.mult).then_inc(S["mr_ok"], 1)
                dve.wait_ge(S["g_ok"], n + 1)

            def weights(n, par, prior):
                dve.wait_ge(S["p_bc"], n + 1)
                for k in (0, 1):
                    dve.wait_ge(S["a_dec"], n * 4 + 2 * (k + 1))
                    dve.tensor_tensor(wt[:, HG * k:HG * (k + 1), :], dec[:, HG * k:HG * (k + 1), :],
                                      mid(ps[:, 3, (2 + k) * P:(3 + k) * P], HG), ALU.mult).then_inc(S["d_wt"], 1)
                dve.wait_ge(S["l_sdec"], n + 0)
                dve.tensor_tensor(e_end[:, :], dec[:, :, P - 1:P].rearrange("p h a -> p (h a)"),
                                  g[:, T_EACS:T_EACS + SSD_HEADS], ALU.mult).then_inc(S["d_eend"], 1)
                dve.wait_ge(S["p_wint"], n + 1)
                dve.wait_ge(in_landed[par], prior * 48 + 48)
                dve.tensor_tensor(qs[:, :, :], fe[par][:, QT:QT + 4, :], b4(7), ALU.mult).then_inc(S["d_qs"], 1)
                dve.wait_ge(S["d_cmem"], n * 4)
                dve.tensor_copy(c_dec[:, :], b4(7)[:, :, P - 1:P].rearrange("p h a -> p (h a)")).then_inc(S["d_cdec"], 1)
                dve.wait_ge(S["a_wm"], n + 1)
                dve.wait_ge(S["p_qk"], n + 1)
                dve.scalar_tensor_tensor(out=st[:, :, :], in0=b4(4), scalar=ML_QK ** -0.5, in1=wm[:, :, :],
                                         op0=ALU.mult, op1=ALU.mult).then_inc(S["d_st"], 1)
                dve.tensor_scalar(gk[:, :], wm[:, :, P - 1:P].rearrange("p h a -> p (h a)"), ML_QK ** -0.5, None,
                                  ALU.mult).then_inc(S["d_gk"], 1)
                dve.wait_ge(S["d_gk"], n + 1)
                dve.wait_ge(S["p_kT"], n + 1)
                dve.tensor_tensor(kg[:, :, :], b4(2), last(gk[:, :], P), ALU.mult).then_inc(S["d_kg"], 1)

            def outputs(n, par, prior):
                dve.wait_ge(S["p_num"], n * 4 + 4)
                dve.tensor_copy(den[:, :], ps[:, 4:8, ML_V:VW].rearrange("p h a -> p (h a)")).then_inc(S["d_den"], 1)
                dve.wait_ge(S["d_den"], n * 4 + 1)
                dve.scalar_tensor_tensor(out=den2[:, :], in0=den[:, :], scalar=-1.0, in1=den[:, :],
                                         op0=ALU.mult, op1=ALU.max).then_inc(S["d_den"], 1)
                dve.wait_ge(S["d_den"], n * 4 + 2)
                dve.tensor_tensor(den2[:, :], den2[:, :], g[:, T_EMT:T_EMT + ML_HEADS], ALU.max).then_inc(S["d_den"], 1)
                dve.wait_ge(S["d_den"], n * 4 + 3)
                dve.reciprocal(den[:, :], den2[:, :]).then_inc(S["d_den"], 1)
                dve.wait_ge(S["d_den"], n * 4 + 4)
                dve.wait_ge(S["p_yT"], n * 4)
                for h in range(ML_HEADS):
                    v = slice(h * ML_V, (h + 1) * ML_V)
                    dve.scalar_tensor_tensor(out=y[:, D + h * ML_V:D + (h + 1) * ML_V], in0=ps[:, 4 + h, 0:ML_V],
                                             scalar=den[:, h:h + 1], in1=gz[par][:, 2, v], op0=ALU.mult,
                                             op1=ALU.mult).then_inc(S["d_h"], 1)
                for k in (0, 1):
                    c = slice(k * 512, (k + 1) * 512)
                    dve.wait_ge(S["p_yoff"], n * 2 + (k + 1))
                    dve.tensor_tensor(hd(t1[:, c]), hd(ps[:, 2 + k, :]),
                                      last(g[:, T_EACS + HG * k:T_EACS + HG * (k + 1)], SSD_DIM), ALU.mult).then_inc(S["d_t1"], 1)
                for k in (0, 1):
                    c = slice(k * 512, (k + 1) * 512)
                    dve.wait_ge(S["p_ydiag"], n * 2 + (k + 1))
                    dve.wait_ge(S["d_t1"], n * 2 + (k + 1))
                    dve.tensor_tensor(y[:, c], ps[:, k, :], t1[:, c], ALU.add).then_inc(S["d_y"], 1)
                dve.wait_ge(S["a_sqm"], n * 4 + 4)
                dve.tensor_scalar(rms[:, 2:6], ssq[:, 2:6], 1.0 / ML_V, EPS, ALU.mult, ALU.add).then_inc(S["d_meanm"], 1)
                dve.wait_ge(S["p_cmem"], n + 1)
                for h in range(ML_HEADS):
                    dve.scalar_tensor_tensor(out=cmem[:, h, :], in0=cmem[:, h, :], scalar=c_dec[:, h:h + 1],
                                             in1=ps[:, 4 + h, 0:VW], op0=ALU.mult, op1=ALU.add).then_inc(S["d_cmem"], 1)
                dve.wait_ge(S["p_state"], n + 1)
                dve.wait_ge(S["l_sdec"], n + 1)
                for k in (0, 1):
                    c = slice(k * 512, (k + 1) * 512)
                    dve.tensor_tensor(state[:, c], state[:, c], ps[:, 2 + k, :], ALU.add).then_inc(S["d_state"], 1)
                dve.wait_ge(S["l_rstdm"], n + 1)
                for h in range(ML_HEADS):
                    v = slice(h * ML_V, (h + 1) * ML_V)
                    yb = y[:, D + h * ML_V:D + (h + 1) * ML_V]
                    a = dve.scalar_tensor_tensor(out=yb, in0=yb, scalar=rms[:, 2 + h:3 + h], in1=gz[par][:, 1, v],
                                                 op0=ALU.mult, op1=ALU.mult)
                a.then_inc(S["d_yb"], 1)
                dve.wait_ge(S["a_sqy"], n * 2 + 2)
                dve.tensor_scalar(rms[:, 0:2], ssq[:, 0:2], 1.0 / 512, EPS, ALU.mult, ALU.add).then_inc(S["d_meany"], 1)

            def turn(n):
                for b in range(4):
                    dve.wait_ge(S["p_yT"], n * 4 + (b + 1))
                    dve.tensor_tensor(yT[:, bass.ds(n, 1), 4 * b:4 * b + 4, :].rearrange("p a k t -> p (a k) t"), b4(b),
                                      last(gcols[:, 4 * b:4 * b + 4], P), ALU.mult).then_inc(S["d_yT"], 1)

            dve.wait_ge(S["zero_ok"], 4)
            tables(0)
            weights(0, 0, 0)

            def body(n, par, prior):
                outputs(n, par, prior)
                tables(n + 1)
                weights(n + 1, 1 - par, prior + par)
                turn(n)

            over(dve, 0, TILES - 1, body)
            outputs(TILES - 1, 1, (TILES - 1) // 2)
            turn(TILES - 1)


def out_projection(nc, tag, yT, x, w_out, x1):
    HALF = D // 2
    QT, Q = 4, AB_OUT_T // 4
    PIECES = 2 * Q
    with ExitStack() as ctx:
        ctx.enter_context(nc.cleanup_on_exit())
        m = Part(nc, ctx, tag)
        y_hi = [m.sb(f"y_hi{i}", [P, TILES, QT, P], F32R) for i in (0, 1)]
        y_lo = [m.sb(f"y_lo{i}", [P, TILES, QT, P], F32R) for i in (0, 1)]
        w_raw = [m.sb(f"w_raw{i}", [P, QT, HALF]) for i in (0, 1)]
        w_hi = [m.sb(f"w_hi{i}", [P, QT, HALF], F32R) for i in (0, 1)]
        w_lo = [m.sb(f"w_lo{i}", [P, QT, HALF], F32R) for i in (0, 1)]
        xr = m.sb("xr", [P, TILES, HALF])
        ps = m.ps("ps", [P, 8, 512])
        S = {n: m.sem(n) for n in "a_yhi a_whi d_ylo d_wlo p_part d_x1 x_landed x1_stored".split()}
        w_landed = [m.sem(f"w_landed{i}") for i in (0, 1)]

        block = ctx.enter_context(nc.Block())

        @block.sync
        def _(sp):
            def load_w(i):
                j, q = divmod(i, Q)
                if i >= 2:
                    sp.wait_ge(S["d_wlo"], i - 1)
                sp.dma_start(w_raw[i % 2][:, :, :], w_out[q * QT * P:(q + 1) * QT * P, j * HALF:(j + 1) * HALF]
                             .rearrange("(k p) n -> p k n", p=P)).then_inc(w_landed[i % 2], 16)

            def load_x(j):
                sp.dma_start(xr[:, :, :], x[:, j * HALF:(j + 1) * HALF].rearrange("(t p) n -> p t n", p=P)
                             ).then_inc(S["x_landed"], 16)

            def store(j):
                for t in range(TILES):
                    sp.wait_ge(S["d_x1"], TILES * j + t + 1)
                    sp.dma_start(x1[t * P:(t + 1) * P, j * HALF:(j + 1) * HALF], xr[:, t, :]).then_inc(S["x1_stored"], 16)

            load_w(0)
            load_w(1)
            load_x(0)
            for i in range(2, Q + 2):
                load_w(i)
            store(0)
            for i in range(Q + 2, PIECES):
                load_w(i)
            sp.wait_ge(S["x1_stored"], 16 * TILES)
            load_x(1)
            store(1)
            sp.wait_ge(S["x1_stored"], 16 * 2 * TILES)

        half = lambda t, c: t[:, 4 * (c % 2):4 * (c % 2) + 4, :, :]
        whole = lambda c: yT[:, 4 * (c % 2):4 * (c % 2) + 4, QT * (c // 2 % Q):QT * (c // 2 % Q) + QT, :]

        @block.scalar
        def _(act):
            for i in range(PIECES):
                if i >= 2:
                    act.wait_ge(S["p_part"], TILES * (i - 1))
                for c in (2 * i, 2 * i + 1):
                    nc.scalar.copy(half(y_hi[i % 2], c), whole(c)).then_inc(S["a_yhi"], 1)
                    if c % 2 == 0:
                        act.wait_ge(w_landed[i % 2], 16 * (i // 2 + 1))
                        nc.scalar.copy(w_hi[i % 2][:, :, :], w_raw[i % 2][:, :, :]).then_inc(S["a_whi"], 1)

        @block.vector
        def _(dve):
            def residual(j):
                dve.wait_ge(S["x_landed"], 16 * (j + 1))
                for t in range(TILES):
                    dve.wait_ge(S["p_part"], TILES * (Q * (j + 1) - 1) + t + 1)
                    dve.tensor_tensor(xr[:, t, :], ps[:, t, :], xr[:, t, :], ALU.add).then_inc(S["d_x1"], 1)

            for i in range(PIECES):
                if i == Q + 1:
                    residual(0)
                for c in (2 * i, 2 * i + 1):
                    dve.wait_ge(S["a_yhi"], c + 1)
                    dve.tensor_tensor(half(y_lo[i % 2], c), whole(c), half(y_hi[i % 2], c).bitcast(F32),
                                      ALU.subtract).then_inc(S["d_ylo"], 1)
                    if c % 2 == 0:
                        dve.wait_ge(S["a_whi"], i + 1)
                        dve.tensor_tensor(w_lo[i % 2][:, :, :], w_raw[i % 2][:, :, :], w_hi[i % 2][:, :, :].bitcast(F32),
                                          ALU.subtract).then_inc(S["d_wlo"], 1)
            residual(1)

        @block.tensor
        def _(pe):
            for i in range(PIECES):
                j, q = divmod(i, Q)
                pe.wait_ge(S["d_wlo"], i + 1)
                wl, wh = w_lo[i % 2], w_hi[i % 2]
                for t in range(TILES):
                    if t % 4 == 0:
                        pe.wait_ge(S["d_ylo"], 2 * i + t // 4 + 1)
                    if j and q == 0:
                        pe.wait_ge(S["d_x1"], t + 1)
                    for k in range(QT):
                        h, l = y_hi[i % 2][:, t, k, :], y_lo[i % 2][:, t, k, :]
                        pe.matmul(ps[:, t, :], h, wh[:, k, :], start=(q == 0 and k == 0), stop=False)
                        pe.matmul(ps[:, t, :], h, wl[:, k, :], start=False, stop=False)
                        mm = pe.matmul(ps[:, t, :], l, wh[:, k, :], start=False, stop=(q == Q - 1 and k == QT - 1))
                    mm.then_inc(S["p_part"], 1)


NORMALISE, PROJECT = 3, 5
at_before = [sum(n // DA_HEADS // 4 + 1 for n in range(m)) for m in range(TILES * DA_HEADS + 1)]


def attention(nc, feat, tok, x1, lams, subln_g, w_out, final_g, out):
    LAMBDA_INIT = 0.8 - 0.6 * float(np.exp(-0.3))
    SCALE = DA_QK ** -0.5
    SLOPES = [2.0 ** (-8.0 * (h + 1) / DA_HEADS) for h in range(DA_HEADS)]
    H = DA_HEADS
    N = TILES * H
    with ExitStack() as ctx:
        ctx.enter_context(nc.cleanup_on_exit())
        m = Part(nc, ctx, "a")
        k_hl = m.sb("k_hl", [P, 2 * H, SEQ], F32R)
        v = m.sb("v", [P, TILES, D])
        wout = m.sb("wout", [P, KT, D])
        k_raw = m.sb("k_raw", [P, H, P])
        q_raw = m.sb("q_raw", [P, 2 * H, P])
        q_hi = [m.sb(f"q_hi{i}", [P, 2, P], F32R) for i in (0, 1)]
        q_lo = [m.sb(f"q_lo{i}", [P, 2, P], F32R) for i in (0, 1)]
        neg_dist = m.sb("neg_dist", [P, SEQ])
        z = m.sb("z", [P, D])
        xr = m.sb("xr", [P, D])
        s0 = [m.sb(f"s0{i}", [P, SEQ]) for i in (0, 1, 2)]
        s1 = [m.sb(f"s1{i}", [P, SEQ]) for i in (0, 1)]
        aT = [m.sb(f"aT{i}", [P, TILES, P]) for i in (0, 1)]
        y = [m.sb(f"y{i}", [P, D]) for i in (0, 1)]
        yT = m.sb("yT", [P, KT, P])
        res = m.sb("res", [P, D])
        final_bc = m.sb("final_bc", [P, D])
        ident = m.sb("ident", [P, P])
        lam_in = res[0:1, 0:4 * DA_QK].rearrange("p (a d) -> p a d", d=DA_QK)
        lam_w = res[0:1, 4 * DA_QK:6 * DA_QK].rearrange("p (a d) -> p a d", d=DA_QK)
        ones_row = res[0:1, 512:512 + P]
        g_row = res[0:1, 512 + P:512 + 2 * P]
        squares = [m.sb(f"squares{i}", [P, DA_V], BF16) for i in (0, 1)]
        lam2 = m.sb("lam2", [1, 4])
        neg_lam = m.sb("neg_lam", [P, 1])
        g_col = m.sb("g_col", [P, 1])
        half = m.sb("half", [P, H])
        mx = [m.sb(f"mx{i}", [P, 2]) for i in (0, 1)]
        nm = [m.sb(f"nm{i}", [P, 2]) for i in (0, 1)]
        sm = [m.sb(f"sm{i}", [P, 2]) for i in (0, 1)]
        rc = [m.sb(f"rc{i}", [P, 2]) for i in (0, 1)]
        coef = [m.sb(f"coef{i}", [P, 1]) for i in (0, 1)]
        r0 = [m.sb(f"r0{i}", [P, H]) for i in (0, 1)]
        rs = [m.sb(f"rs{i}", [P, H]) for i in (0, 1)]
        fs = m.sb("fs", [P, 1])
        fss = m.sb("fss", [P, 1])
        ps = m.ps("ps", [P, 8, 512])

        names = """const_in wout_in pool_ok iota_ok dist_ok lam_mul lam_sum lam_exp lam_ok
                   p_const c_ok p_s0 p_s1 p_at p_o p_yT p_out
                   d_t d_nm d_rc d_coef d_r0 d_a d_o d_mean d_yT d_x2 d_fmean d_res d_qlo
                   a_khi a_qhi a_p a_at a_ss a_fss l_klo l_rstd l_yn l_yz l_frstd
                   k_landed v_landed q0_landed q1_landed z_landed x_landed""".split()
        S = {n: m.sem(n) for n in names}
        out_stored = m.sem("out_stored")
        score = [ps[:, 2 * j:2 * j + 2, :].rearrange("p b n -> p (b n)") for j in (0, 1)]
        b4 = lambda b: ps[:, b, :].rearrange("p (a t) -> p a t", a=4)
        hv = lambda ap: ap.rearrange("p (h v) -> p h v", v=DA_V)
        F = DA_QK

        block = ctx.enter_context(nc.Block())


        PIECES = 6

        def piece_of(n):
            t, k = divmod(n - PROJECT - H, H)
            return (t, k) if 0 <= t < TILES - 1 and k < PIECES else (None, None)

        @block.sync
        def _(sp):
            def half_keys(c):
                t, u = c // 2, c % 2
                if c:
                    sp.wait_ge(S["l_klo"], c)
                src = feat[2 * H + H * u:2 * H + H * (u + 1), :, t * P:(t + 1) * P].rearrange("f d t -> d f t")
                for r in (slice(0, F), slice(F, P)):
                    sp.dma_start(k_raw[r, :, :], src).then_inc(S["k_landed"], 16)

            def queries(t, u):
                if t:
                    sp.wait_ge(S["d_qlo"], H * (t - 1) + 4 * u + 4)
                src = feat[H * u:H * (u + 1), :, t * P:(t + 1) * P].rearrange("f d t -> d f t")
                for r in (slice(0, F), slice(F, P)):
                    sp.dma_start(q_raw[r, H * u:H * (u + 1), :], src).then_inc(S[f"q{u}_landed"], 16)

            def values_in(t):
                if t:
                    sp.wait_ge(S["v_landed"], 16 * t)
                sp.dma_start(v[:, t, :], tok[t * P:(t + 1) * P, 0:D]).then_inc(S["v_landed"], 16)

            def gate(t):
                if t:
                    sp.wait_ge(S["l_yz"], t)
                sp.dma_start(z[:, :], tok[t * P:(t + 1) * P, D:2 * D]).then_inc(S["z_landed"], 16)

            def residual_in(t):
                if t:
                    sp.wait_ge(S["d_res"], t)
                sp.dma_start(xr[:, :], x1[t * P:(t + 1) * P, :]).then_inc(S["x_landed"], 16)

            queries(0, 0)
            half_keys(0)
            for i, r in enumerate(lams):
                sp.dma_start(lam_in[:, i, :], r).then_inc(S["const_in"], 16)
            sp.dma_start(g_row, subln_g).then_inc(S["const_in"], 16)
            sp.dma_start(final_bc[0:1, :], final_g).then_inc(S["const_in"], 16)
            values_in(0)
            half_keys(1)
            queries(0, 1)
            gate(0)
            residual_in(0)
            sp.dma_start(wout[:, :, :], w_out.rearrange("(k p) n -> p k n", p=P)).then_inc(S["wout_in"], 16)
            for t in range(TILES):
                if t + 1 < TILES:
                    half_keys(2 * t + 2)
                    values_in(t + 1)
                    queries(t + 1, 0)
                    half_keys(2 * t + 3)
                if t:
                    gate(t)
                if t >= 2:
                    residual_in(t - 1)
                    sp.dma_start(out[(t - 2) * P:(t - 1) * P, :], res[:, :]).then_inc(out_stored, 16)
                if t + 1 < TILES:
                    queries(t + 1, 1)
            residual_in(TILES - 1)
            sp.dma_start(out[SEQ - 2 * P:SEQ - P, :], res[:, :]).then_inc(out_stored, 16)
            sp.wait_ge(S["d_res"], TILES)
            sp.dma_start(out[SEQ - P:SEQ, :], res[:, :]).then_inc(out_stored, 16)
            sp.wait_ge(out_stored, 16 * TILES)

        @block.gpsimd
        def _(gp):
            gp.memset(ident[:, :], 0.0).then_inc(S["pool_ok"], 1)
            gp.memset(ones_row, 1.0).then_inc(S["pool_ok"], 1)
            gp.memset(half[:, :], -0.5).then_inc(S["pool_ok"], 1)
            gp.wait_ge(S["pool_ok"], 3)
            gp.affine_select(out=ident[:, :], in_=ident[:, :], compare_op=ALU.not_equal, fill=1.0, base=0,
                             pattern=[[-1, P]], channel_multiplier=1).then_inc(S["pool_ok"], 1)
            gp.iota(neg_dist[:, :], pattern=[[-1, SEQ]], base=SEQ - P, channel_multiplier=1,
                    allow_small_or_imprecise_dtypes=True).then_inc(S["iota_ok"], 1)
            gp.wait_ge(S["dist_ok"], 1)
            gp.affine_select(out=neg_dist[:, SEQ - 64:SEQ], in_=neg_dist[:, SEQ - 64:SEQ], compare_op=ALU.is_ge,
                             fill=MASKED, base=-64, pattern=[[0, 64]], channel_multiplier=1).then_inc(S["iota_ok"], 1)
            gp.wait_ge(S["iota_ok"], 2)

            def low_keys(c):
                t, u = c // 2, c % 2
                part = k_hl[F:P, H * u:H * (u + 1), t * P:(t + 1) * P]
                gp.wait_ge(S["a_khi"], c + 1)
                gp.tensor_tensor(part, k_raw[F:P, :, :], part.bitcast(F32), ALU.subtract).then_inc(S["l_klo"], 1)
                gp.wait_ge(S["l_klo"], c + 1)

            low_keys(0)
            low_keys(1)
            for n in range(N + H):
                t, h = n // H, n % H
                if t + 1 < TILES and h in (3, 4):
                    if h == 3 and t >= 3:
                        gp.wait_ge(S["l_frstd"], t - 2)
                    if h == 4 and t:
                        gp.wait_ge(S["l_yz"], t)
                    low_keys(2 * (t + 1) + h - 3)
                if t and h == NORMALISE:
                    b = (t - 1) % 2
                    gp.wait_ge(S["d_mean"], t)
                    gp.tensor_tensor(rs[b][:, :], rs[b][:, :], half[:, :], ALU.pow).then_inc(S["l_rstd"], 1)
                    gp.wait_ge(S["l_rstd"], t)
                    gp.tensor_tensor(hv(y[b][:, :]), hv(y[b][:, :]), last(rs[b][:, :], DA_V), ALU.mult).then_inc(S["l_yn"], 1)
                    gp.wait_ge(S["l_yn"], t)
                    gp.wait_ge(S["z_landed"], 16 * t)
                    gp.tensor_tensor(y[b][:, :], y[b][:, :], z[:, :], ALU.mult).then_inc(S["l_yz"], 1)
                if t >= 2 and h == (PROJECT + PIECES + 2) % H:
                    gp.wait_ge(S["d_fmean"], t - 1)
                    gp.tensor_tensor(fs[:, :], fs[:, :], half[:, 0:1], ALU.pow).then_inc(S["l_frstd"], 1)
            gp.wait_ge(S["d_fmean"], TILES)
            gp.tensor_tensor(fs[:, :], fs[:, :], half[:, 0:1], ALU.pow).then_inc(S["l_frstd"], 1)

        @block.tensor
        def _(pe):
            pe.wait_ge(S["lam_ok"], 1)
            pe.wait_ge(S["const_in"], 16 * 6)
            pe.wait_ge(S["pool_ok"], 4)
            pe.matmul(ps[:, 7, 0:1], ones_row, lam2[:, 2:3], start=True, stop=True)
            pe.matmul(ps[:, 7, 1:2], g_row, ones_row[:, 0:1], start=True, stop=True)
            for j in (0, 1):
                mm = pe.matmul(ps[:, 4 + j, :], ones_row, final_bc[0:1, j * 512:(j + 1) * 512], start=True, stop=True)
            mm.then_inc(S["p_const"], 1)

            def scores(n):
                t, h = n // H, n % H
                W = (t + 1) * P
                pe.wait_ge(S["d_qlo"], n + 1)
                if h % 4 == 0:
                    pe.wait_ge(S["l_klo"], 2 * t + h // 4 + 1)
                for j in (0, 1):
                    if n:
                        pe.wait_ge(S["d_t"], 2 * n - 1 + j)
                    for c in range(0, W, 512):
                        w = min(512, W - c)
                        o, k = ps[:, 2 * j + c // 512, 0:w], k_hl[:, 2 * h + j, c:c + w]
                        pe.matmul(o, q_hi[n % 2][:, j, :], k, start=True, stop=False)
                        mm = pe.matmul(o, q_lo[n % 2][:, j, :], k, start=False, stop=True)
                    mm.then_inc(S["p_s0" if j == 0 else "p_s1"], 1)

            def turn(n):
                t, h = n // H, n % H
                pe.wait_ge(S["d_a"], n + 1)
                pe.wait_ge(S["a_at"], at_before[n])
                if n == 0:
                    pe.wait_ge(S["c_ok"], 3)
                for k in range(t + 1):
                    mm = pe.transpose(ps[:, 4 + k // 4, (k % 4) * P:(k % 4 + 1) * P], s0[n % 3][:, k * P:(k + 1) * P],
                                      ident[:, :])
                    if k == 3 or k == t:
                        mm.then_inc(S["p_at"], 1)

            def values(n):
                t, h = n // H, n % H
                pe.wait_ge(S["a_at"], at_before[n + 1])
                if h == 0:
                    pe.wait_ge(S["v_landed"], 16 * (t + 1))
                if n:
                    pe.wait_ge(S["d_o"], n)
                for k in range(t + 1):
                    mm = pe.matmul(ps[:, 6, 0:DA_V], aT[n % 2][:, k, :],
                                   v[:, k, h * DA_V:(h + 1) * DA_V], start=(k == 0), stop=(k == t))
                mm.then_inc(S["p_o"], 1)

            def project(t, piece):
                if piece < 2:
                    if piece == 0:
                        pe.wait_ge(S["l_yz"], t + 1)
                        pe.wait_ge(S["d_x2"], 2 * t)
                    else:
                        pe.wait_ge(S["d_yT"], 2 * t + 1)
                    for k in range(4):
                        c = (4 * piece + k) * P
                        mm = pe.transpose(ps[:, 7, k * P:(k + 1) * P], y[t % 2][:, c:c + P], ident[:, :])
                    mm.then_inc(S["p_yT"], 1)
                    return
                j, part = piece // 2 - 1, piece % 2
                if part == 0:
                    if t == 0 and j == 0:
                        pe.wait_ge(S["wout_in"], 16)
                    if j == 0:
                        pe.wait_ge(S["d_yT"], 2 * t + 2)
                    else:
                        pe.wait_ge(S["d_x2"], 2 * t + 1)
                for k in range(4 * part, 4 * part + 4):
                    mm = pe.matmul(ps[:, 7, :], yT[:, k, :], wout[:, k, j * 512:(j + 1) * 512],
                                   start=(k == 0), stop=(k == KT - 1))
                if part == 1:
                    mm.then_inc(S["p_out"], 1)

            scores(0)
            for n in range(N + 2):
                if n + 1 < N:
                    scores(n + 1)
                if 0 <= n - 1 < N:
                    turn(n - 1)
                if 0 <= n - 2:
                    values(n - 2)
                tile, piece = piece_of(n)
                if piece is not None:
                    project(tile, piece)
            for n in range(N + 2, N + H):
                tile, piece = piece_of(n)
                if piece is not None:
                    project(tile, piece)
            for piece in range(PIECES):
                project(TILES - 1, piece)

        @block.scalar
        def _(act):
            def high_keys(c):
                t, u = c // 2, c % 2
                act.wait_ge(S["k_landed"], 32 * (c + 1))
                nc.scalar.copy(k_hl[:, H * u:H * (u + 1), t * P:(t + 1) * P], k_raw[:, :, :]).then_inc(S["a_khi"], 1)

            def high_queries(n):
                t, h = n // H, n % H
                if h % 4 == 0:
                    act.wait_ge(S[f"q{h // 4}_landed"], 32 * (t + 1))
                if n >= 2:
                    act.wait_ge(S["p_s1"], n - 1)
                    act.wait_ge(S["d_qlo"], n - 1)
                nc.scalar.activation(q_hi[n % 2][:, :, :], q_raw[:, 2 * h:2 * h + 2, :], ACT.Copy,
                                     scale=SCALE / SLOPES[h]).then_inc(S["a_qhi"], 1)

            high_keys(0)
            high_keys(1)
            high_queries(0)
            high_queries(1)
            act.wait_ge(S["lam_sum"], 2)
            nc.scalar.activation(lam2[:, 0:2], lam2[:, 0:2], ACT.Exp).then_inc(S["lam_exp"], 1)

            def softmax(n):
                t, h = n // H, n % H
                W = (t + 1) * P
                act.wait_ge(S["d_nm"], n + 1)
                if n >= 2:
                    act.wait_ge(S["d_coef"], n - 1)
                for j, s in ((0, s0[n % 3]), (1, s1[n % 2])):
                    nc.scalar.activation(s[:, 0:W], s[:, 0:W], ACT.Exp, bias=nm[n % 2][:, j:j + 1],
                                         scale=SLOPES[h], accum_out=sm[n % 2][:, j:j + 1]).then_inc(S["a_p"], 1)

            def evict(n):
                t = n // H
                if n >= 2:
                    act.wait_ge(S["p_o"], n - 1)
                for b in range(t // 4 + 1):
                    w = min(4, t + 1 - 4 * b)
                    act.wait_ge(S["p_at"], at_before[n] + b + 1)
                    nc.scalar.copy(aT[n % 2][:, 4 * b:4 * b + w, :], b4(4 + b)[:, 0:w, :]).then_inc(S["a_at"], 1)

            def head_square(n):
                t, h = n // H, n % H
                act.wait_ge(S["d_o"], n + 1)
                if n >= 2:
                    act.wait_ge(S["a_ss"], n - 1)
                if h == 0 and t >= 2:
                    act.wait_ge(S["l_yn"], t - 1)
                nc.scalar.activation(squares[n % 2][:, :], y[t % 2][:, h * DA_V:(h + 1) * DA_V], ACT.Square,
                                     accum_out=rs[t % 2][:, h:h + 1]).then_inc(S["a_ss"], 1)

            def final_squares(t):
                act.wait_ge(S["d_x2"], 2 * t + 2)
                act.wait_ge(out_stored, 16 * t)
                if t:
                    act.wait_ge(S["d_fmean"], t)
                nc.scalar.activation(res[:, :], xr[:, :], ACT.Square, accum_out=fss[:, :]).then_inc(S["a_fss"], 1)

            softmax(0)
            for n in range(N + 3):
                t, h = n // H, n % H
                if n + 2 < N:
                    high_queries(n + 2)
                if n + 1 < N:
                    softmax(n + 1)
                if 0 <= n - 1 < N:
                    evict(n - 1)
                if n >= 3:
                    head_square(n - 3)
                if t + 1 < TILES and h in (3, 4):
                    high_keys(2 * (t + 1) + h - 3)
                if t >= 2 and h == (PROJECT + PIECES + 1) % H:
                    final_squares(t - 2)
            final_squares(TILES - 2)
            final_squares(TILES - 1)

        @block.vector
        def _(dve):
            dve.wait_ge(S["const_in"], 16 * 6)
            for i in (0, 1):
                dve.tensor_tensor_reduce(lam_w[:, i, :], lam_in[:, 2 * i, :], lam_in[:, 2 * i + 1, :], 1.0, 0.0,
                                         ALU.mult, ALU.add, lam2[:, i:i + 1]).then_inc(S["lam_sum"], 1)
            dve.wait_ge(S["iota_ok"], 1)
            dve.scalar_tensor_tensor(out=neg_dist[:, :], in0=neg_dist[:, :], scalar=-1.0, in1=neg_dist[:, :], op0=ALU.mult,
                                     op1=ALU.min).then_inc(S["dist_ok"], 1)
            dve.wait_ge(S["iota_ok"], 2)
            dve.wait_ge(S["lam_exp"], 1)
            dve.tensor_tensor(lam2[:, 3:4], lam2[:, 1:2], lam2[:, 0:1], ALU.subtract).then_inc(S["lam_mul"], 1)
            dve.wait_ge(S["lam_mul"], 1)
            dve.tensor_scalar(lam2[:, 2:3], lam2[:, 3:4], -LAMBDA_INIT, None, ALU.add).then_inc(S["lam_ok"], 1)
            dve.wait_ge(S["p_const"], 1)
            dve.tensor_copy(neg_lam[:, :], ps[:, 7, 0:1]).then_inc(S["c_ok"], 1)
            dve.tensor_scalar(g_col[:, :], ps[:, 7, 1:2], 1.0 - LAMBDA_INIT, None, ALU.mult).then_inc(S["c_ok"], 1)
            dve.tensor_copy(final_bc[:, :], ps[:, 4:6, :].rearrange("p b n -> p (b n)")).then_inc(S["c_ok"], 1)
            dve.wait_ge(S["c_ok"], 3)

            def maxima(n):
                h = n % H
                W = (n // H + 1) * P
                if n >= 2:
                    dve.wait_ge(S["d_a"], n - 1)
                if n >= 3:
                    dve.wait_ge(S["p_at"], at_before[n - 2])
                for j, s in ((0, s0[n % 3]), (1, s1[n % 2])):
                    dve.wait_ge(S["p_s0" if j == 0 else "p_s1"], n + 1)
                    dve.tensor_tensor_reduce(s[:, 0:W], score[j][:, 0:W], neg_dist[:, SEQ - W:SEQ], 1.0, -3e38,
                                             ALU.add, ALU.max, mx[n % 2][:, j:j + 1]).then_inc(S["d_t"], 1)
                dve.wait_ge(S["d_t"], 2 * n + 2)
                dve.tensor_scalar(nm[n % 2][:, :], mx[n % 2][:, :], -SLOPES[h], None, ALU.mult).then_inc(S["d_nm"], 1)

            def combine(n):
                t, h = n // H, n % H
                W = (t + 1) * P
                b = n % 2
                dve.wait_ge(S["a_p"], 2 * n + 2)
                dve.reciprocal(rc[b][:, :], sm[b][:, :]).then_inc(S["d_rc"], 1)
                dve.wait_ge(S["d_rc"], n + 1)
                dve.scalar_tensor_tensor(out=coef[b][:, :], in0=sm[b][:, 0:1], scalar=neg_lam[:, 0:1],
                                         in1=rc[b][:, 1:2], op0=ALU.mult, op1=ALU.mult).then_inc(S["d_coef"], 1)
                dve.tensor_copy(r0[t % 2][:, h:h + 1], rc[b][:, 0:1]).then_inc(S["d_r0"], 1)
                dve.wait_ge(S["d_coef"], n + 1)
                dve.scalar_tensor_tensor(out=s0[n % 3][:, 0:W], in0=s1[b][:, 0:W], scalar=coef[b][:, 0:1],
                                         in1=s0[n % 3][:, 0:W], op0=ALU.mult, op1=ALU.add).then_inc(S["d_a"], 1)

            def over_sum(n):
                t, h = n // H, n % H
                dve.wait_ge(S["p_o"], n + 1)
                if h == 0 and t >= 2:
                    dve.wait_ge(S["p_yT"], 2 * (t - 1))
                dve.tensor_scalar(y[t % 2][:, h * DA_V:(h + 1) * DA_V], ps[:, 6, 0:DA_V],
                                  r0[t % 2][:, h:h + 1], None, ALU.mult).then_inc(S["d_o"], 1)

            def low_queries(n):
                h = n % H
                dve.wait_ge(S["a_qhi"], n + 1)
                dve.scalar_tensor_tensor(out=q_lo[n % 2][:, :, :], in0=q_raw[:, 2 * h:2 * h + 2, :],
                                         scalar=SCALE / SLOPES[h], in1=q_hi[n % 2][:, :, :].bitcast(F32),
                                         op0=ALU.mult, op1=ALU.subtract).then_inc(S["d_qlo"], 1)

            def head_means(t):
                dve.wait_ge(S["a_ss"], H * (t + 1))
                dve.tensor_scalar(rs[t % 2][:, :], rs[t % 2][:, :], 1.0 / DA_V, EPS, ALU.mult, ALU.add).then_inc(S["d_mean"], 1)

            def piece_out(t, piece):
                if piece < 2:
                    dve.wait_ge(S["p_yT"], 2 * t + piece + 1)
                    dve.tensor_scalar(yT[:, 4 * piece:4 * piece + 4, :], b4(7), g_col[:, 0:1], None,
                                      ALU.mult).then_inc(S["d_yT"], 1)
                elif piece % 2 == 1:
                    j = piece // 2 - 1
                    c = slice(j * 512, (j + 1) * 512)
                    dve.wait_ge(S["x_landed"], 16 * (t + 1))
                    dve.wait_ge(S["p_out"], 2 * t + j + 1)
                    dve.tensor_tensor(xr[:, c], ps[:, 7, :], xr[:, c], ALU.add).then_inc(S["d_x2"], 1)

            def final(t):
                dve.wait_ge(S["a_fss"], t + 1)
                dve.tensor_scalar(fs[:, :], fss[:, :], 1.0 / D, EPS, ALU.mult, ALU.add).then_inc(S["d_fmean"], 1)
                dve.wait_ge(S["l_frstd"], t + 1)
                dve.scalar_tensor_tensor(out=res[:, :], in0=xr[:, :], scalar=fs[:, 0:1], in1=final_bc[:, :],
                                         op0=ALU.mult, op1=ALU.mult).then_inc(S["d_res"], 1)

            low_queries(0)
            low_queries(1)
            maxima(0)
            for n in range(N + 4):
                t, h = n // H, n % H
                if 0 <= n - 3 < N:
                    over_sum(n - 3)
                tile, piece = piece_of(n - 1)
                if piece is not None:
                    piece_out(tile, piece)
                if n + 1 < N:
                    maxima(n + 1)
                if n + 2 < N:
                    low_queries(n + 2)
                if n < N:
                    combine(n)
                if t and h == NORMALISE:
                    head_means(t - 1)
                if t >= 2 and h == (PROJECT + PIECES + 2) % H:
                    final(t - 2)
            for n in range(N + 4, N + H + 1):
                tile, piece = piece_of(n - 1)
                if piece is not None:
                    piece_out(tile, piece)
            final(TILES - 2)
            for piece in range(PIECES):
                piece_out(TILES - 1, piece)
            final(TILES - 1)


def hybrid(nc, x, ab_norm_g, ab_w_in, ab_ssd_conv_w, ab_ssd_conv_b, ab_dt_bias, ab_a_log, ab_d_skip, ab_ssd_norm_g,
           ab_ml_conv_w, ab_ml_conv_b, ab_i_bias, ab_f_bias, ab_ml_norm_g, ab_w_out, c_norm_g, c_w_in, c_lam_q1,
           c_lam_k1, c_lam_q2, c_lam_k2, c_subln_g, c_w_out, final_norm_g, out):
    def scratch(name, shape):
        return nc.dram_tensor(name, shape, F32, kind="Internal").ap()

    def rows(v):
        return v.rearrange("a (r c) -> (a r) c", c=P)

    feat0 = scratch("feat0", [FEAT_T, P, SEQ])
    tok0 = scratch("tok0", [SEQ, 4 * D])
    gates = scratch("gates", [GATES, SEQ])
    x1 = scratch("x1", [SEQ, D])
    feat1 = scratch("feat1", [4 * DA_HEADS, DA_QK, SEQ])
    tok1 = scratch("tok1", [SEQ, 2 * D])
    x_in = x[0]
    taps = [r for j in range(CONV) for r in (rows(ab_ssd_conv_w[0, j:j + 1, :]), rows(ab_ml_conv_w[0, j:j + 1, :]))]

    projection(nc, "p", x_in, ab_w_in[0], [rows(ab_norm_g)] + taps + [rows(ab_ssd_conv_b), rows(ab_ml_conv_b)],
               [C_XBC, C_XBC + BLK, C_XBC + 2 * BLK, C_Q, C_K], feat0,
               [(C_ZA, ACT.Silu), (C_ZA + BLK, ACT.Silu), (C_ZB, ACT.Silu), (C_ZB + BLK, ACT.Silu),
                (C_OG, ACT.Sigmoid), (C_OG + BLK, ACT.Sigmoid), (C_V, ACT.Copy), (C_V + BLK, ACT.Copy)],
               tok0, conv=True, gate_out=gates)
    with ExitStack() as outer:
        yT = Part(nc, outer, "y").sb("yT", [P, TILES, AB_OUT_T, P])
        with ExitStack() as ctx:
            m = Part(nc, ctx, "k")
            keep = dict(table=m.sb("table", [P, TILES, T_ALL]), maxrows=m.sb("maxrows", [ML_HEADS, TILES, 2, P]),
                        ident=m.sb("ident", [P, P]), ident_bf=m.sb("ident_bf", [P, P], BF16), tri=m.sb("tri", [P, P]),
                        later=m.sb("later", [P, P], BF16), head_row=m.sb("head_row", [ML_HEADS, ML_HEADS, P]),
                        half=m.sb("half", [P, ML_HEADS]))
            scan_gates(nc, keep, gates, ab_dt_bias, ab_a_log, ab_i_bias, ab_f_bias)
            scan_chunks(nc, keep, yT, feat0, tok0, [rows(ab_ssd_norm_g), rows(ab_ml_norm_g)], ab_d_skip)
        out_projection(nc, "o", yT, x_in, ab_w_out[0], x1)
    projection(nc, "q", x1, c_w_in[0], [rows(c_norm_g)], [0, BLK, D, D + BLK], feat1.rearrange("(n j) d t -> n (j d) t", j=2),
               [(2 * D, ACT.Copy), (2 * D + BLK, ACT.Copy), (3 * D, ACT.Silu), (3 * D + BLK, ACT.Silu)], tok1)
    attention(nc, feat1, tok1, x1, [c_lam_q1, c_lam_k1, c_lam_q2, c_lam_k2], c_subln_g, c_w_out[0],
              final_norm_g.rearrange("(a n) -> a n", a=1), out[0])


_INS = ['x', 'ab_norm_g', 'ab_w_in', 'ab_ssd_conv_w', 'ab_ssd_conv_b', 'ab_dt_bias', 'ab_a_log', 'ab_d_skip',
        'ab_ssd_norm_g', 'ab_ml_conv_w', 'ab_ml_conv_b', 'ab_i_bias', 'ab_f_bias', 'ab_ml_norm_g', 'ab_w_out',
        'c_norm_g', 'c_w_in', 'c_lam_q1', 'c_lam_k1', 'c_lam_q2', 'c_lam_k2', 'c_subln_g', 'c_w_out',
        'final_norm_g']


def kernel(**inputs):
    import concourse.bacc as bacc
    from concourse.bass_utils import run_bass_kernel_spmd

    nc = bacc.Bacc("TRN2", target_bir_lowering=False, num_devices=1)
    arrays, args = {}, []
    for name in _INS:
        a = np.ascontiguousarray(inputs[name])
        arrays[f"in_{name}"] = a
        args.append(nc.dram_tensor(f"in_{name}", a.shape, mybir.dt.from_np(a.dtype), kind="ExternalInput").ap())
    args.append(nc.dram_tensor("out_0", (1, SEQ, D), F32, kind="ExternalOutput").ap())
    hybrid(nc, *args)
    r = run_bass_kernel_spmd(nc, [arrays], core_ids=[0])
    return r.results[0]["out_0"]
```

```python
from contextlib import ExitStack

import numpy as np

import concourse.bass as bass
from concourse import mybir

F32 = mybir.dt.float32
F32R = mybir.dt.float32r
BF16 = mybir.dt.bfloat16
ALU = mybir.AluOpType
ACT = mybir.ActivationFunctionType
AX = mybir.AxisListType

P = 128
SEQ = 1024
D = 1024
TILES = SEQ // P
KT = D // P
BLK = 512
EPS = 1e-6
MASKED = -1e30

SSD_HEADS, SSD_DIM, SSD_STATE, SSD_GROUPS = 16, 64, 128, 2
SSD_INNER = SSD_HEADS * SSD_DIM
SSD_XBC = SSD_INNER + 2 * SSD_GROUPS * SSD_STATE
ML_HEADS, ML_QK, ML_V = 4, 128, 256
ML_INNER = ML_HEADS * ML_V
CONV = 4
GATES = SSD_HEADS + 2 * ML_HEADS
DECAYS = SSD_HEADS + ML_HEADS
XBC_T = SSD_XBC // P
QK_T = 2 * ML_HEADS * ML_QK // P
FEAT_T = XBC_T + QK_T
AB_OUT_T = (SSD_INNER + ML_INNER) // P

DA_HEADS, DA_QK, DA_V = 8, 64, 128

C_ZA = 0
C_XBC = C_ZA + SSD_INNER
C_DT = C_XBC + SSD_XBC
C_ZB = C_DT + SSD_HEADS
C_Q = C_ZB + ML_INNER
C_K = C_Q + ML_HEADS * ML_QK
C_V = C_K + ML_HEADS * ML_QK
C_IG = C_V + ML_INNER
C_OG = C_IG + 2 * ML_HEADS


def over(eng, first, count, body):
    while first < 2 and count:
        body(first, first % 2, first // 2)
        first, count = first + 1, count - 1
    pairs = count // 2
    if pairs:
        with eng.Fori(0, pairs) as i:
            for j in (0, 1):
                body(i * 2 + (first + j), (first + j) % 2, i + (first + j) // 2)
    if count % 2:
        n = first + count - 1
        body(n, n % 2, n // 2)


class Part:

    def __init__(self, nc, ctx, tag):
        self.nc, self.ctx, self.tag = nc, ctx, tag

    def sb(self, name, shape, dt=F32):
        return self.ctx.enter_context(self.nc.sbuf_tensor(f"{self.tag}_{name}", shape, dt))

    def ps(self, name, shape, dt=F32):
        return self.ctx.enter_context(self.nc.psum_tensor(f"{self.tag}_{name}", shape, dt))

    def sem(self, name):
        return self.nc.alloc_semaphore(f"{self.tag}_{name}")


def mid(ap, n):
    a = ap.unsqueeze(1)
    return a.broadcast_to([a.shape[0], n] + list(a.shape[2:]))


def last(ap, n):
    a = ap.unsqueeze(len(ap.shape))
    return a.broadcast_to(list(a.shape[:-1]) + [n])


def identity(gp, t, sem, done):
    gp.memset(t[:, :], 0.0).then_inc(sem, 1)
    gp.wait_ge(sem, done - 1)
    gp.affine_select(out=t[:, :], in_=t[:, :], compare_op=ALU.not_equal, fill=1.0, base=0,
                     pattern=[[-1, P]], channel_multiplier=1).then_inc(sem, 1)


def projection(nc, tag, x, w_in, rows, feat_cols, feat_out, tok_blocks, tok_out, conv=False, gate_out=None):
    nrows = sum(r.shape[0] for r in rows)
    nf, nt = len(feat_cols), len(tok_blocks)
    nb = nf + nt
    w_tiled = w_in.rearrange("(k p) n -> p k n", p=P)
    with ExitStack() as ctx:
        ctx.enter_context(nc.cleanup_on_exit())
        m = Part(nc, ctx, tag)
        h_hi = m.sb("h_hi", [P, KT, SEQ], F32R)
        h_lo = m.sb("h_lo", [P, KT, SEQ], F32R)
        w_raw = [m.sb(f"w_raw{i}", [P, KT, BLK]) for i in (0, 1)]
        w_hi = [m.sb(f"w_hi{i}", [P, KT, BLK], F32R) for i in (0, 1)]
        w_lo = [m.sb(f"w_lo{i}", [P, KT, BLK], F32R) for i in (0, 1)]
        XIN = 4
        x_in = [w_raw[1][:, 2 * i:2 * i + 2, :].rearrange("p a n -> p (a n)") for i in range(XIN)]
        h_f = [[m.sb(f"h_f{i}{s}", [P, 4, P]) for s in (0, 1)] for i in (0, 1)]
        stage = [m.sb(f"stage{i}", [P, BLK]) for i in range(4)]
        ident = m.sb("ident", [P, P])
        row_in = m.sb("row_in", [P, P])
        cols = m.sb("cols", [P, nrows])
        junk = m.sb("junk", [P, D])
        sumsq = [m.sb(f"sumsq{i}", [P, 1]) for i in (0, 1)]
        rstd = [m.sb(f"rstd{i}", [P, 1]) for i in (0, 1)]
        EARLY = TILES // 2
        BEHIND = ((4, 5), (6,), (7,), ())
        diag = [m.sb(f"diag{i}", [P, P]) for i in (0, 1)]
        half = m.sb("half", [P, 1])
        if conv:
            c_raw = [m.sb(f"c_raw{i}", [P, CONV - 1 + SEQ]) for i in (0, 1)]
            c_acc = [junk, m.sb("c_acc1", [P, SEQ])]
        if gate_out is not None:
            g_raw = m.sb("g_raw", [P, KT, GATES])
            g_hi = m.sb("g_hi", [P, KT, GATES], F32R)
            g_lo = m.sb("g_lo", [P, KT, GATES], F32R)
            g_st = m.sb("g_st", [GATES, SEQ])
        bank = [m.ps(f"bank{i}", [P, 512]) for i in range(8)]
        t_bank = [[bank[1], bank[3]], [bank[5], bank[7]]]
        FIRST_ORDER = [0, 2, 4, 6, 1, 3, 5, 7]
        FIRST = 4

        rows_in = m.sem("rows_in")
        x_landed = [m.sem(f"x_landed{i}") for i in range(XIN)]
        w0_landed = [m.sem(f"w0_landed{i}") for i in range(FIRST)]
        w_landed = [m.sem(f"w_landed{i}") for i in (0, 1)]
        g_landed = m.sem("g_landed")
        ident_ok = m.sem("ident_ok")
        zeroed = m.sem("zeroed")
        rows_T = m.sem("rows_T")
        cols_ok = m.sem("cols_ok")
        squared = m.sem("squared")
        mean_ok = m.sem("mean_ok")
        rstd_ok = m.sem("rstd_ok")
        diag_ok = m.sem("diag_ok")
        normed = m.sem("normed")
        x_T = m.sem("x_T")
        hf_ok = m.sem("hf_ok")
        hhi_ok = m.sem("hhi_ok")
        h_ok = m.sem("h_ok")
        hi_ok = m.sem("hi_ok")
        split = m.sem("split")
        g_split = m.sem("g_split")
        full = m.sem("full")
        staged = m.sem("staged")
        stored = [m.sem(f"stored{i}") for i in range(4)]
        conv_in = m.sem("conv_in")
        tapped = m.sem("tapped")
        conv_ok = m.sem("conv_ok")
        silu_ok = m.sem("silu_ok")
        c_stored = [m.sem(f"c_stored{i}") for i in (0, 1)]
        g_full = m.sem("g_full")
        g_staged = m.sem("g_staged")
        g_stored = m.sem("g_stored")

        block = ctx.enter_context(nc.Block())

        @block.sync
        def _(sp):
            at = 0
            sp.dma_start(x_in[0], x[0:P, :]).then_inc(x_landed[0], 16)
            for r in rows:
                sp.dma_start(row_in[at:at + r.shape[0], :], r).then_inc(rows_in, 16)
                at += r.shape[0]

            def load_x(t):
                if t >= XIN:
                    sp.wait_ge(x_T, 2 * (t - XIN + 1))
                sp.dma_start(x_in[t % XIN], x[t * P:(t + 1) * P, :]).then_inc(x_landed[t % XIN], 16)

            def load_w0(f):
                c = feat_cols[0] + f * P
                sp.dma_start(w_raw[0][:, :, f * P:(f + 1) * P], w_tiled[:, :, c:c + P]).then_inc(w0_landed[f], 16)

            def load_w(b):
                c = feat_cols[b] if b < nf else tok_blocks[b - nf][0]
                if b >= 2:
                    sp.wait_ge(split, FIRST + b - 2)
                sp.dma_start(w_raw[b % 2][:, :, :], w_tiled[:, :, c:c + BLK]).then_inc(w_landed[b % 2], 16)

            load_x(1)
            load_w0(0)
            load_x(2)
            load_x(3)
            for f in range(1, FIRST):
                load_w0(f)
                load_x(3 + f)
            load_x(7)
            sp.wait_ge(x_T, 2 * TILES)
            load_w(1)
            if gate_out is not None:
                with nc.allow_non_contiguous_dma(reason="24 gate columns"):
                    sp.dma_start(g_raw[:, :, 0:SSD_HEADS], w_tiled[:, :, C_DT:C_DT + SSD_HEADS]).then_inc(g_landed, 16)
                    sp.dma_start(g_raw[:, :, SSD_HEADS:GATES],
                                 w_tiled[:, :, C_IG:C_IG + 2 * ML_HEADS]).then_inc(g_landed, 16)
            for b in range(nb):
                if b + 2 < nb:
                    load_w(b + 2)
                if b < nf and conv:
                    for f in range(4):
                        n = 4 * b + f
                        sp.wait_ge(silu_ok, n + 1)
                        sp.dma_start(feat_out[n, :, :], c_acc[f % 2][:, :]).then_inc(c_stored[f % 2], 16)
                    continue
                for o in range(8):
                    sp.wait_ge(staged, 8 * (b - (nf if conv else 0)) + o + 1)
                    if b < nf:
                        dst = feat_out[4 * b + o // 2, :, (o % 2) * BLK:(o % 2 + 1) * BLK]
                    else:
                        dst = tok_out[o * P:(o + 1) * P, (b - nf) * BLK:(b - nf + 1) * BLK]
                    sp.dma_start(dst, stage[o % 4][:, :]).then_inc(stored[o % 4], 16)
            if gate_out is not None:
                sp.wait_ge(g_staged, 2)
                sp.dma_start(gate_out, g_st[:, :]).then_inc(g_stored, 16)
                sp.wait_ge(g_stored, 16)
            for s in range(4):
                sp.wait_ge(stored[s], 16 * 2 * (nb - (nf if conv else 0)))
            if conv:
                for s in (0, 1):
                    sp.wait_ge(c_stored[s], 16 * 2 * nf)

        @block.gpsimd
        def _(gp):
            identity(gp, ident, ident_ok, 2)
            gp.memset(half[:, :], -0.5).then_inc(zeroed, 1)
            if conv:
                for c in c_raw:
                    gp.memset(c[:, 0:CONV - 1], 0.0).then_inc(zeroed, 1)
            gp.wait_ge(zeroed, 1)

            for t in range(TILES):
                r = rstd[t % 2][:, :]
                gp.wait_ge(squared, t + 1)
                if t >= 2:
                    gp.wait_ge(*((diag_ok, t - 1) if t - 2 < EARLY else (normed, t - 1 - EARLY)))
                gp.tensor_scalar(r, sumsq[t % 2][:, :], 1.0 / D, EPS, ALU.mult, ALU.add).then_inc(mean_ok, 1)
                gp.wait_ge(mean_ok, t + 1)
                gp.tensor_tensor(r, r, half[:, :], ALU.pow).then_inc(rstd_ok, 1)
                if t < EARLY:
                    gp.wait_ge(rstd_ok, t + 1)
                    if t >= 2:
                        gp.wait_ge(x_T, 2 * (t - 1))
                    gp.tensor_tensor(diag[t % 2][:, :], ident[:, :], r.broadcast_to([P, P]), ALU.mult).then_inc(diag_ok, 1)
                if t == 1:
                    c = slice(0, P)
                    gp.wait_ge(hi_ok, 1)
                    gp.tensor_tensor(w_lo[0][:, :, c], w_raw[0][:, :, c], w_hi[0][:, :, c].bitcast(F32),
                                     ALU.subtract).then_inc(split, 1)

        @block.scalar
        def _(act):
            def square(t):
                act.wait_ge(x_landed[t % XIN], 16 * (t // XIN + 1))
                if t:
                    act.wait_ge(squared, t)
                if t >= 2:
                    act.wait_ge(mean_ok, t - 1)
                nc.scalar.activation(junk[:, :], x_in[t % XIN], ACT.Square, accum_out=sumsq[t % 2][:, :]).then_inc(squared, 1)

            def scale(t):
                act.wait_ge(rstd_ok, t + 1)
                nc.scalar.activation(x_in[t % XIN], x_in[t % XIN], ACT.Copy, scale=rstd[t % 2][:, 0:1]).then_inc(normed, 1)

            def high(t):
                for s in (0, 1):
                    act.wait_ge(hf_ok, t * 2 + (s + 1))
                    nc.scalar.copy(h_hi[:, 4 * s:4 * s + 4, t * P:(t + 1) * P], h_f[t % 2][s][:, :, :]).then_inc(hhi_ok, 1)

            square(0)
            square(1)
            act.wait_ge(w0_landed[0], 16)
            nc.scalar.copy(w_hi[0][:, :, 0:P], w_raw[0][:, :, 0:P]).then_inc(hi_ok, 1)
            high(0)
            for t in range(2, EARLY):
                square(t)
                high(t - 1)
            high(EARLY - 1)
            square(EARLY)
            scale(EARLY)
            for t in range(EARLY + 1, TILES):
                square(t)
                scale(t)
                high(t - 1)
            high(TILES - 1)

            if conv:
                def feature_block(b, order=range(8)):
                    for f in range(4):
                        for s in (0, 1):
                            o = 2 * f + s
                            act.wait_ge(full, b * 8 + (order.index(o) + 1))
                            nc.scalar.copy(c_raw[f % 2][:, CONV - 1 + s * BLK:CONV - 1 + (s + 1) * BLK],
                                           bank[o][:, :]).then_inc(conv_in, 1)
                        act.wait_ge(conv_ok, b * 4 + (f + 1))
                        nc.scalar.activation(c_acc[f % 2][:, :], c_acc[f % 2][:, :], ACT.Silu).then_inc(silu_ok, 1)

                feature_block(0, FIRST_ORDER)
                with act.Fori(1, nf) as b:
                    feature_block(b)
            for b in range(0 if not conv else nf, nb):
                func = ACT.Copy if b < nf else tok_blocks[b - nf][1]
                for o in range(8):
                    k = b - (nf if conv else 0)
                    act.wait_ge(full, 8 * b + (FIRST_ORDER.index(o) if b == 0 else o) + 1)
                    act.wait_ge(stored[o % 4], 16 * (2 * k + o // 4))
                    nc.scalar.activation(stage[o % 4][:, :], bank[o][:, :], func).then_inc(staged, 1)
            if gate_out is not None:
                for s in (0, 1):
                    act.wait_ge(g_full, s + 1)
                    nc.scalar.copy(g_st[:, s * BLK:(s + 1) * BLK], bank[s][0:GATES, :]).then_inc(g_staged, 1)

        @block.vector
        def _(dve):
            dve.wait_ge(rows_T, 1)
            dve.tensor_copy(cols[:, :], bank[7][:, 0:nrows]).then_inc(cols_ok, 1)
            dve.wait_ge(cols_ok, 1)

            def gained(t):
                for s in (0, 1):
                    dve.wait_ge(x_T, t * 2 + (s + 1))
                    if t >= 2:
                        dve.wait_ge(h_ok, 2 * (t - 1))
                    dve.tensor_tensor(h_f[t % 2][s][:, :, :], t_bank[t % 2][s][:, :].rearrange("p (a b) -> p a b", a=4),
                                      last(cols[:, 4 * s:4 * s + 4], P), ALU.mult).then_inc(hf_ok, 1)

            def low(t):
                ts = slice(t * P, (t + 1) * P)
                for s in (0, 1):
                    dve.wait_ge(hhi_ok, t * 2 + (s + 1))
                    dve.tensor_tensor(h_lo[:, 4 * s:4 * s + 4, ts], h_f[t % 2][s][:, :, :],
                                      h_hi[:, 4 * s:4 * s + 4, ts].bitcast(F32), ALU.subtract).then_inc(h_ok, 1)

            def split_first(f):
                c = slice(f * P, (f + 1) * P)
                dve.wait_ge(w0_landed[f], 16)
                dve.tensor_copy(w_hi[0][:, :, c], w_raw[0][:, :, c]).then_inc(hi_ok, 1)
                dve.wait_ge(hi_ok, f + 1)
                dve.tensor_tensor(w_lo[0][:, :, c], w_raw[0][:, :, c], w_hi[0][:, :, c].bitcast(F32),
                                  ALU.subtract).then_inc(split, 1)

            gained(0)
            for t in range(1, EARLY):
                gained(t)
                low(t - 1)
            low(EARLY - 1)
            dve.wait_ge(split, 1)
            split_first(1)
            for t in range(EARLY, TILES):
                gained(t)
                low(t)
                if t - EARLY + 2 < FIRST:
                    split_first(t - EARLY + 2)

            def split_block(n, par, prior):
                dve.wait_ge(w_landed[par], prior * 16 + 16 * par)
                if not isinstance(n, int) or n >= 2:
                    dve.wait_ge(full, (n - 1) * 8)
                dve.tensor_copy(w_hi[par][:, :, :], w_raw[par][:, :, :]).then_inc(hi_ok, 1)
                dve.wait_ge(hi_ok, n + FIRST)
                dve.tensor_tensor(w_lo[par][:, :, :], w_raw[par][:, :, :], w_hi[par][:, :, :].bitcast(F32),
                                  ALU.subtract).then_inc(split, 1)

            if gate_out is not None:
                dve.wait_ge(g_landed, 32)
                dve.tensor_copy(g_hi[:, :, :], g_raw[:, :, :]).then_inc(g_split, 1)
                dve.wait_ge(g_split, 1)
                dve.tensor_tensor(g_lo[:, :, :], g_raw[:, :, :], g_hi[:, :, :].bitcast(F32),
                                  ALU.subtract).then_inc(g_split, 1)
            if conv:
                dve.wait_ge(zeroed, 3)

                def conv_tile(n, b, f):
                    raw, acc = c_raw[f % 2], c_acc[f % 2]
                    dve.wait_ge(conv_in, n * 2 + 2)
                    dve.wait_ge(c_stored[f % 2], b * 32 + 16 * (f // 2))
                    dve.tensor_scalar(acc[:, :], raw[:, 0:SEQ], cols[:, bass.ds(n + KT, 1)],
                                      cols[:, bass.ds(n + (KT + CONV * FEAT_T), 1)], ALU.mult, ALU.add).then_inc(tapped, 1)
                    for j in range(1, CONV):
                        dve.wait_ge(tapped, n * (CONV - 1) + j)
                        out = dve.scalar_tensor_tensor(
                            out=acc[:, :], in0=raw[:, j:j + SEQ], scalar=cols[:, bass.ds(n + (KT + j * FEAT_T), 1)],
                            in1=acc[:, :], op0=ALU.mult, op1=ALU.add)
                        out.then_inc(tapped if j < CONV - 1 else conv_ok, 1)

                def feature_block(b, par, prior):
                    split_block(b + 1, 1 - par, prior + par)
                    for f in range(4):
                        conv_tile(b * 4 + f, b, f)

                over(dve, 0, nf, feature_block)
                over(dve, nf + 1, nb - nf - 1, split_block)
            else:
                over(dve, 1, nb - 1, split_block)

        @block.tensor
        def _(pe):
            def transpose_tile(t):
                pe.wait_ge(*((diag_ok, t + 1) if t < EARLY else (normed, t - EARLY + 1)))
                if t == 1:
                    pe.wait_ge(cols_ok, 1)
                if t >= 2:
                    pe.wait_ge(hf_ok, (t - 1) * 2)
                for s in (0, 1):
                    for k in range(4):
                        out = t_bank[t % 2][s][:, k * P:(k + 1) * P]
                        part = x_in[t % XIN][:, (4 * s + k) * P:(4 * s + k + 1) * P]
                        if t < EARLY:
                            mm = pe.matmul(out, part, diag[t % 2][:, :], start=True, stop=True)
                        else:
                            mm = pe.transpose(out, part, ident[:, :])
                    mm.then_inc(x_T, 1)

            def products(out, pairs):
                for q, (a, c) in enumerate(pairs):
                    mm = pe.matmul(out, a, c, start=(q == 0), stop=(q == len(pairs) - 1))
                return mm

            def feature_output(par, o):
                f, s = o // 2, o % 2
                fs, ts = slice(f * P, (f + 1) * P), slice(s * BLK, (s + 1) * BLK)
                products(bank[o][:, :], [pair for k in range(KT) for pair in (
                    (w_hi[par][:, k, fs], h_hi[:, k, ts]), (w_hi[par][:, k, fs], h_lo[:, k, ts]),
                    (w_lo[par][:, k, fs], h_hi[:, k, ts]))]).then_inc(full, 1)

            def feature_block(n, par, prior):
                pe.wait_ge(split, n + FIRST)
                for o in range(8):
                    pe.wait_ge(conv_in if conv else staged, (n - 1) * 8 + (o + 1))
                    feature_output(par, o)

            def token_block(n, par, prior):
                pe.wait_ge(split, n + FIRST)
                for o in range(8):
                    if not conv:
                        pe.wait_ge(staged, (n - 1) * 8 + (o + 1))
                    elif isinstance(n, int) and n == nf:
                        pe.wait_ge(conv_in, 8 * (nf - 1) + o + 1)
                    else:
                        pe.wait_ge(staged, (n - (nf + 1)) * 8 + (o + 1))
                    ts = slice(o * P, (o + 1) * P)
                    products(bank[o][:, :], [pair for k in range(KT) for pair in (
                        (h_hi[:, k, ts], w_hi[par][:, k, :]), (h_hi[:, k, ts], w_lo[par][:, k, :]),
                        (h_lo[:, k, ts], w_hi[par][:, k, :]))]).then_inc(full, 1)

            transpose_tile(0)
            pe.wait_ge(rows_in, 16 * len(rows))
            pe.wait_ge(ident_ok, 2)
            pe.transpose(bank[7][:, 0:nrows], row_in[0:nrows, :], ident[0:nrows, 0:nrows]).then_inc(rows_T, 1)
            for t in range(1, EARLY):
                transpose_tile(t)
            pe.wait_ge(h_ok, TILES)
            for f in range(4):
                pe.wait_ge(split, f + 1)
                feature_output(0, 2 * f)
                for t in BEHIND[f]:
                    transpose_tile(t)
            pe.wait_ge(h_ok, 2 * TILES)
            for f in range(4):
                feature_output(0, 2 * f + 1)
            over(pe, 1, nf - 1, feature_block)
            token_block(nf, nf % 2, nf // 2)
            over(pe, nf + 1, nt - 1, token_block)
            if gate_out is not None:
                pe.wait_ge(g_split, 2)
                pe.wait_ge(staged, 8 * (nt - 1) + 2)
                for s in (0, 1):
                    ts = slice(s * BLK, (s + 1) * BLK)
                    mm = products(bank[s][0:GATES, :], [pair for k in range(KT) for pair in (
                        (g_hi[:, k, :], h_hi[:, k, ts]), (g_hi[:, k, :], h_lo[:, k, ts]),
                        (g_lo[:, k, :], h_hi[:, k, ts]))])
                    mm.then_inc(g_full, 1)


T_DT, T_DA, T_EACS, T_NACS, T_U, T_EMT = 0, 16, 32, 48, 64, 68
T_ALL = 72


def load_chunk(sp, chunk, feat, tok, n, par):
    t = bass.ds(n * P, P)
    landed = chunk["landed"][par]
    sp.dma_start(chunk["fe"][par][:, :, :], feat[:, :, t].rearrange("f p t -> p f t")).then_inc(landed, 16)
    sp.dma_start(chunk["gz"][par][:, :, :], tok[t, 0:3 * D].rearrange("p (k n) -> p k n", k=3)).then_inc(landed, 16)
    sp.dma_start(chunk["va"][par][:, :, 0:ML_V], tok[t, 3 * D:4 * D].rearrange("p (h v) -> p h v", h=ML_HEADS)
                 ).then_inc(landed, 16)


OUT_QT = 4


def load_out_weights(sp, w_ahead, w_out, i):
    j, q = divmod(i, AB_OUT_T // OUT_QT)
    sp.dma_start(w_ahead["raw"][i % 2][:, :, :], w_out[q * OUT_QT * P:(q + 1) * OUT_QT * P, j * D // 2:(j + 1) * D // 2]
                 .rearrange("(k p) n -> p k n", p=P)).then_inc(w_ahead["landed"][i % 2], 16)


def scan_gates(nc, keep, gate_rows, dt_bias, a_log, i_bias, f_bias, feat, tok, chunk, load_consts):
    with ExitStack() as ctx:
        ctx.enter_context(nc.cleanup_on_exit())
        m = Part(nc, ctx, "g")
        rows = m.sb("rows", [GATES, SEQ])
        vec = m.sb("vec", [1, GATES + SSD_HEADS])
        ones_row = m.sb("ones_row", [1, P])
        vec_bc = m.sb("vec_bc", [P, GATES + SSD_HEADS])
        a_neg = m.sb("a_neg", [P, SSD_HEADS])
        raw = m.sb("raw", [P, TILES, GATES])
        arg = m.sb("arg", [P, TILES, DECAYS])
        narg = m.sb("narg", [P, TILES, DECAYS])
        e = m.sb("e", [P, TILES, DECAYS])
        s = m.sb("s", [P, TILES, DECAYS])
        s2 = m.sb("s2", [P, TILES, DECAYS])
        q = m.sb("q", [P, TILES, DECAYS])
        sp_ = m.sb("sp", [P, TILES, DECAYS])
        x = m.sb("x", [P, TILES, DECAYS])
        u_row = m.sb("u_row", [ML_HEADS, TILES, P])
        b_row = m.sb("b_row", [ML_HEADS, TILES, P])
        m_row = m.sb("m_row", [ML_HEADS, TILES, P])
        m_prev = m.sb("m_prev", [ML_HEADS, TILES + 1])
        w_log = m.sb("w_log", [ML_HEADS, TILES, P])
        e_row = m.sb("e_row", [ML_HEADS, TILES, P])
        ones = m.sb("ones", [P, P])
        table, maxrows, ident, tri = keep["table"], keep["maxrows"], keep["ident"], keep["tri"]
        p_raw = m.ps("p_raw", [P, 512])
        p_vec = m.ps("p_vec", [P, 512])
        p_cs = m.ps("p_cs", [P, 512])
        p_u = m.ps("p_u", [P, 2, 512])
        p_b = m.ps("p_b", [P, 2, 512])

        landed = m.sem("landed")
        pool_ok = m.sem("pool_ok")
        pe_raw = m.sem("pe_raw")
        pe_vec = m.sem("pe_vec")
        pe_cs = m.sem("pe_cs")
        pe_rows = m.sem("pe_rows")
        pe_emt = m.sem("pe_emt")
        step = m.sem("step")
        a_exp = m.sem("a_exp")
        e_exp = m.sem("e_exp")
        eacs_exp = m.sem("eacs_exp")
        w_exp = m.sem("w_exp")
        emt_exp = m.sem("emt_exp")
        b_ok = m.sem("b_ok")
        MAXIMA_DONE = 27 + 2 * TILES

        block = ctx.enter_context(nc.Block())

        @block.sync
        def _(sp):
            sp.dma_start(rows[:, :], gate_rows).then_inc(landed, 16)
            at = 0
            for v in (dt_bias, i_bias, f_bias, a_log):
                n = v.shape[1]
                sp.dma_start(vec[:, at:at + n], v).then_inc(landed, 16)
                at += n
            load_consts(sp)
            for n in (0, 1):
                load_chunk(sp, chunk, feat, tok, n, n)

        @block.gpsimd
        def _(gp):
            n = 0
            gp.memset(ident[:, :], 0.0).then_inc(pool_ok, 1)
            gp.memset(keep["ident_bf"][:, :], 0.0).then_inc(pool_ok, 1)
            gp.memset(ones[:, :], 1.0).then_inc(pool_ok, 1)
            gp.memset(tri[:, :], 1.0).then_inc(pool_ok, 1)
            gp.memset(keep["later"][:, :], 0.0).then_inc(pool_ok, 1)
            gp.memset(keep["head_row"][:, :, :], 1.0).then_inc(pool_ok, 1)
            gp.memset(ones_row[:, :], 1.0).then_inc(pool_ok, 1)
            gp.memset(m_prev[:, :], 0.0).then_inc(pool_ok, 1)
            gp.memset(keep["half"][:, :], -0.5).then_inc(pool_ok, 1)
            gp.wait_ge(pool_ok, 9)
            for t in (ident, keep["ident_bf"]):
                gp.affine_select(out=t[:, :], in_=t[:, :], compare_op=ALU.not_equal, fill=1.0, base=0,
                                 pattern=[[-1, P]], channel_multiplier=1).then_inc(pool_ok, 1)
            gp.affine_select(out=tri[:, :], in_=tri[:, :], compare_op=ALU.is_ge, fill=0.0, base=0,
                             pattern=[[1, P]], channel_multiplier=-1).then_inc(pool_ok, 1)
            gp.affine_select(out=keep["later"][:, :], in_=keep["later"][:, :], compare_op=ALU.is_ge, fill=MASKED,
                             base=0, pattern=[[1, P]], channel_multiplier=-1).then_inc(pool_ok, 1)
            gp.affine_select(out=keep["head_row"][:, :, :], in_=keep["head_row"][:, :, :], compare_op=ALU.is_equal,
                             fill=0.0, base=0, pattern=[[1, ML_HEADS], [0, P]],
                             channel_multiplier=-1).then_inc(pool_ok, 1)

        @block.tensor
        def _(pe):
            pe.wait_ge(landed, 16 * 5)
            pe.wait_ge(pool_ok, 14)
            pe.matmul(p_vec[:, 0:GATES + SSD_HEADS], ones_row[:, :], vec[:, :], start=True, stop=True).then_inc(pe_vec, 1)
            for c in range(TILES):
                mm = pe.transpose(p_raw[:, c * GATES:(c + 1) * GATES], rows[:, c * P:(c + 1) * P],
                                  ident[0:GATES, 0:GATES])
            mm.then_inc(pe_raw, 1)
            pe.wait_ge(step, 21)
            pe.matmul(p_cs[:, 0:TILES * DECAYS], tri[:, :], x[:, :, :].rearrange("p c h -> p (c h)"),
                      start=True, stop=True).then_inc(pe_cs, 1)
            pe.wait_ge(step, 24)
            for c in range(TILES):
                pe.transpose(p_u[0:ML_HEADS, c // 4, (c % 4) * P:(c % 4 + 1) * P], table[:, c, T_U:T_U + ML_HEADS],
                             ident[:, :])
            for c in range(TILES):
                mm = pe.transpose(p_b[0:ML_HEADS, c // 4, (c % 4) * P:(c % 4 + 1) * P], s[:, c, SSD_HEADS:DECAYS],
                                  ident[:, :])
            mm.then_inc(pe_rows, 1)
            pe.wait_ge(emt_exp, 1)
            for c in range(TILES):
                mm = pe.transpose(p_vec[:, c * ML_HEADS:(c + 1) * ML_HEADS], e_row[:, c, :],
                                  ident[0:ML_HEADS, 0:ML_HEADS])
            mm.then_inc(pe_emt, 1)

        @block.scalar
        def _(act):
            act.wait_ge(step, 1)
            nc.scalar.activation(a_neg[:, :], vec_bc[:, GATES:], ACT.Exp).then_inc(a_exp, 1)
            act.wait_ge(step, 6)
            nc.scalar.activation(e[:, :, :], narg[:, :, :], ACT.Exp).then_inc(e_exp, 1)
            act.wait_ge(step, 22)
            nc.scalar.activation(table[:, :, T_EACS:T_EACS + SSD_HEADS], s[:, :, 0:SSD_HEADS],
                                 ACT.Exp).then_inc(eacs_exp, 1)
            act.wait_ge(pe_rows, 1)
            nc.scalar.copy(b_row[:, :, :].rearrange("h c t -> h (c t)"),
                           p_b[0:ML_HEADS, :, :].rearrange("h a b -> h (a b)")).then_inc(b_ok, 1)
            act.wait_ge(step, MAXIMA_DONE + 1)
            nc.scalar.activation(e_row[:, :, :], b_row[:, :, :], ACT.Exp, scale=-1.0).then_inc(emt_exp, 1)
            act.wait_ge(step, MAXIMA_DONE + 3)
            nc.scalar.activation(maxrows[:, :, 1, :], w_log[:, :, :], ACT.Exp).then_inc(w_exp, 1)

        @block.vector
        def _(dve):
            steps = [0]

            def chain(ins):
                steps[0] += 1
                ins.then_inc(step, 1)
                dve.wait_ge(step, steps[0])

            f = slice(SSD_HEADS, DECAYS)
            dve.wait_ge(pe_vec, 1)
            chain(dve.tensor_copy(vec_bc[:, :], p_vec[:, 0:GATES + SSD_HEADS]))
            dve.wait_ge(pe_raw, 1)
            chain(dve.tensor_tensor(raw[:, :, :], p_raw[:, 0:TILES * GATES].rearrange("p (c g) -> p c g", g=GATES),
                                    mid(vec_bc[:, 0:GATES], TILES), ALU.add))
            chain(dve.tensor_copy(arg[:, :, 0:SSD_HEADS], raw[:, :, 0:SSD_HEADS]))
            chain(dve.tensor_scalar(arg[:, :, f], raw[:, :, SSD_HEADS + ML_HEADS:GATES], -1.0, None, ALU.mult))
            chain(dve.tensor_scalar(q[:, :, :], arg[:, :, :], -1.0, None, ALU.mult))
            chain(dve.tensor_tensor(narg[:, :, :], arg[:, :, :], q[:, :, :], ALU.min))
            dve.wait_ge(e_exp, 1)
            chain(dve.tensor_scalar(q[:, :, :], e[:, :, :], 2.0, None, ALU.add))
            chain(dve.reciprocal(s[:, :, :], q[:, :, :]))
            chain(dve.tensor_tensor(s[:, :, :], s[:, :, :], e[:, :, :], ALU.mult))
            chain(dve.tensor_tensor(s2[:, :, :], s[:, :, :], s[:, :, :], ALU.mult))
            chain(dve.tensor_scalar(q[:, :, :], s2[:, :, :], 1.0 / 15, None, ALU.mult))
            for k in (13, 11, 9, 7, 5, 3):
                chain(dve.scalar_tensor_tensor(out=q[:, :, :], in0=q[:, :, :], scalar=1.0 / k, in1=s2[:, :, :],
                                               op0=ALU.add, op1=ALU.mult))
            chain(dve.scalar_tensor_tensor(out=q[:, :, :], in0=q[:, :, :], scalar=1.0, in1=s[:, :, :],
                                           op0=ALU.add, op1=ALU.mult))
            chain(dve.tensor_scalar(sp_[:, :, :], arg[:, :, :], 0.0, None, ALU.max))
            chain(dve.scalar_tensor_tensor(out=sp_[:, :, :], in0=q[:, :, :], scalar=2.0, in1=sp_[:, :, :],
                                           op0=ALU.mult, op1=ALU.add))
            assert steps[0] == 20, steps
            dve.wait_ge(a_exp, 1)
            dve.tensor_scalar(x[:, :, f], sp_[:, :, f], -1.0, None, ALU.mult)
            dve.scalar_tensor_tensor(out=x[:, :, 0:SSD_HEADS], in0=sp_[:, :, 0:SSD_HEADS], scalar=-1.0,
                                     in1=mid(a_neg[:, :], TILES), op0=ALU.mult, op1=ALU.mult).then_inc(step, 1)
            steps[0] += 1
            dve.wait_ge(pe_cs, 1)
            chain(dve.tensor_copy(s[:, :, :], p_cs[:, 0:TILES * DECAYS].rearrange("p (c h) -> p c h", h=DECAYS)))
            chain(dve.tensor_scalar(table[:, :, T_NACS:T_NACS + SSD_HEADS], s[:, :, 0:SSD_HEADS], -1.0, None, ALU.mult))
            chain(dve.tensor_tensor(table[:, :, T_U:T_U + ML_HEADS], raw[:, :, SSD_HEADS:SSD_HEADS + ML_HEADS],
                                    s[:, :, f], ALU.subtract))
            chain(dve.tensor_copy(table[:, :, T_DT:T_DT + SSD_HEADS], sp_[:, :, 0:SSD_HEADS]))
            chain(dve.tensor_copy(table[:, :, T_DA:T_DA + SSD_HEADS], x[:, :, 0:SSD_HEADS]))
            dve.wait_ge(pe_rows, 1)
            flat = lambda t: t[:, :, :].rearrange("h c t -> h (c t)")
            chain(dve.tensor_copy(flat(u_row), p_u[0:ML_HEADS, :, :].rearrange("h a b -> h (a b)")))
            dve.wait_ge(b_ok, 1)
            for c in range(TILES):
                chain(dve.tensor_tensor_scan(m_row[:, c, :], u_row[:, c, :], u_row[:, c, :], m_prev[:, c:c + 1],
                                             ALU.max, ALU.max))
                chain(dve.tensor_tensor(m_prev[:, c + 1:c + 2], m_row[:, c, P - 1:P], b_row[:, c, P - 1:P], ALU.add))
            assert steps[0] == MAXIMA_DONE, steps
            chain(dve.tensor_tensor(b_row[:, :, :], b_row[:, :, :], m_row[:, :, :], ALU.add))
            chain(dve.tensor_scalar(maxrows[:, :, 0, :], m_row[:, :, :], -1.0, None, ALU.mult))
            chain(dve.tensor_tensor(w_log[:, :, :], maxrows[:, :, 0, :], last(m_prev[:, 0:TILES], P), ALU.add))
            dve.wait_ge(pe_emt, 1)
            chain(dve.tensor_copy(table[:, :, T_EMT:T_EMT + ML_HEADS],
                                  p_vec[:, 0:TILES * ML_HEADS].rearrange("p (c h) -> p c h", h=ML_HEADS)))


def scan_chunks(nc, keep, yT, feat, tok, chunk, w_out, w_ahead):
    VW = ML_V + 1
    HG = SSD_HEADS // SSD_GROUPS
    XS, BT, CT, QT, KTL = 0, 8, 10, 12, 16
    with ExitStack() as ctx:
        ctx.enter_context(nc.cleanup_on_exit())
        m = Part(nc, ctx, "s")
        fe, gz, va, drow, row_in = (chunk[n] for n in ("fe", "gz", "va", "drow", "row_in"))
        g = m.sb("g", [P, T_ALL])
        mr = m.sb("mr", [ML_HEADS, 2, P])
        x_tok = m.sb("x_tok", [P, D])
        xdt = m.sb("xdt", [P, D])
        xe = m.sb("xe", [P, D])
        b_tok = m.sb("b_tok", [P, SSD_GROUPS, SSD_STATE])
        dec = m.sb("dec", [P, SSD_HEADS, P])
        wt = m.sb("wt", [P, SSD_HEADS, P])
        e_end = m.sb("e_end", [P, SSD_HEADS])
        wm = m.sb("wm", [P, ML_HEADS, P])
        st = m.sb("st", [P, ML_HEADS, P])
        qs = m.sb("qs", [P, ML_HEADS, P])
        kg = m.sb("kg", [P, ML_HEADS, P])
        gk = m.sb("gk", [P, ML_HEADS])
        c_dec = m.sb("c_dec", [P, ML_HEADS])
        state = m.sb("state", [P, D])
        cmem = m.sb("cmem", [P, ML_HEADS, VW])
        t1 = m.sb("t1", [P, D])
        y = m.sb("y", [P, 2 * D])
        den = m.sb("den", [P, ML_HEADS])
        den2 = m.sb("den2", [P, ML_HEADS])
        x_sq = m.sb("x_sq", [P, 512])
        ssq = m.sb("ssq", [P, 6])
        rms = m.sb("rms", [P, 6])
        d_bc = m.sb("d_bc", [P, SSD_HEADS])
        gcols = m.sb("gcols", [P, AB_OUT_T])
        ident, ident_bf, tri, later = keep["ident"], keep["ident_bf"], keep["tri"], keep["later"]
        head_row, half, table, maxrows = keep["head_row"], keep["half"], keep["table"], keep["maxrows"]
        ps = m.ps("ps", [P, 8, 512])

        names = """drow_T cols_T cols_ok drow_ok v_ones zero_ok g_ok mr_ok
                   p_xT p_bc p_kT p_acs p_negm p_wint p_qk p_num p_yoff p_ydiag p_state p_cmem p_yT
                   d_xtok d_btok a_dec a_wm a_sqm a_sqy a_ynorm
                   d_wt d_eend d_st d_qs d_cdec d_gk d_kg d_den d_h d_cmem d_t1 d_y d_state d_yb d_yT
                   d_meanm d_meany
                   l_xdt l_xe l_xd l_yd l_yz l_sdec l_rstdm l_rstdy""".split()
        S = {n: m.sem(n) for n in names}
        S["const_in"], in_landed = chunk["const_in"], chunk["landed"]
        hd = lambda ap: ap.rearrange("p (h d) -> p h d", d=SSD_DIM)
        b4 = lambda b: ps[:, b, :].rearrange("p (a t) -> p a t", a=4)

        TURNS = ((2, 3), (0, 1))
        behind_first = lambda n: not isinstance(n, int) or n > 0

        block = ctx.enter_context(nc.Block())

        @block.sync
        def _(sp):
            def body(n, par, prior):
                sp.wait_ge(S["p_cmem"], n + 1)
                sp.wait_ge(S["d_yb"], n + 1)
                sp.wait_ge(S["l_yz"], n + 1)
                load_chunk(sp, chunk, feat, tok, n + 2, par)

            over(sp, 0, TILES - 2, body)
            for i in (0, 1):
                load_out_weights(sp, w_ahead, w_out, i)

        @block.tensor
        def _(pe):
            pe.wait_ge(S["const_in"], 16 * 3)
            pe.transpose(ps[:, 7, 0:AB_OUT_T], row_in[:, :], ident[0:AB_OUT_T, 0:AB_OUT_T]).then_inc(S["cols_T"], 1)
            pe.matmul(ps[:, 6, 0:SSD_HEADS], tri[0:1, :], drow[:, :], start=True, stop=True).then_inc(S["drow_T"], 1)
            pe.wait_ge(S["cols_ok"], 1)
            pe.wait_ge(S["drow_ok"], 1)

            def decays(n, q):
                bank = 4 + q % 2
                if q >= 2:
                    pe.wait_ge(S["a_dec"], n * 4 + (q - 1))
                for k in range(4):
                    h = T_DA + 4 * q + k
                    pe.matmul(ps[:, bank, k * P:(k + 1) * P], g[:, h:h + 1].broadcast_to([P, P]), tri[:, :],
                              start=(k == 0), stop=False, skip_group_check=True)
                pe.matmul(ps[:, bank, :], ident_bf[:, :], mid(later[:, :], 4), start=False, stop=True,
                          skip_group_check=True).then_inc(S["p_acs"], 1)

            def weights(n, par, prior):
                pe.wait_ge(S["g_ok"], n + 1)
                pe.wait_ge(S["d_cmem"], n * 4)
                decays(n, 0)
                decays(n, 1)
                pe.wait_ge(in_landed[par], prior * 48 + 48)
                f = fe[par]
                pe.wait_ge(S["d_y"], n * 2)
                for k in range(8):
                    mm = pe.transpose(ps[:, k // 4, (k % 4) * P:(k % 4 + 1) * P], f[:, XS + k, :], ident[:, :])
                mm.then_inc(S["p_xT"], 1)
                pe.wait_ge(S["d_state"], n * 2)
                for k in range(2):
                    pe.transpose(ps[:, 3, k * P:(k + 1) * P], f[:, BT + k, :], ident[:, :])
                for k in range(2):
                    mm = pe.matmul(ps[:, 3, (2 + k) * P:(3 + k) * P], f[:, BT + k, :], f[:, CT + k, :], start=True, stop=True)
                mm.then_inc(S["p_bc"], 1)
                decays(n, 2)
                pe.wait_ge(S["mr_ok"], n + 1)
                for k in range(4):
                    mm = pe.matmul(ps[:, 7, k * P:(k + 1) * P], head_row[:, k, :], mr[:, 1, :], start=True, stop=True)
                mm.then_inc(S["p_wint"], 1)
                for k in range(4):
                    pe.matmul(ps[:, 6, k * P:(k + 1) * P], head_row[:, k, :], mr[:, 0, :],
                              start=(k == 0), stop=False, skip_group_check=True)
                pe.matmul(ps[:, 6, :], ident_bf[:, :], mid(later[:, :], 4), start=False, stop=True,
                          skip_group_check=True).then_inc(S["p_negm"], 1)
                decays(n, 3)
                for k in range(4):
                    mm = pe.transpose(ps[:, 2, k * P:(k + 1) * P], f[:, KTL + k, :], ident[:, :])
                mm.then_inc(S["p_kT"], 1)
                pe.wait_ge(S["a_dec"], n * 4 + 3)
                for k in range(4):
                    mm = pe.matmul(ps[:, 4, k * P:(k + 1) * P], f[:, KTL + k, :], f[:, QT + k, :], start=True, stop=True)
                mm.then_inc(S["p_qk"], 1)

            def turn(n, part):
                pe.wait_ge(S["d_yb"] if part == 0 else S["a_ynorm"], (n + 1) * (part + 1))
                for i, b in enumerate(TURNS[part]):
                    if part:
                        pe.wait_ge(S["d_yT"], n * 4 + (i + 1))
                    for k in range(4):
                        c = (4 * b + k) * P
                        mm = pe.transpose(ps[:, i, k * P:(k + 1) * P], y[:, c:c + P], ident[:, :])
                    mm.then_inc(S["p_yT"], 1)

            def outputs(n, par, prior):
                f = fe[par]
                pe.wait_ge(S["d_st"], n + 1)
                pe.wait_ge(S["d_qs"], n + 1)
                pe.wait_ge(S["d_cdec"], n + 1)
                pe.wait_ge(S["a_wm"], n + 1)
                pe.wait_ge(S["d_cmem"], n * 4)
                pe.wait_ge(S["a_dec"], n * 4 + 4)
                for h in range(ML_HEADS):
                    pe.matmul(ps[:, 4 + h, 0:VW], st[:, h, :], va[par][:, h, :], start=True, stop=False)
                    mm = pe.matmul(ps[:, 4 + h, 0:VW], qs[:, h, :], cmem[:, h, :], start=False, stop=True)
                    mm.then_inc(S["p_num"], 1)
                if behind_first(n):
                    turn(n - 1, 1)
                pe.wait_ge(S["d_kg"], n + 1)
                pe.wait_ge(S["d_btok"], n + 1)
                pe.wait_ge(S["d_wt"], n * 2 + 2)
                pe.wait_ge(S["d_state"], n * 2)
                for k in range(2):
                    mm = pe.matmul(ps[:, 2 + k, :], f[:, CT + k, :], state[:, k * 512:(k + 1) * 512], start=True, stop=True)
                    mm.then_inc(S["p_yoff"], 1)
                pe.wait_ge(S["l_xdt"], n + 1)
                pe.wait_ge(S["d_xtok"], n * 2 + 2)
                pe.wait_ge(S["d_yT"], n * 4)
                for h in range(SSD_HEADS):
                    mm = pe.matmul(ps[:, h // HG, (h % HG) * SSD_DIM:(h % HG + 1) * SSD_DIM], wt[:, h, :],
                                   xdt[:, h * SSD_DIM:(h + 1) * SSD_DIM], start=True, stop=True)
                    if h % HG == HG - 1:
                        mm.then_inc(S["p_ydiag"], 1)
                for h in range(ML_HEADS):
                    pe.wait_ge(S["d_h"], n * 4 + (h + 1))
                    mm = pe.matmul(ps[:, 4 + h, 0:VW], kg[:, h, :], va[par][:, h, :], start=True, stop=True)
                mm.then_inc(S["p_cmem"], 1)
                pe.wait_ge(S["l_xe"], n + 1)
                pe.wait_ge(S["d_t1"], n * 2 + 2)
                for k in range(2):
                    mm = pe.matmul(ps[:, 2 + k, :], b_tok[:, k, :], xe[:, k * 512:(k + 1) * 512], start=True, stop=True)
                mm.then_inc(S["p_state"], 1)

            weights(0, 0, 0)
            pe.wait_ge(S["zero_ok"], 2)
            pe.wait_ge(S["v_ones"], 2)

            def body(n, par, prior):
                outputs(n, par, prior)
                weights(n + 1, 1 - par, prior + par)
                pe.wait_ge(S["d_xtok"], n * 2 + 4)
                turn(n, 0)

            over(pe, 0, TILES - 1, body)
            outputs(TILES - 1, 1, (TILES - 1) // 2)
            pe.wait_ge(S["d_y"], 2 * TILES)
            turn(TILES - 1, 0)
            turn(TILES - 1, 1)

        @block.scalar
        def _(act):
            def decays(n, first):
                if first:
                    act.wait_ge(S["g_ok"], n + 1)
                    act.wait_ge(S["d_wt"], n * 2)
                    act.wait_ge(S["d_eend"], n + 0)
                    act.wait_ge(S["l_xe"], n + 0)
                for q in (0, 1) if first else (2, 3):
                    act.wait_ge(S["p_acs"], n * 4 + (q + 1))
                    for k in range(4):
                        h = 4 * q + k
                        a = nc.scalar.activation(dec[:, h, :], ps[:, 4 + q % 2, k * P:(k + 1) * P], ACT.Exp,
                                                 bias=g[:, T_NACS + h:T_NACS + h + 1])
                    a.then_inc(S["a_dec"], 1)

            def memory_weights(n):
                act.wait_ge(S["p_negm"], n + 1)
                act.wait_ge(S["d_st"], n + 0)
                act.wait_ge(S["d_gk"], n + 0)
                for k in range(ML_HEADS):
                    a = nc.scalar.activation(wm[:, k, :], ps[:, 6, k * P:(k + 1) * P], ACT.Exp,
                                             bias=g[:, T_U + k:T_U + k + 1])
                a.then_inc(S["a_wm"], 1)

            def memory_squares(n):
                act.wait_ge(S["d_h"], n * 4 + 4)
                act.wait_ge(S["d_meanm"], n + 0)
                act.wait_ge(S["a_sqy"], n * 2)
                for h in range(ML_HEADS):
                    act.wait_ge(S["a_sqm"], n * 4 + h)
                    nc.scalar.activation(x_sq[:, 0:ML_V], y[:, D + h * ML_V:D + (h + 1) * ML_V], ACT.Square,
                                         accum_out=ssq[:, 2 + h:3 + h]).then_inc(S["a_sqm"], 1)

            def ssd_squares(n):
                act.wait_ge(S["l_yz"], n + 1)
                act.wait_ge(S["a_sqm"], n * 4 + 4)
                act.wait_ge(S["d_meany"], n + 0)
                for k in (0, 1):
                    act.wait_ge(S["a_sqy"], n * 2 + k)
                    nc.scalar.activation(x_sq[:, :], y[:, k * 512:(k + 1) * 512], ACT.Square,
                                         accum_out=ssq[:, k:k + 1]).then_inc(S["a_sqy"], 1)

            def ssd_norm(n):
                act.wait_ge(S["l_rstdy"], n + 1)
                for k in (0, 1):
                    nc.scalar.activation(y[:, k * 512:(k + 1) * 512], y[:, k * 512:(k + 1) * 512], ACT.Copy,
                                         scale=rms[:, k:k + 1]).then_inc(S["a_ynorm"], 1)

            decays(0, True)
            decays(0, False)
            memory_weights(0)

            def body(n, par, prior):
                memory_squares(n)
                decays(n + 1, True)
                ssd_squares(n)
                decays(n + 1, False)
                memory_weights(n + 1)
                ssd_norm(n)

            over(act, 0, TILES - 1, body)
            memory_squares(TILES - 1)
            ssd_squares(TILES - 1)
            ssd_norm(TILES - 1)

        @block.gpsimd
        def _(gp):
            for v in va:
                gp.memset(v[:, :, ML_V:VW], 1.0).then_inc(S["v_ones"], 1)
            gp.memset(state[:, :], 0.0).then_inc(S["zero_ok"], 1)
            gp.memset(cmem[:, :, :], 0.0).then_inc(S["zero_ok"], 1)
            gp.wait_ge(S["zero_ok"], 2)
            gp.wait_ge(S["drow_ok"], 1)

            def body(n, par, prior):
                gp.wait_ge(S["d_xtok"], n * 2 + 2)
                gp.wait_ge(S["g_ok"], n + 1)
                gp.tensor_tensor(hd(xdt[:, :]), hd(x_tok[:, :]), last(g[:, T_DT:T_DT + SSD_HEADS], SSD_DIM),
                                 ALU.mult).then_inc(S["l_xdt"], 1)
                gp.wait_ge(S["l_xdt"], n + 1)
                gp.tensor_tensor(hd(x_tok[:, :]), hd(x_tok[:, :]), last(d_bc[:, :], SSD_DIM), ALU.mult).then_inc(S["l_xd"], 1)
                gp.wait_ge(S["a_dec"], n * 4 + 4)
                gp.tensor_tensor(hd(xe[:, :]), hd(xdt[:, :]),
                                 dec[:, :, P - 1:P].broadcast_to([P, SSD_HEADS, SSD_DIM]), ALU.mult).then_inc(S["l_xe"], 1)
                gp.wait_ge(S["p_yoff"], n * 2 + 2)
                gp.wait_ge(S["d_eend"], n + 1)
                gp.wait_ge(S["d_state"], n * 2)
                gp.tensor_tensor(hd(state[:, :]), hd(state[:, :]), last(e_end[:, :], SSD_DIM), ALU.mult).then_inc(S["l_sdec"], 1)
                gp.wait_ge(S["d_y"], n * 2 + 2)
                gp.wait_ge(S["l_xd"], n + 1)
                gp.tensor_tensor(y[:, 0:D], y[:, 0:D], x_tok[:, :], ALU.add).then_inc(S["l_yd"], 1)
                gp.wait_ge(S["d_meanm"], n + 1)
                gp.tensor_tensor(rms[:, 2:6], rms[:, 2:6], half[:, 0:4], ALU.pow).then_inc(S["l_rstdm"], 1)
                gp.wait_ge(S["l_yd"], n + 1)
                gp.wait_ge(in_landed[par], prior * 48 + 48)
                gp.tensor_tensor(y[:, 0:D], y[:, 0:D], gz[par][:, 0, :], ALU.mult).then_inc(S["l_yz"], 1)
                gp.wait_ge(S["d_meany"], n + 1)
                gp.tensor_tensor(rms[:, 0:2], rms[:, 0:2], half[:, 0:2], ALU.pow).then_inc(S["l_rstdy"], 1)

            over(gp, 0, TILES, body)

        @block.vector
        def _(dve):
            dve.wait_ge(S["cols_T"], 1)
            dve.tensor_copy(gcols[:, :], ps[:, 7, 0:AB_OUT_T]).then_inc(S["cols_ok"], 1)
            dve.wait_ge(S["drow_T"], 1)
            dve.tensor_copy(d_bc[:, :], ps[:, 6, 0:SSD_HEADS]).then_inc(S["drow_ok"], 1)

            def tables(n):
                dve.wait_ge(S["a_dec"], n * 4)
                dve.wait_ge(S["a_wm"], n + 0)
                dve.wait_ge(S["p_wint"], n + 0)
                dve.wait_ge(S["l_xdt"], n + 0)
                dve.tensor_scalar(g[:, :], table[:, bass.ds(n, 1), :].rearrange("p a k -> p (a k)"), 1.0, None,
                                  ALU.mult).then_inc(S["g_ok"], 1)
                dve.tensor_scalar(mr[:, :, :], maxrows[:, bass.ds(n, 1), :, :].rearrange("h a k t -> h (a k) t"),
                                  1.0, None, ALU.mult).then_inc(S["mr_ok"], 1)
                dve.wait_ge(S["g_ok"], n + 1)

            def weights(n, par, prior, means=lambda: None, turned=lambda: None):
                dve.wait_ge(S["p_xT"], n + 1)
                dve.wait_ge(S["l_yd"], n + 0)
                dve.wait_ge(S["l_xdt"], n + 0)
                for k in (0, 1):
                    dve.tensor_copy(x_tok[:, k * 512:(k + 1) * 512], ps[:, k, :]).then_inc(S["d_xtok"], 1)
                dve.wait_ge(S["p_bc"], n + 1)
                dve.tensor_copy(b_tok[:, :, :], ps[:, 3, 0:2 * P].rearrange("p (a t) -> p a t", a=2)).then_inc(S["d_btok"], 1)

                def ssd_weights(k):
                    dve.wait_ge(S["a_dec"], n * 4 + 2 * (k + 1))
                    dve.tensor_tensor(wt[:, HG * k:HG * (k + 1), :], dec[:, HG * k:HG * (k + 1), :],
                                      mid(ps[:, 3, (2 + k) * P:(3 + k) * P], HG), ALU.mult).then_inc(S["d_wt"], 1)

                ssd_weights(0)
                means()
                dve.wait_ge(S["p_wint"], n + 1)
                dve.wait_ge(in_landed[par], prior * 48 + 48)
                dve.tensor_tensor(qs[:, :, :], fe[par][:, QT:QT + 4, :], b4(7), ALU.mult).then_inc(S["d_qs"], 1)
                dve.wait_ge(S["d_cmem"], n * 4)
                dve.tensor_copy(c_dec[:, :], b4(7)[:, :, P - 1:P].rearrange("p h a -> p (h a)")).then_inc(S["d_cdec"], 1)
                dve.wait_ge(S["a_wm"], n + 1)
                dve.wait_ge(S["p_qk"], n + 1)
                dve.scalar_tensor_tensor(out=st[:, :, :], in0=b4(4), scalar=ML_QK ** -0.5, in1=wm[:, :, :],
                                         op0=ALU.mult, op1=ALU.mult).then_inc(S["d_st"], 1)
                dve.wait_ge(S["l_sdec"], n + 0)
                dve.wait_ge(S["a_dec"], n * 4 + 4)
                dve.tensor_tensor(e_end[:, :], dec[:, :, P - 1:P].rearrange("p h a -> p (h a)"),
                                  g[:, T_EACS:T_EACS + SSD_HEADS], ALU.mult).then_inc(S["d_eend"], 1)
                dve.tensor_scalar(gk[:, :], wm[:, :, P - 1:P].rearrange("p h a -> p (h a)"), ML_QK ** -0.5, None,
                                  ALU.mult).then_inc(S["d_gk"], 1)
                turned()
                ssd_weights(1)
                dve.wait_ge(S["d_gk"], n + 1)
                dve.wait_ge(S["p_kT"], n + 1)
                dve.tensor_tensor(kg[:, :, :], b4(2), last(gk[:, :], P), ALU.mult).then_inc(S["d_kg"], 1)

            def turn(n, part):
                for i, b in enumerate(TURNS[part]):
                    dve.wait_ge(S["p_yT"], n * 4 + (2 * part + i + 1))
                    dve.tensor_tensor(yT[:, bass.ds(n, 1), 4 * b:4 * b + 4, :].rearrange("p a k t -> p (a k) t"), b4(i),
                                      last(gcols[:, 4 * b:4 * b + 4], P), ALU.mult).then_inc(S["d_yT"], 1)

            def outputs(n, par, prior, next_tables=lambda: None):
                dve.wait_ge(S["p_num"], n * 4 + 4)
                dve.tensor_copy(den[:, :], ps[:, 4:8, ML_V:VW].rearrange("p h a -> p (h a)")).then_inc(S["d_den"], 1)
                dve.wait_ge(S["d_den"], n * 4 + 1)
                dve.scalar_tensor_tensor(out=den2[:, :], in0=den[:, :], scalar=-1.0, in1=den[:, :],
                                         op0=ALU.mult, op1=ALU.max).then_inc(S["d_den"], 1)
                dve.wait_ge(S["d_den"], n * 4 + 2)
                dve.tensor_tensor(den2[:, :], den2[:, :], g[:, T_EMT:T_EMT + ML_HEADS], ALU.max).then_inc(S["d_den"], 1)
                dve.wait_ge(S["d_den"], n * 4 + 3)
                dve.reciprocal(den[:, :], den2[:, :]).then_inc(S["d_den"], 1)
                dve.wait_ge(S["d_den"], n * 4 + 4)
                if behind_first(n):
                    turn(n - 1, 1)
                for h in range(ML_HEADS):
                    v = slice(h * ML_V, (h + 1) * ML_V)
                    dve.scalar_tensor_tensor(out=y[:, D + h * ML_V:D + (h + 1) * ML_V], in0=ps[:, 4 + h, 0:ML_V],
                                             scalar=den[:, h:h + 1], in1=gz[par][:, 2, v], op0=ALU.mult,
                                             op1=ALU.mult).then_inc(S["d_h"], 1)
                for k in (0, 1):
                    c = slice(k * 512, (k + 1) * 512)
                    dve.wait_ge(S["p_yoff"], n * 2 + (k + 1))
                    dve.tensor_tensor(hd(t1[:, c]), hd(ps[:, 2 + k, :]),
                                      last(g[:, T_EACS + HG * k:T_EACS + HG * (k + 1)], SSD_DIM), ALU.mult).then_inc(S["d_t1"], 1)
                for k in (0, 1):
                    c = slice(k * 512, (k + 1) * 512)
                    dve.wait_ge(S["p_ydiag"], n * 2 + (k + 1))
                    dve.wait_ge(S["d_t1"], n * 2 + (k + 1))
                    dve.tensor_tensor(y[:, c], ps[:, k, :], t1[:, c], ALU.add).then_inc(S["d_y"], 1)
                dve.wait_ge(S["a_sqm"], n * 4 + 4)
                dve.tensor_scalar(rms[:, 2:6], ssq[:, 2:6], 1.0 / ML_V, EPS, ALU.mult, ALU.add).then_inc(S["d_meanm"], 1)
                dve.wait_ge(S["p_cmem"], n + 1)
                for h in range(ML_HEADS):
                    dve.scalar_tensor_tensor(out=cmem[:, h, :], in0=cmem[:, h, :], scalar=c_dec[:, h:h + 1],
                                             in1=ps[:, 4 + h, 0:VW], op0=ALU.mult, op1=ALU.add).then_inc(S["d_cmem"], 1)
                next_tables()
                dve.wait_ge(S["p_state"], n + 1)
                dve.wait_ge(S["l_sdec"], n + 1)
                for k in (0, 1):
                    c = slice(k * 512, (k + 1) * 512)
                    dve.tensor_tensor(state[:, c], state[:, c], ps[:, 2 + k, :], ALU.add).then_inc(S["d_state"], 1)
                dve.wait_ge(S["l_rstdm"], n + 1)
                for h in range(ML_HEADS):
                    v = slice(h * ML_V, (h + 1) * ML_V)
                    yb = y[:, D + h * ML_V:D + (h + 1) * ML_V]
                    a = dve.scalar_tensor_tensor(out=yb, in0=yb, scalar=rms[:, 2 + h:3 + h], in1=gz[par][:, 1, v],
                                                 op0=ALU.mult, op1=ALU.mult)
                a.then_inc(S["d_yb"], 1)

            def ssd_means(n):
                dve.wait_ge(S["a_sqy"], n * 2 + 2)
                dve.tensor_scalar(rms[:, 0:2], ssq[:, 0:2], 1.0 / 512, EPS, ALU.mult, ALU.add).then_inc(S["d_meany"], 1)

            tables(0)
            weights(0, 0, 0)
            dve.wait_ge(S["zero_ok"], 2)

            def body(n, par, prior):
                outputs(n, par, prior, lambda: tables(n + 1))
                weights(n + 1, 1 - par, prior + par, lambda: ssd_means(n), lambda: turn(n, 0))

            over(dve, 0, TILES - 1, body)
            outputs(TILES - 1, 1, (TILES - 1) // 2)
            ssd_means(TILES - 1)
            turn(TILES - 1, 0)
            turn(TILES - 1, 1)


def out_projection(nc, tag, yT, x, w_out, w_ahead, x1):
    HALF = D // 2
    QT, Q = OUT_QT, AB_OUT_T // OUT_QT
    PIECES = 2 * Q
    with ExitStack() as ctx:
        ctx.enter_context(nc.cleanup_on_exit())
        m = Part(nc, ctx, tag)
        y_hi = [m.sb(f"y_hi{i}", [P, TILES, QT, P], F32R) for i in (0, 1)]
        y_lo = [m.sb(f"y_lo{i}", [P, TILES, QT, P], F32R) for i in (0, 1)]
        w_raw, w_landed = w_ahead["raw"], w_ahead["landed"]
        w_hi = [m.sb(f"w_hi{i}", [P, QT, HALF], F32R) for i in (0, 1)]
        w_lo = [m.sb(f"w_lo{i}", [P, QT, HALF], F32R) for i in (0, 1)]
        xr = m.sb("xr", [P, TILES, HALF])
        ps = m.ps("ps", [P, 8, 512])
        S = {n: m.sem(n) for n in "a_yhi a_whi d_ylo d_wlo p_part d_x1 x_landed x1_stored".split()}

        block = ctx.enter_context(nc.Block())

        @block.sync
        def _(sp):
            def load_w(i):
                sp.wait_ge(S["d_wlo"], i - 1)
                load_out_weights(sp, w_ahead, w_out, i)

            def load_x(j):
                sp.dma_start(xr[:, :, :], x[:, j * HALF:(j + 1) * HALF].rearrange("(t p) n -> p t n", p=P)
                             ).then_inc(S["x_landed"], 16)

            def store(j):
                for t in range(TILES):
                    sp.wait_ge(S["d_x1"], TILES * j + t + 1)
                    sp.dma_start(x1[t * P:(t + 1) * P, j * HALF:(j + 1) * HALF], xr[:, t, :]).then_inc(S["x1_stored"], 16)

            load_x(0)
            for i in range(2, Q + 2):
                load_w(i)
            store(0)
            for i in range(Q + 2, PIECES):
                load_w(i)
            sp.wait_ge(S["x1_stored"], 16 * TILES)
            load_x(1)
            store(1)
            sp.wait_ge(S["x1_stored"], 16 * 2 * TILES)

        half = lambda t, c: t[:, 4 * (c % 2):4 * (c % 2) + 4, :, :]
        whole = lambda c: yT[:, 4 * (c % 2):4 * (c % 2) + 4, QT * (c // 2 % Q):QT * (c // 2 % Q) + QT, :]

        @block.scalar
        def _(act):
            for i in range(PIECES):
                if i >= 2:
                    act.wait_ge(S["p_part"], TILES * (i - 1))
                for c in (2 * i, 2 * i + 1):
                    nc.scalar.copy(half(y_hi[i % 2], c), whole(c)).then_inc(S["a_yhi"], 1)
                    if c % 2 == 0:
                        act.wait_ge(w_landed[i % 2], 16 * (i // 2 + 1))
                        nc.scalar.copy(w_hi[i % 2][:, :, :], w_raw[i % 2][:, :, :]).then_inc(S["a_whi"], 1)

        @block.vector
        def _(dve):
            def residual(j):
                dve.wait_ge(S["x_landed"], 16 * (j + 1))
                for t in range(TILES):
                    dve.wait_ge(S["p_part"], TILES * (Q * (j + 1) - 1) + t + 1)
                    dve.tensor_tensor(xr[:, t, :], ps[:, t, :], xr[:, t, :], ALU.add).then_inc(S["d_x1"], 1)

            for i in range(PIECES):
                if i == Q + 1:
                    residual(0)
                for c in (2 * i, 2 * i + 1):
                    dve.wait_ge(S["a_yhi"], c + 1)
                    dve.tensor_tensor(half(y_lo[i % 2], c), whole(c), half(y_hi[i % 2], c).bitcast(F32),
                                      ALU.subtract).then_inc(S["d_ylo"], 1)
                    if c % 2 == 0:
                        dve.wait_ge(S["a_whi"], i + 1)
                        dve.tensor_tensor(w_lo[i % 2][:, :, :], w_raw[i % 2][:, :, :], w_hi[i % 2][:, :, :].bitcast(F32),
                                          ALU.subtract).then_inc(S["d_wlo"], 1)
            residual(1)

        @block.tensor
        def _(pe):
            for i in range(PIECES):
                j, q = divmod(i, Q)
                pe.wait_ge(S["d_wlo"], i + 1)
                wl, wh = w_lo[i % 2], w_hi[i % 2]
                for t in range(TILES):
                    if t % 4 == 0:
                        pe.wait_ge(S["d_ylo"], 2 * i + t // 4 + 1)
                    if j and q == 0:
                        pe.wait_ge(S["d_x1"], t + 1)
                    for k in range(QT):
                        h, l = y_hi[i % 2][:, t, k, :], y_lo[i % 2][:, t, k, :]
                        pe.matmul(ps[:, t, :], h, wh[:, k, :], start=(q == 0 and k == 0), stop=False)
                        pe.matmul(ps[:, t, :], h, wl[:, k, :], start=False, stop=False)
                        mm = pe.matmul(ps[:, t, :], l, wh[:, k, :], start=False, stop=(q == Q - 1 and k == QT - 1))
                    mm.then_inc(S["p_part"], 1)


NORMALISE, PROJECT = 3, 5
at_before = [sum(n // DA_HEADS // 4 + 1 for n in range(m)) for m in range(TILES * DA_HEADS + 1)]


def attention(nc, feat, tok, x1, lams, subln_g, w_out, final_g, out):
    LAMBDA_INIT = 0.8 - 0.6 * float(np.exp(-0.3))
    SCALE = DA_QK ** -0.5
    SLOPES = [2.0 ** (-8.0 * (h + 1) / DA_HEADS) for h in range(DA_HEADS)]
    H = DA_HEADS
    N = TILES * H
    with ExitStack() as ctx:
        ctx.enter_context(nc.cleanup_on_exit())
        m = Part(nc, ctx, "a")
        k_hl = m.sb("k_hl", [P, 2 * H, SEQ], F32R)
        v = m.sb("v", [P, TILES, D])
        wout = m.sb("wout", [P, KT, D])
        k_raw = m.sb("k_raw", [P, H, P])
        q_raw = m.sb("q_raw", [P, 2 * H, P])
        q_hi = [m.sb(f"q_hi{i}", [P, 2, P], F32R) for i in (0, 1)]
        q_lo = [m.sb(f"q_lo{i}", [P, 2, P], F32R) for i in (0, 1)]
        neg_dist = m.sb("neg_dist", [P, SEQ])
        z = m.sb("z", [P, D])
        xr = m.sb("xr", [P, D])
        s0 = [m.sb(f"s0{i}", [P, SEQ]) for i in (0, 1, 2)]
        s1 = [m.sb(f"s1{i}", [P, SEQ]) for i in (0, 1)]
        aT = [m.sb(f"aT{i}", [P, TILES, P]) for i in (0, 1)]
        y = [m.sb(f"y{i}", [P, D]) for i in (0, 1)]
        yT = m.sb("yT", [P, KT, P])
        res = m.sb("res", [P, D])
        final_bc = m.sb("final_bc", [P, D])
        ident = m.sb("ident", [P, P])
        lam_in = res[0:1, 0:4 * DA_QK].rearrange("p (a d) -> p a d", d=DA_QK)
        lam_w = res[0:1, 4 * DA_QK:6 * DA_QK].rearrange("p (a d) -> p a d", d=DA_QK)
        ones_row = res[0:1, 512:512 + P]
        g_row = res[0:1, 512 + P:512 + 2 * P]
        squares = [m.sb(f"squares{i}", [P, DA_V], BF16) for i in (0, 1)]
        lam2 = m.sb("lam2", [1, 4])
        neg_lam = m.sb("neg_lam", [P, 1])
        g_col = m.sb("g_col", [P, 1])
        half = m.sb("half", [P, H])
        mx = [m.sb(f"mx{i}", [P, 2]) for i in (0, 1)]
        nm = [m.sb(f"nm{i}", [P, 2]) for i in (0, 1)]
        sm = [m.sb(f"sm{i}", [P, 2]) for i in (0, 1)]
        rc = [m.sb(f"rc{i}", [P, 2]) for i in (0, 1)]
        coef = [m.sb(f"coef{i}", [P, 1]) for i in (0, 1)]
        r0 = [m.sb(f"r0{i}", [P, H]) for i in (0, 1)]
        rs = [m.sb(f"rs{i}", [P, H]) for i in (0, 1)]
        fs = m.sb("fs", [P, 1])
        fss = m.sb("fss", [P, 1])
        ps = m.ps("ps", [P, 8, 512])

        names = """const_in pool_ok iota_ok dist_ok lam_mul lam_sum lam_exp lam_ok
                   p_const c_ok p_s0 p_s1 p_at p_o p_yT p_out
                   d_t d_nm d_rc d_coef d_r0 d_a d_o d_mean d_yT d_x2 d_fmean d_res d_qlo
                   a_khi a_qhi a_p a_at a_ss a_fss l_klo l_rstd l_yn l_yz l_frstd
                   k_landed v_landed q0_landed q1_landed z_landed x_landed""".split()
        S = {n: m.sem(n) for n in names}
        out_stored = m.sem("out_stored")
        wout_in = [m.sem(f"wout_in{i}") for i in range(4)]
        score = [ps[:, 2 * j:2 * j + 2, :].rearrange("p b n -> p (b n)") for j in (0, 1)]
        b4 = lambda b: ps[:, b, :].rearrange("p (a t) -> p a t", a=4)
        hv = lambda ap: ap.rearrange("p (h v) -> p h v", v=DA_V)
        F = DA_QK

        block = ctx.enter_context(nc.Block())

        KEYS_AT = (2, 5)

        PRODUCTS = {2: (0, 0, 3), 3: (0, 3, 6), 4: (0, 6, 8), 5: (1, 0, 3), 6: (1, 3, 6), 7: (1, 6, 8)}
        PIECES = 8
        bank_of = lambda t, piece: 7 if t < TILES - 1 else (4, 5, 6, 6, 6, 7, 7, 7)[piece]

        def piece_of(n):
            t, k = divmod(n - PROJECT - H, H)
            return (t, k) if 0 <= t < TILES - 1 else (None, None)

        @block.sync
        def _(sp):
            def half_keys(c):
                t, u = c // 2, c % 2
                if c:
                    sp.wait_ge(S["l_klo"], c)
                src = feat[2 * H + H * u:2 * H + H * (u + 1), :, t * P:(t + 1) * P].rearrange("f d t -> d f t")
                for r in (slice(0, F), slice(F, P)):
                    sp.dma_start(k_raw[r, :, :], src).then_inc(S["k_landed"], 16)

            def queries(t, u):
                if t:
                    sp.wait_ge(S["d_qlo"], H * (t - 1) + 4 * u + 4)
                src = feat[H * u:H * (u + 1), :, t * P:(t + 1) * P].rearrange("f d t -> d f t")
                for r in (slice(0, F), slice(F, P)):
                    sp.dma_start(q_raw[r, H * u:H * (u + 1), :], src).then_inc(S[f"q{u}_landed"], 16)

            def values_in(t):
                if t:
                    sp.wait_ge(S["v_landed"], 16 * t)
                sp.dma_start(v[:, t, :], tok[t * P:(t + 1) * P, 0:D]).then_inc(S["v_landed"], 16)

            def gate(t):
                if t:
                    sp.wait_ge(S["l_yz"], t)
                sp.dma_start(z[:, :], tok[t * P:(t + 1) * P, D:2 * D]).then_inc(S["z_landed"], 16)

            def residual_in(t):
                if t:
                    sp.wait_ge(S["d_res"], t)
                sp.dma_start(xr[:, :], x1[t * P:(t + 1) * P, :]).then_inc(S["x_landed"], 16)

            def weights_in(part):
                rows = slice(part * 2 * P, (part + 1) * 2 * P)
                sp.dma_start(wout[:, 2 * part:2 * part + 2, :], w_out[rows, :].rearrange("(k p) n -> p k n", p=P)
                             ).then_inc(wout_in[part], 16)

            queries(0, 0)
            half_keys(0)
            for i, r in enumerate(lams):
                sp.dma_start(lam_in[:, i, :], r).then_inc(S["const_in"], 16)
            sp.dma_start(g_row, subln_g).then_inc(S["const_in"], 16)
            sp.dma_start(final_bc[0:1, :], final_g).then_inc(S["const_in"], 16)
            half_keys(1)
            values_in(0)
            queries(0, 1)
            for t in range(TILES):
                if t + 1 < TILES:
                    half_keys(2 * t + 2)
                    queries(t + 1, 0)
                    values_in(t + 1)
                    half_keys(2 * t + 3)
                if t < 2:
                    weights_in(2 * t)
                gate(t)
                if t == 0:
                    residual_in(0)
                if t + 1 < TILES:
                    queries(t + 1, 1)
                if t >= 2:
                    residual_in(t - 1)
                    sp.dma_start(out[(t - 2) * P:(t - 1) * P, :], res[:, :]).then_inc(out_stored, 16)
                if t < 2:
                    weights_in(2 * t + 1)
            residual_in(TILES - 1)
            sp.dma_start(out[SEQ - 2 * P:SEQ - P, :], res[:, :]).then_inc(out_stored, 16)
            sp.wait_ge(S["d_res"], TILES)
            sp.dma_start(out[SEQ - P:SEQ, :], res[:, :]).then_inc(out_stored, 16)
            sp.wait_ge(out_stored, 16 * TILES)

        @block.gpsimd
        def _(gp):
            gp.memset(ident[:, :], 0.0).then_inc(S["pool_ok"], 1)
            gp.memset(ones_row, 1.0).then_inc(S["pool_ok"], 1)
            gp.memset(half[:, :], -0.5).then_inc(S["pool_ok"], 1)
            gp.wait_ge(S["pool_ok"], 3)
            gp.affine_select(out=ident[:, :], in_=ident[:, :], compare_op=ALU.not_equal, fill=1.0, base=0,
                             pattern=[[-1, P]], channel_multiplier=1).then_inc(S["pool_ok"], 1)
            gp.iota(neg_dist[:, :], pattern=[[-1, SEQ]], base=SEQ - P, channel_multiplier=1,
                    allow_small_or_imprecise_dtypes=True).then_inc(S["iota_ok"], 1)
            gp.wait_ge(S["dist_ok"], 1)
            gp.affine_select(out=neg_dist[:, SEQ - 64:SEQ], in_=neg_dist[:, SEQ - 64:SEQ], compare_op=ALU.is_ge,
                             fill=MASKED, base=-64, pattern=[[0, 64]], channel_multiplier=1).then_inc(S["iota_ok"], 1)
            gp.wait_ge(S["iota_ok"], 2)

            def low_keys(c):
                t, u = c // 2, c % 2
                part = k_hl[F:P, H * u:H * (u + 1), t * P:(t + 1) * P]
                gp.wait_ge(S["a_khi"], c + 1)
                gp.tensor_tensor(part, k_raw[F:P, :, :], part.bitcast(F32), ALU.subtract).then_inc(S["l_klo"], 1)
                gp.wait_ge(S["l_klo"], c + 1)

            low_keys(0)
            low_keys(1)
            for n in range(N + H):
                t, h = n // H, n % H
                if t + 1 < TILES and h in KEYS_AT:
                    if h == KEYS_AT[0] and t >= 3:
                        gp.wait_ge(S["l_frstd"], t - 2)
                    if h == KEYS_AT[1] and t:
                        gp.wait_ge(S["l_yz"], t)
                    low_keys(2 * (t + 1) + KEYS_AT.index(h))
                if t and h == NORMALISE:
                    b = (t - 1) % 2
                    gp.wait_ge(S["d_mean"], t)
                    gp.tensor_tensor(rs[b][:, :], rs[b][:, :], half[:, :], ALU.pow).then_inc(S["l_rstd"], 1)
                    if t == TILES:
                        continue
                    gp.wait_ge(S["l_rstd"], t)
                    gp.tensor_tensor(hv(y[b][:, :]), hv(y[b][:, :]), last(rs[b][:, :], DA_V), ALU.mult).then_inc(S["l_yn"], 1)
                    gp.wait_ge(S["l_yn"], t)
                    gp.wait_ge(S["z_landed"], 16 * t)
                    gp.tensor_tensor(y[b][:, :], y[b][:, :], z[:, :], ALU.mult).then_inc(S["l_yz"], 1)
                if t >= 2 and h == (PROJECT + PIECES + 2) % H:
                    gp.wait_ge(S["d_fmean"], t - 1)
                    gp.tensor_tensor(fs[:, :], fs[:, :], half[:, 0:1], ALU.pow).then_inc(S["l_frstd"], 1)
            gp.wait_ge(S["d_fmean"], TILES)
            gp.tensor_tensor(fs[:, :], fs[:, :], half[:, 0:1], ALU.pow).then_inc(S["l_frstd"], 1)

        @block.tensor
        def _(pe):
            def scores(n):
                t, h = n // H, n % H
                W = (t + 1) * P
                pe.wait_ge(S["d_qlo"], n + 1)
                if h % 4 == 0:
                    pe.wait_ge(S["l_klo"], 2 * t + h // 4 + 1)
                for j in (0, 1):
                    if n:
                        pe.wait_ge(S["d_t"], 2 * n - 1 + j)
                    for c in range(0, W, 512):
                        w = min(512, W - c)
                        o, k = ps[:, 2 * j + c // 512, 0:w], k_hl[:, 2 * h + j, c:c + w]
                        pe.matmul(o, q_hi[n % 2][:, j, :], k, start=True, stop=False)
                        mm = pe.matmul(o, q_lo[n % 2][:, j, :], k, start=False, stop=True)
                    mm.then_inc(S["p_s0" if j == 0 else "p_s1"], 1)

            def turn(n):
                t, h = n // H, n % H
                pe.wait_ge(S["d_a"], n + 1)
                pe.wait_ge(S["a_at"], at_before[n])
                if n == 0:
                    pe.wait_ge(S["c_ok"], 3)
                for k in range(t + 1):
                    mm = pe.transpose(ps[:, 4 + k // 4, (k % 4) * P:(k % 4 + 1) * P], s0[n % 3][:, k * P:(k + 1) * P],
                                      ident[:, :])
                    if k == 3 or k == t:
                        mm.then_inc(S["p_at"], 1)

            def values(n):
                t, h = n // H, n % H
                pe.wait_ge(S["a_at"], at_before[n + 1])
                if h == 0:
                    pe.wait_ge(S["v_landed"], 16 * (t + 1))
                if n:
                    pe.wait_ge(S["d_o"], n)
                for k in range(t + 1):
                    mm = pe.matmul(ps[:, 6, 0:DA_V], aT[n % 2][:, k, :],
                                   v[:, k, h * DA_V:(h + 1) * DA_V], start=(k == 0), stop=(k == t))
                mm.then_inc(S["p_o"], 1)

            def project(t, piece):
                bank = bank_of(t, piece)
                if piece < 2:
                    if piece == 0:
                        pe.wait_ge(S["l_yz"], t + 1)
                        if t < TILES - 1:
                            pe.wait_ge(S["d_x2"], 2 * t)
                        else:
                            pe.wait_ge(S["a_at"], at_before[N])
                    elif t < TILES - 1:
                        pe.wait_ge(S["d_yT"], 2 * t + 1)
                    for k in range(4):
                        c = (4 * piece + k) * P
                        mm = pe.transpose(ps[:, bank, k * P:(k + 1) * P], y[t % 2][:, c:c + P], ident[:, :])
                    mm.then_inc(S["p_yT"], 1)
                    return
                j, first, end = PRODUCTS[piece]
                if first == 0 and j == 0:
                    if t == TILES - 1:
                        pe.wait_ge(S["d_o"], N)
                    pe.wait_ge(S["d_yT"], 2 * t + 2)
                if first == 0 and j == 1:
                    pe.wait_ge(S["d_x2"], 2 * t + (1 if t < TILES - 1 else 0))
                for k in range(first, end):
                    if t == 0 and j == 0 and k % 2 == 0:
                        pe.wait_ge(wout_in[k // 2], 16)
                    mm = pe.matmul(ps[:, bank, :], yT[:, k, :], wout[:, k, j * 512:(j + 1) * 512],
                                   start=(k == 0), stop=(k == KT - 1))
                if end == KT:
                    mm.then_inc(S["p_out"], 1)

            scores(0)
            scores(1)
            pe.wait_ge(S["lam_ok"], 1)
            pe.wait_ge(S["const_in"], 16 * 6)
            pe.wait_ge(S["pool_ok"], 4)
            pe.matmul(ps[:, 7, 0:1], ones_row, lam2[:, 2:3], start=True, stop=True)
            pe.matmul(ps[:, 7, 1:2], g_row, ones_row[:, 0:1], start=True, stop=True)
            for j in (0, 1):
                mm = pe.matmul(ps[:, 4 + j, :], ones_row, final_bc[0:1, j * 512:(j + 1) * 512], start=True, stop=True)
            mm.then_inc(S["p_const"], 1)
            for n in range(N + 2):
                if n and n + 1 < N:
                    scores(n + 1)
                if 0 <= n - 1 < N:
                    turn(n - 1)
                if 0 <= n - 2:
                    values(n - 2)
                tile, piece = piece_of(n)
                if piece is not None:
                    project(tile, piece)
            for n in range(N + 2, N + PROJECT + PIECES - H):
                tile, piece = piece_of(n)
                if piece is not None:
                    project(tile, piece)
            for piece in range(PIECES):
                project(TILES - 1, piece)

        @block.scalar
        def _(act):
            def high_keys(c):
                t, u = c // 2, c % 2
                act.wait_ge(S["k_landed"], 32 * (c + 1))
                nc.scalar.copy(k_hl[:, H * u:H * (u + 1), t * P:(t + 1) * P], k_raw[:, :, :]).then_inc(S["a_khi"], 1)

            def high_queries(n):
                t, h = n // H, n % H
                if h % 4 == 0:
                    act.wait_ge(S[f"q{h // 4}_landed"], 32 * (t + 1))
                if n >= 2:
                    act.wait_ge(S["p_s1"], n - 1)
                    act.wait_ge(S["d_qlo"], n - 1)
                nc.scalar.activation(q_hi[n % 2][:, :, :], q_raw[:, 2 * h:2 * h + 2, :], ACT.Copy,
                                     scale=SCALE / SLOPES[h]).then_inc(S["a_qhi"], 1)

            high_keys(0)
            high_queries(0)
            high_queries(1)

            def softmax(n):
                t, h = n // H, n % H
                W = (t + 1) * P
                act.wait_ge(S["d_nm"], n + 1)
                if n >= 2:
                    act.wait_ge(S["d_coef"], n - 1)
                for j, s in ((0, s0[n % 3]), (1, s1[n % 2])):
                    nc.scalar.activation(s[:, 0:W], s[:, 0:W], ACT.Exp, bias=nm[n % 2][:, j:j + 1],
                                         scale=SLOPES[h], accum_out=sm[n % 2][:, j:j + 1]).then_inc(S["a_p"], 1)

            def evict(n):
                t = n // H
                if n >= 2:
                    act.wait_ge(S["p_o"], n - 1)
                for b in range(t // 4 + 1):
                    w = min(4, t + 1 - 4 * b)
                    act.wait_ge(S["p_at"], at_before[n] + b + 1)
                    nc.scalar.copy(aT[n % 2][:, 4 * b:4 * b + w, :], b4(4 + b)[:, 0:w, :]).then_inc(S["a_at"], 1)

            def head_square(n):
                t, h = n // H, n % H
                act.wait_ge(S["d_o"], n + 1)
                if n >= 2:
                    act.wait_ge(S["a_ss"], n - 1)
                if h == 0 and t >= 2:
                    act.wait_ge(S["l_yn"], t - 1)
                nc.scalar.activation(squares[n % 2][:, :], y[t % 2][:, h * DA_V:(h + 1) * DA_V], ACT.Square,
                                     accum_out=rs[t % 2][:, h:h + 1]).then_inc(S["a_ss"], 1)

            def final_squares(t):
                act.wait_ge(S["d_x2"], 2 * t + 2)
                act.wait_ge(out_stored, 16 * t)
                if t:
                    act.wait_ge(S["d_fmean"], t)
                nc.scalar.activation(res[:, :], xr[:, :], ACT.Square, accum_out=fss[:, :]).then_inc(S["a_fss"], 1)

            softmax(0)
            act.wait_ge(S["lam_sum"], 2)
            nc.scalar.activation(lam2[:, 0:2], lam2[:, 0:2], ACT.Exp).then_inc(S["lam_exp"], 1)
            high_keys(1)
            for n in range(N + 3):
                t, h = n // H, n % H
                if n + 2 < N:
                    high_queries(n + 2)
                if n >= 3:
                    head_square(n - 3)
                if n + 1 < N:
                    softmax(n + 1)
                if 0 <= n - 1 < N:
                    evict(n - 1)
                if t + 1 < TILES and h in KEYS_AT:
                    high_keys(2 * (t + 1) + KEYS_AT.index(h))
                if t >= 2 and h == (PROJECT + PIECES + 1) % H:
                    final_squares(t - 2)
            final_squares(TILES - 2)
            final_squares(TILES - 1)

        @block.vector
        def _(dve):
            dve.wait_ge(S["iota_ok"], 1)
            dve.scalar_tensor_tensor(out=neg_dist[:, :], in0=neg_dist[:, :], scalar=-1.0, in1=neg_dist[:, :], op0=ALU.mult,
                                     op1=ALU.min).then_inc(S["dist_ok"], 1)
            dve.wait_ge(S["iota_ok"], 2)
            def maxima(n):
                h = n % H
                W = (n // H + 1) * P
                if n >= 2:
                    dve.wait_ge(S["d_a"], n - 1)
                if n >= 3:
                    dve.wait_ge(S["p_at"], at_before[n - 2])
                for j, s in ((0, s0[n % 3]), (1, s1[n % 2])):
                    dve.wait_ge(S["p_s0" if j == 0 else "p_s1"], n + 1)
                    dve.tensor_tensor_reduce(s[:, 0:W], score[j][:, 0:W], neg_dist[:, SEQ - W:SEQ], 1.0, -3e38,
                                             ALU.add, ALU.max, mx[n % 2][:, j:j + 1]).then_inc(S["d_t"], 1)
                dve.wait_ge(S["d_t"], 2 * n + 2)
                dve.tensor_scalar(nm[n % 2][:, :], mx[n % 2][:, :], -SLOPES[h], None, ALU.mult).then_inc(S["d_nm"], 1)

            def combine(n):
                t, h = n // H, n % H
                W = (t + 1) * P
                b = n % 2
                dve.wait_ge(S["a_p"], 2 * n + 2)
                dve.reciprocal(rc[b][:, :], sm[b][:, :]).then_inc(S["d_rc"], 1)
                dve.wait_ge(S["d_rc"], n + 1)
                dve.scalar_tensor_tensor(out=coef[b][:, :], in0=sm[b][:, 0:1], scalar=neg_lam[:, 0:1],
                                         in1=rc[b][:, 1:2], op0=ALU.mult, op1=ALU.mult).then_inc(S["d_coef"], 1)
                dve.tensor_copy(r0[t % 2][:, h:h + 1], rc[b][:, 0:1]).then_inc(S["d_r0"], 1)
                dve.wait_ge(S["d_coef"], n + 1)
                dve.scalar_tensor_tensor(out=s0[n % 3][:, 0:W], in0=s1[b][:, 0:W], scalar=coef[b][:, 0:1],
                                         in1=s0[n % 3][:, 0:W], op0=ALU.mult, op1=ALU.add).then_inc(S["d_a"], 1)

            def over_sum(n):
                t, h = n // H, n % H
                dve.wait_ge(S["p_o"], n + 1)
                if h == 0 and t >= 2:
                    dve.wait_ge(S["p_yT"], 2 * (t - 1))
                dve.tensor_scalar(y[t % 2][:, h * DA_V:(h + 1) * DA_V], ps[:, 6, 0:DA_V],
                                  r0[t % 2][:, h:h + 1], None, ALU.mult).then_inc(S["d_o"], 1)

            def low_queries(n):
                h = n % H
                dve.wait_ge(S["a_qhi"], n + 1)
                dve.scalar_tensor_tensor(out=q_lo[n % 2][:, :, :], in0=q_raw[:, 2 * h:2 * h + 2, :],
                                         scalar=SCALE / SLOPES[h], in1=q_hi[n % 2][:, :, :].bitcast(F32),
                                         op0=ALU.mult, op1=ALU.subtract).then_inc(S["d_qlo"], 1)

            def head_means(t):
                dve.wait_ge(S["a_ss"], H * (t + 1))
                dve.tensor_scalar(rs[t % 2][:, :], rs[t % 2][:, :], 1.0 / DA_V, EPS, ALU.mult, ALU.add).then_inc(S["d_mean"], 1)

            def norm_gate_last():
                b = (TILES - 1) % 2
                dve.wait_ge(S["l_rstd"], TILES)
                dve.tensor_tensor(hv(y[b][:, :]), hv(y[b][:, :]), last(rs[b][:, :], DA_V), ALU.mult).then_inc(S["l_yn"], 1)
                dve.wait_ge(S["l_yn"], TILES)
                dve.wait_ge(S["z_landed"], 16 * TILES)
                dve.tensor_tensor(y[b][:, :], y[b][:, :], z[:, :], ALU.mult).then_inc(S["l_yz"], 1)

            def piece_out(t, piece):
                if piece < 2:
                    dve.wait_ge(S["p_yT"], 2 * t + piece + 1)
                    dve.tensor_scalar(yT[:, 4 * piece:4 * piece + 4, :], b4(bank_of(t, piece)), g_col[:, 0:1], None,
                                      ALU.mult).then_inc(S["d_yT"], 1)
                elif PRODUCTS[piece][2] == KT:
                    j = PRODUCTS[piece][0]
                    c = slice(j * 512, (j + 1) * 512)
                    dve.wait_ge(S["x_landed"], 16 * (t + 1))
                    dve.wait_ge(S["p_out"], 2 * t + j + 1)
                    dve.tensor_tensor(xr[:, c], ps[:, bank_of(t, piece), :], xr[:, c], ALU.add).then_inc(S["d_x2"], 1)

            def final(t):
                dve.wait_ge(S["a_fss"], t + 1)
                dve.tensor_scalar(fs[:, :], fss[:, :], 1.0 / D, EPS, ALU.mult, ALU.add).then_inc(S["d_fmean"], 1)
                dve.wait_ge(S["l_frstd"], t + 1)
                dve.scalar_tensor_tensor(out=res[:, :], in0=xr[:, :], scalar=fs[:, 0:1], in1=final_bc[:, :],
                                         op0=ALU.mult, op1=ALU.mult).then_inc(S["d_res"], 1)

            low_queries(0)
            low_queries(1)
            maxima(0)
            dve.wait_ge(S["const_in"], 16 * 6)
            for i in (0, 1):
                dve.tensor_tensor_reduce(lam_w[:, i, :], lam_in[:, 2 * i, :], lam_in[:, 2 * i + 1, :], 1.0, 0.0,
                                         ALU.mult, ALU.add, lam2[:, i:i + 1]).then_inc(S["lam_sum"], 1)
            dve.wait_ge(S["lam_exp"], 1)
            dve.tensor_tensor(lam2[:, 3:4], lam2[:, 1:2], lam2[:, 0:1], ALU.subtract).then_inc(S["lam_mul"], 1)
            dve.wait_ge(S["lam_mul"], 1)
            dve.tensor_scalar(lam2[:, 2:3], lam2[:, 3:4], -LAMBDA_INIT, None, ALU.add).then_inc(S["lam_ok"], 1)
            dve.wait_ge(S["p_const"], 1)
            dve.tensor_copy(neg_lam[:, :], ps[:, 7, 0:1]).then_inc(S["c_ok"], 1)
            dve.tensor_scalar(g_col[:, :], ps[:, 7, 1:2], 1.0 - LAMBDA_INIT, None, ALU.mult).then_inc(S["c_ok"], 1)
            dve.tensor_copy(final_bc[:, :], ps[:, 4:6, :].rearrange("p b n -> p (b n)")).then_inc(S["c_ok"], 1)
            dve.wait_ge(S["c_ok"], 3)
            for n in range(N + 4):
                t, h = n // H, n % H
                if 0 <= n - 3 < N:
                    over_sum(n - 3)
                if n == N + NORMALISE:
                    head_means(TILES - 1)
                tile, piece = piece_of(n - 1)
                if piece is not None:
                    piece_out(tile, piece)
                if n + 1 < N:
                    maxima(n + 1)
                if t and h == NORMALISE and n < N:
                    head_means(t - 1)
                if n + 2 < N:
                    low_queries(n + 2)
                if n < N:
                    combine(n)
                if t >= 2 and h == (PROJECT + PIECES + 2) % H:
                    final(t - 2)
            norm_gate_last()
            for n in range(N + 4, N + PROJECT + PIECES - H + 1):
                tile, piece = piece_of(n - 1)
                if piece is not None:
                    piece_out(tile, piece)
            piece_out(TILES - 1, 0)
            piece_out(TILES - 1, 1)
            final(TILES - 2)
            for piece in range(2, PIECES):
                piece_out(TILES - 1, piece)
            final(TILES - 1)


def hybrid(nc, x, ab_norm_g, ab_w_in, ab_ssd_conv_w, ab_ssd_conv_b, ab_dt_bias, ab_a_log, ab_d_skip, ab_ssd_norm_g,
           ab_ml_conv_w, ab_ml_conv_b, ab_i_bias, ab_f_bias, ab_ml_norm_g, ab_w_out, c_norm_g, c_w_in, c_lam_q1,
           c_lam_k1, c_lam_q2, c_lam_k2, c_subln_g, c_w_out, final_norm_g, out):
    def scratch(name, shape):
        return nc.dram_tensor(name, shape, F32, kind="Internal").ap()

    def rows(v):
        return v.rearrange("a (r c) -> (a r) c", c=P)

    feat0 = scratch("feat0", [FEAT_T, P, SEQ])
    tok0 = scratch("tok0", [SEQ, 4 * D])
    gates = scratch("gates", [GATES, SEQ])
    x1 = scratch("x1", [SEQ, D])
    feat1 = scratch("feat1", [4 * DA_HEADS, DA_QK, SEQ])
    tok1 = scratch("tok1", [SEQ, 2 * D])
    x_in = x[0]
    taps = [r for j in range(CONV) for r in (rows(ab_ssd_conv_w[0, j:j + 1, :]), rows(ab_ml_conv_w[0, j:j + 1, :]))]

    projection(nc, "p", x_in, ab_w_in[0], [rows(ab_norm_g)] + taps + [rows(ab_ssd_conv_b), rows(ab_ml_conv_b)],
               [C_XBC, C_XBC + BLK, C_XBC + 2 * BLK, C_Q, C_K], feat0,
               [(C_ZA, ACT.Silu), (C_ZA + BLK, ACT.Silu), (C_ZB, ACT.Silu), (C_ZB + BLK, ACT.Silu),
                (C_OG, ACT.Sigmoid), (C_OG + BLK, ACT.Sigmoid), (C_V, ACT.Copy), (C_V + BLK, ACT.Copy)],
               tok0, conv=True, gate_out=gates)
    with ExitStack() as outer:
        outer.enter_context(nc.cleanup_on_exit())
        o = Part(nc, outer, "y")
        yT = o.sb("yT", [P, TILES, AB_OUT_T, P])
        w_ahead = dict(raw=[o.sb(f"w_raw{i}", [P, OUT_QT, D // 2]) for i in (0, 1)],
                       landed=[o.sem(f"w_landed{i}") for i in (0, 1)])
        with ExitStack() as ctx:
            ctx.enter_context(nc.cleanup_on_exit())
            m = Part(nc, ctx, "k")
            keep = dict(table=m.sb("table", [P, TILES, T_ALL]), maxrows=m.sb("maxrows", [ML_HEADS, TILES, 2, P]),
                        ident=m.sb("ident", [P, P]), ident_bf=m.sb("ident_bf", [P, P], BF16), tri=m.sb("tri", [P, P]),
                        later=m.sb("later", [P, P], BF16), head_row=m.sb("head_row", [ML_HEADS, ML_HEADS, P]),
                        half=m.sb("half", [P, ML_HEADS]))
            chunk = dict(fe=[m.sb(f"fe{i}", [P, FEAT_T, P]) for i in (0, 1)],
                         gz=[m.sb(f"gz{i}", [P, 3, D]) for i in (0, 1)],
                         va=[m.sb(f"va{i}", [P, ML_HEADS, ML_V + 1]) for i in (0, 1)],
                         drow=m.sb("drow", [1, SSD_HEADS]), row_in=m.sb("row_in", [AB_OUT_T, P]),
                         landed=[m.sem(f"in_landed{i}") for i in (0, 1)], const_in=m.sem("const_in"))

            def load_consts(sp):
                sp.dma_start(chunk["drow"][:, :], ab_d_skip).then_inc(chunk["const_in"], 16)
                half_rows = AB_OUT_T // 2
                for i, g in enumerate((ab_ssd_norm_g, ab_ml_norm_g)):
                    sp.dma_start(chunk["row_in"][i * half_rows:(i + 1) * half_rows, :], rows(g)
                                 ).then_inc(chunk["const_in"], 16)

            scan_gates(nc, keep, gates, ab_dt_bias, ab_a_log, ab_i_bias, ab_f_bias, feat0, tok0, chunk, load_consts)
            scan_chunks(nc, keep, yT, feat0, tok0, chunk, ab_w_out[0], w_ahead)
        out_projection(nc, "o", yT, x_in, ab_w_out[0], w_ahead, x1)
    projection(nc, "q", x1, c_w_in[0], [rows(c_norm_g)], [0, BLK, D, D + BLK], feat1.rearrange("(n j) d t -> n (j d) t", j=2),
               [(2 * D, ACT.Copy), (2 * D + BLK, ACT.Copy), (3 * D, ACT.Silu), (3 * D + BLK, ACT.Silu)], tok1)
    attention(nc, feat1, tok1, x1, [c_lam_q1, c_lam_k1, c_lam_q2, c_lam_k2], c_subln_g, c_w_out[0],
              final_norm_g.rearrange("(a n) -> a n", a=1), out[0])


_INS = ['x', 'ab_norm_g', 'ab_w_in', 'ab_ssd_conv_w', 'ab_ssd_conv_b', 'ab_dt_bias', 'ab_a_log', 'ab_d_skip',
        'ab_ssd_norm_g', 'ab_ml_conv_w', 'ab_ml_conv_b', 'ab_i_bias', 'ab_f_bias', 'ab_ml_norm_g', 'ab_w_out',
        'c_norm_g', 'c_w_in', 'c_lam_q1', 'c_lam_k1', 'c_lam_q2', 'c_lam_k2', 'c_subln_g', 'c_w_out',
        'final_norm_g']


def kernel(**inputs):
    import concourse.bacc as bacc
    from concourse.bass_utils import run_bass_kernel_spmd

    nc = bacc.Bacc("TRN2", target_bir_lowering=False, num_devices=1)
    arrays, args = {}, []
    for name in _INS:
        a = np.ascontiguousarray(inputs[name])
        arrays[f"in_{name}"] = a
        args.append(nc.dram_tensor(f"in_{name}", a.shape, mybir.dt.from_np(a.dtype), kind="ExternalInput").ap())
    args.append(nc.dram_tensor("out_0", (1, SEQ, D), F32, kind="ExternalOutput").ap())
    hybrid(nc, *args)
    r = run_bass_kernel_spmd(nc, [arrays], core_ids=[0])
    return r.results[0]["out_0"]
```
